# Optimizing a Trainium2 kernel written in Bass

```python
import math
import jax, jax.numpy as jnp
from jax import lax
import numpy as np

D_MODEL = 1024
BATCH = 1
SEQ = 512
DEPTH = 2

H_A = 8
D_A = 64
H_I = 4
D_I = 64
TOPK_MAX = 256
H_B = 4
D_B = 64
D_FF = 2816
CONV_W = 3
PLE_DIM = 256
ROPE_THETA = 10000.0
Q_BLOCK = 128
EPS = 1e-6

W_A = H_A * D_A
W_B = H_B * 2 * D_B
N_IN = W_A + D_A + D_A + H_I * D_I + D_I + H_I + 2 * (H_B * 2 * D_B) + W_B + 2 * D_MODEL


def _split_points():
    sizes = [W_A, D_A, D_A, H_I * D_I, D_I, H_I, H_B * 2 * D_B, H_B * 2 * D_B, W_B, D_MODEL, D_MODEL]
    pts, acc = [], 0
    for s in sizes[:-1]:
        acc += s
        pts.append(acc)
    return pts

def rms_norm(x, g):
    xf = x.astype(jnp.float32)
    y = xf * lax.rsqrt(jnp.mean(xf * xf, axis=-1, keepdims=True) + EPS)
    return (y * g.astype(jnp.float32)).astype(x.dtype)

def rope_tables(length, dim):
    inv = 1.0 / (ROPE_THETA ** (jnp.arange(0, dim, 2, dtype=jnp.float32) / dim))
    ang = jnp.arange(length, dtype=jnp.float32)[:, None] * inv[None, :]
    return jnp.cos(ang), jnp.sin(ang)

def apply_rope(x, cos, sin):
    half = x.shape[-1] // 2
    shape = (cos.shape[0],) + (1,) * (x.ndim - 3) + (half,)
    c, s = cos.reshape(shape), sin.reshape(shape)
    xf = x.astype(jnp.float32)
    x1, x2 = xf[..., :half], xf[..., half:]
    return jnp.concatenate([x1 * c - x2 * s, x2 * c + x1 * s], axis=-1).astype(x.dtype)

def gather_rows(t, idx):
    return jax.vmap(lambda tb, ib: tb[ib])(t, idx)

def token_mixers(u, w_in, g_qa, g_ka, g_qb, g_kb, lam_q1, lam_k1, lam_q2, lam_k2,
                 g_subln, w_branch_a, w_branch_b, w_out, lam_init, cos, sin):
    bsz, length, _ = u.shape
    k_top = min(TOPK_MAX, length // 4)
    proj = u @ w_in
    qa, ka, va, qi, ki, wi, qb, kb, vb, gate_a, gate_b = jnp.split(proj, _split_points(), axis=-1)

    qa = apply_rope(rms_norm(qa.reshape(bsz, length, H_A, D_A), g_qa), cos, sin)
    ka = apply_rope(rms_norm(ka, g_ka), cos, sin)
    qi = apply_rope(qi.reshape(bsz, length, H_I, D_I), cos, sin)
    ki = apply_rope(ki, cos, sin)
    wi = wi * (H_I ** -0.5 * D_I ** -0.5)

    qb = apply_rope(rms_norm(qb.reshape(bsz, length, H_B, 2, D_B), g_qb), cos, sin)
    kb = apply_rope(rms_norm(kb.reshape(bsz, length, H_B, 2, D_B), g_kb), cos, sin)
    q1, q2 = qb[..., 0, :], qb[..., 1, :]
    k1, k2 = kb[..., 0, :], kb[..., 1, :]
    vb = vb.reshape(bsz, length, H_B, 2 * D_B)
    lam = (jnp.exp(jnp.sum(lam_q1.astype(jnp.float32) * lam_k1.astype(jnp.float32)))
           - jnp.exp(jnp.sum(lam_q2.astype(jnp.float32) * lam_k2.astype(jnp.float32))) + lam_init)

    scale_a = D_A ** -0.5
    scale_b = D_B ** -0.5
    s_pos = jnp.arange(length)

    def qslice(t, start):
        return lax.dynamic_slice_in_dim(t, start, Q_BLOCK, axis=1)

    def block(start):
        t_pos = start + jnp.arange(Q_BLOCK)
        causal = s_pos[None, :] <= t_pos[:, None]
        rel = jax.nn.relu(jnp.einsum('bthd,bsd->bths', qslice(qi, start), ki).astype(jnp.float32))
        iscore = jnp.einsum('bths,bth->bts', rel, qslice(wi, start).astype(jnp.float32))
        iscore = jnp.where(causal[None], iscore, -jnp.inf)
        _, sel = lax.top_k(iscore, k_top)
        k_sel = gather_rows(ka, sel)
        v_sel = gather_rows(va, sel)
        logit = jnp.einsum('bthd,btkd->bthk', qslice(qa, start), k_sel).astype(jnp.float32) * scale_a
        valid = (sel <= t_pos[None, :, None])[:, :, None, :]
        attn_a = jax.nn.softmax(jnp.where(valid, logit, -jnp.inf), axis=-1)
        o_a = jnp.einsum('bthk,btkd->bthd', attn_a.astype(va.dtype), v_sel)
        s1 = jnp.einsum('bthd,bshd->bhts', qslice(q1, start), k1).astype(jnp.float32) * scale_b
        s2 = jnp.einsum('bthd,bshd->bhts', qslice(q2, start), k2).astype(jnp.float32) * scale_b
        a1 = jax.nn.softmax(jnp.where(causal, s1, -jnp.inf), axis=-1)
        a2 = jax.nn.softmax(jnp.where(causal, s2, -jnp.inf), axis=-1)
        o_b = jnp.einsum('bhts,bshe->bthe', (a1 - lam * a2).astype(vb.dtype), vb)
        return o_a, o_b

    starts = jnp.arange(0, length, Q_BLOCK, dtype=jnp.int32)
    o_a, o_b = lax.map(block, starts)
    o_a = jnp.moveaxis(o_a, 0, 1).reshape(bsz, length, W_A)
    o_b = jnp.moveaxis(o_b, 0, 1).reshape(bsz, length, H_B, 2 * D_B)
    o_b = (rms_norm(o_b, g_subln) * (1.0 - lam_init)).reshape(bsz, length, W_B)

    mix = jax.nn.sigmoid(gate_a) * (o_a @ w_branch_a) + jax.nn.sigmoid(gate_b) * (o_b @ w_branch_b)
    return mix @ w_out

def conv_ffn(u, w_up, conv_w, conv_b, w_down):
    up = u @ w_up
    pad = jnp.pad(up, ((0, 0), (CONV_W - 1, 0), (0, 0)))
    length = up.shape[1]
    conv = conv_b + sum(pad[:, j:j + length] * conv_w[j] for j in range(CONV_W))
    gate, val = jnp.split(conv, 2, axis=-1)
    return (jax.nn.gelu(gate, approximate=True) * val) @ w_down

def first_inputs(seed: int = 0) -> dict:
    key = jax.random.key(seed)
    ks = jax.random.split(key, 24)
    f32 = jnp.float32

    def nrm(k, shape, scale):
        return jax.random.normal(k, shape, f32) * scale

    def gain(k, shape):
        return 1.0 + 0.05 * jax.random.normal(k, shape, f32)

    return {
        'x': nrm(ks[0], (BATCH, SEQ, D_MODEL), 1.0),
        'p': nrm(ks[1], (DEPTH, BATCH, SEQ, PLE_DIM), 1.0),
        'g_mix_norm': gain(ks[2], (DEPTH, D_MODEL)),
        'w_in': nrm(ks[3], (DEPTH, D_MODEL, N_IN), D_MODEL ** -0.5),
        'g_qa': gain(ks[4], (DEPTH, D_A)),
        'g_ka': gain(ks[5], (DEPTH, D_A)),
        'g_qb': gain(ks[6], (DEPTH, D_B)),
        'g_kb': gain(ks[7], (DEPTH, D_B)),
        'lam_q1': nrm(ks[8], (DEPTH, D_B), 0.1),
        'lam_k1': nrm(ks[9], (DEPTH, D_B), 0.1),
        'lam_q2': nrm(ks[10], (DEPTH, D_B), 0.1),
        'lam_k2': nrm(ks[11], (DEPTH, D_B), 0.1),
        'g_subln': gain(ks[12], (DEPTH, 2 * D_B)),
        'w_branch_a': nrm(ks[13], (DEPTH, W_A, D_MODEL), W_A ** -0.5),
        'w_branch_b': nrm(ks[14], (DEPTH, W_B, D_MODEL), W_B ** -0.5),
        'w_out': nrm(ks[15], (DEPTH, D_MODEL, D_MODEL), D_MODEL ** -0.5),
        'g_ffn_norm': gain(ks[16], (DEPTH, D_MODEL)),
        'w_up': nrm(ks[17], (DEPTH, D_MODEL, 2 * D_FF), D_MODEL ** -0.5),
        'conv_w': nrm(ks[18], (DEPTH, CONV_W, 2 * D_FF), CONV_W ** -0.5),
        'conv_b': nrm(ks[19], (DEPTH, 2 * D_FF), 0.02),
        'w_down': nrm(ks[20], (DEPTH, D_FF, D_MODEL), D_FF ** -0.5),
        'g_ple_norm': gain(ks[21], (DEPTH, D_MODEL)),
        'w_ple_gate': nrm(ks[22], (DEPTH, D_MODEL, D_MODEL), D_MODEL ** -0.5),
        'w_ple_proj': nrm(ks[23], (DEPTH, PLE_DIM, D_MODEL), PLE_DIM ** -0.5),
    }

def first_block(x, p, g_mix_norm, w_in, g_qa, g_ka, g_qb, g_kb, lam_q1, lam_k1, lam_q2, lam_k2,
              g_subln, w_branch_a, w_branch_b, w_out, g_ffn_norm, w_up, conv_w, conv_b, w_down,
              g_ple_norm, w_ple_gate, w_ple_proj):
    length = x.shape[1]
    cos, sin = rope_tables(length, D_A)
    h = x
    for i in range(DEPTH):
        lam_init = 0.8 - 0.6 * math.exp(-0.3 * i)
        u = rms_norm(h, g_mix_norm[i])
        h = h + token_mixers(u, w_in[i], g_qa[i], g_ka[i], g_qb[i], g_kb[i], lam_q1[i], lam_k1[i],
                             lam_q2[i], lam_k2[i], g_subln[i], w_branch_a[i], w_branch_b[i], w_out[i],
                             lam_init, cos, sin)
        h = h + conv_ffn(rms_norm(h, g_ffn_norm[i]), w_up[i], conv_w[i], conv_b[i], w_down[i])
        ple_gate = jax.nn.sigmoid(rms_norm(h, g_ple_norm[i]) @ w_ple_gate[i])
        h = h + ple_gate * (p[i].astype(h.dtype) @ w_ple_proj[i])
    return h


DEPTH_2 = 1

CHUNK = 64
N_PREV_CHUNKS = 8
BAND = (N_PREV_CHUNKS + 1) * CHUNK
HEAD_DIM = 64
N_HEADS_ATTN = 8
N_HEADS_RWKV = 8
D_ATTN = N_HEADS_ATTN * HEAD_DIM
D_RWKV = N_HEADS_RWKV * HEAD_DIM
REL_CLIP = 128
DECAY_LORA = 64
AAA_LORA = 64
MV_LORA = 32
GATE_LORA = 160
N_GROUPS = 4
EXPERTS_PER_GROUP = 8
N_EXPERTS = N_GROUPS * EXPERTS_PER_GROUP
TOP_K_IN_GROUP = 2
D_EXPERT = 256
D_PLE = 256
DEEPNORM_ALPHA = (2 * DEPTH_2) ** 0.25
DEEPNORM_BETA = (8 * DEPTH_2) ** -0.25
LN_EPS = 1e-5
GN_EPS = 64e-5
NEG_INF = -1e30

Q0 = 0
K0 = D_ATTN
V0 = 2 * D_ATTN
RW0 = 3 * D_ATTN
RW_COLS = 3 * D_RWKV + DECAY_LORA + AAA_LORA + GATE_LORA
GATE0 = RW0 + RW_COLS
N_IN_2 = GATE0 + 2 * D_MODEL


def layer_norm(x, g, b):
    x32 = x.astype(jnp.float32)
    mu = jnp.mean(x32, axis=-1, keepdims=True)
    var = jnp.mean(jnp.square(x32 - mu), axis=-1, keepdims=True)
    y = (x32 - mu) * lax.rsqrt(var + LN_EPS)
    return (y * g.astype(jnp.float32) + b.astype(jnp.float32)).astype(x.dtype)

def chunked_band_attention(q, k, v, rel_bias):
    B, S, _ = q.shape
    nc = S // CHUNK
    q = q.reshape(B, nc, CHUNK, N_HEADS_ATTN, HEAD_DIM)
    pad = ((0, 0), (N_PREV_CHUNKS * CHUNK, 0), (0, 0))
    kp = jnp.pad(k, pad).reshape(B, nc + N_PREV_CHUNKS, CHUNK, N_HEADS_ATTN, HEAD_DIM)
    vp = jnp.pad(v, pad).reshape(B, nc + N_PREV_CHUNKS, CHUNK, N_HEADS_ATTN, HEAD_DIM)
    kb = jnp.concatenate([kp[:, j:j + nc] for j in range(N_PREV_CHUNKS + 1)], axis=2)
    vb = jnp.concatenate([vp[:, j:j + nc] for j in range(N_PREV_CHUNKS + 1)], axis=2)
    scores = jnp.einsum("bcqhd,bckhd->bhcqk", q, kb).astype(jnp.float32) * (HEAD_DIM ** -0.5)
    qi = jnp.arange(CHUNK)[:, None]
    kj = jnp.arange(BAND)[None, :]
    dist = qi - (kj - N_PREV_CHUNKS * CHUNK)
    idx = jnp.clip(dist, -REL_CLIP, REL_CLIP) + REL_CLIP
    bias = rel_bias[:, idx].astype(jnp.float32)
    key_chunk = jnp.arange(nc)[:, None] - N_PREV_CHUNKS + (jnp.arange(BAND) // CHUNK)[None, :]
    valid = key_chunk >= 0
    scores = jnp.where(valid[None, None, :, None, :], scores + bias[None, :, None], NEG_INF)
    prob = jax.nn.softmax(scores, axis=-1).astype(v.dtype)
    out = jnp.einsum("bhcqk,bckhd->bcqhd", prob, vb)
    return out.reshape(B, S, D_ATTN)

def rwkv7_scan(r, w, k, v, a, b):
    B, S, H, N = r.shape
    xs = tuple(jnp.swapaxes(t.astype(jnp.float32), 0, 1) for t in (r, w, k, v, a, b))

    def step(state, inp):
        rt, wt, kt, vt, at, bt = inp
        sa = jnp.einsum("bhij,bhj->bhi", state, at)
        state = state * wt[:, :, None, :] + sa[..., None] * bt[:, :, None, :] + vt[..., None] * kt[:, :, None, :]
        return state, jnp.einsum("bhij,bhj->bhi", state, rt)

    state0 = jnp.zeros((B, H, N, N), jnp.float32)
    _, ys = lax.scan(step, state0, xs)
    return jnp.swapaxes(ys, 0, 1)

def rwkv7_time_mix(cols, mu, v_first, decay_base, decay_up, aaa_base, aaa_up, gate_up,
                   k_k, k_a, r_k, gn_g, gn_b, vres):
    B, S, _ = cols.shape
    prev = jnp.pad(cols, ((0, 0), (1, 0), (0, 0)))[:, :-1]
    cols = cols + (prev - cols) * mu
    splits = [D_RWKV, 2 * D_RWKV, 3 * D_RWKV, 3 * D_RWKV + DECAY_LORA, 3 * D_RWKV + DECAY_LORA + AAA_LORA]
    r, k, v, wd, ad, gd = jnp.split(cols, splits, axis=-1)
    w_log = -jax.nn.softplus(-(decay_base + jnp.tanh(wd) @ decay_up)) - 0.5
    decay = jnp.exp(-jnp.exp(w_log.astype(jnp.float32)))
    a = jax.nn.sigmoid(aaa_base + ad @ aaa_up)
    g = jax.nn.sigmoid(gd) @ gate_up
    heads = lambda t: t.reshape(B, S, N_HEADS_RWKV, HEAD_DIM)
    kk = heads(k * k_k).astype(jnp.float32)
    kk = kk * lax.rsqrt(jnp.maximum(jnp.sum(kk * kk, axis=-1, keepdims=True), 1e-24))
    k = k * (1.0 + (a - 1.0) * k_a)
    if vres is None:
        v_first = v
    else:
        vres_base, vres_down, vres_up = vres
        v = v + (v_first - v) * jax.nn.sigmoid(vres_base + (v @ vres_down) @ vres_up)
    r_h, k_h, v_h, a_h = heads(r), heads(k), heads(v), heads(a)
    y = rwkv7_scan(r_h, heads(decay), k_h, v_h, -kk, kk * a_h.astype(jnp.float32))
    m = jnp.mean(y, axis=-1, keepdims=True)
    var = jnp.mean(jnp.square(y - m), axis=-1, keepdims=True)
    yn = ((y - m) * lax.rsqrt(var + GN_EPS)).reshape(B, S, D_RWKV)
    yn = yn * gn_g.astype(jnp.float32) + gn_b.astype(jnp.float32)
    bonus = (jnp.sum(r_h * k_h * r_k, axis=-1, keepdims=True) * v_h).reshape(B, S, D_RWKV)
    out = (yn.astype(cols.dtype) + bonus) * g
    return out, v_first

def hier_moe(x, w_grp, b_grp, w_exp, b_exp, e_gate, e_up, e_down):
    B, S, D = x.shape
    T = B * S
    xt = x.reshape(T, D)
    glog = (xt @ w_grp + b_grp).astype(jnp.float32)
    gprob = jax.nn.softmax(glog, axis=-1)
    grp = jnp.argmax(glog, axis=-1)
    g_gate = jnp.take_along_axis(gprob, grp[:, None], axis=1)
    elog = (xt @ w_exp + b_exp).astype(jnp.float32).reshape(T, N_GROUPS, EXPERTS_PER_GROUP)
    sel = jnp.take_along_axis(elog, grp[:, None, None], axis=1)[:, 0]
    top_v, top_i = lax.top_k(sel, TOP_K_IN_GROUP)
    wk = jax.nn.softmax(top_v, axis=-1) * g_gate
    eid = grp[:, None] * EXPERTS_PER_GROUP + top_i
    comb = jnp.sum(jax.nn.one_hot(eid, N_EXPERTS, dtype=jnp.float32) * wk[..., None], axis=1).astype(x.dtype)
    out = jnp.zeros_like(xt)
    for e in range(N_EXPERTS):
        h = jax.nn.silu(xt @ e_gate[e]) * (xt @ e_up[e])
        out = out + (h * comb[:, e:e + 1]) @ e_down[e]
    return out.reshape(B, S, D)

def second_inputs(seed: int = 0) -> dict:
    key = jax.random.key(seed)
    keys = iter(jax.random.split(key, 48))
    nrm = lambda shape, s: jax.random.normal(next(keys), shape, jnp.float32) * s
    uni = lambda shape, lo, hi: jax.random.uniform(next(keys), shape, jnp.float32, lo, hi)
    col_scale = jnp.ones((N_IN_2,), jnp.float32)
    col_scale = col_scale.at[V0:RW0].set(DEEPNORM_BETA)
    col_scale = col_scale.at[RW0 + 2 * D_RWKV:RW0 + 3 * D_RWKV].set(DEEPNORM_BETA)
    return {
        "x": nrm((BATCH, SEQ, D_MODEL), 1.0),
        "p": nrm((DEPTH_2, BATCH, SEQ, D_PLE), 1.0),
        "ln_in_g": 1.0 + nrm((D_MODEL,), 0.02),
        "ln_in_b": nrm((D_MODEL,), 0.02),
        "rel_bias": nrm((N_HEADS_ATTN, 2 * REL_CLIP + 1), 0.1),
        "w_in": nrm((DEPTH_2, D_MODEL, N_IN_2), D_MODEL ** -0.5) * col_scale,
        "tok_mix": uni((DEPTH_2, RW_COLS), 0.0, 1.0),
        "decay_base": uni((DEPTH_2, D_RWKV), -6.0, -1.0),
        "decay_up": nrm((DEPTH_2, DECAY_LORA, D_RWKV), DECAY_LORA ** -0.5),
        "aaa_base": nrm((DEPTH_2, D_RWKV), 0.1),
        "aaa_up": nrm((DEPTH_2, AAA_LORA, D_RWKV), AAA_LORA ** -0.5),
        "gate_up": nrm((DEPTH_2, GATE_LORA, D_RWKV), GATE_LORA ** -0.5),
        "k_k": 0.85 + nrm((DEPTH_2, D_RWKV), 0.02),
        "k_a": 1.0 + nrm((DEPTH_2, D_RWKV), 0.02),
        "r_k": nrm((DEPTH_2, N_HEADS_RWKV, HEAD_DIM), 0.1),
        "vres_base": nrm((DEPTH_2 - 1, D_RWKV), 0.1),
        "vres_down": nrm((DEPTH_2 - 1, D_RWKV, MV_LORA), D_RWKV ** -0.5),
        "vres_up": nrm((DEPTH_2 - 1, MV_LORA, D_RWKV), MV_LORA ** -0.5),
        "gn_g": 1.0 + nrm((DEPTH_2, D_RWKV), 0.02),
        "gn_b": nrm((DEPTH_2, D_RWKV), 0.02),
        "w_branch_attn": nrm((DEPTH_2, D_ATTN, D_MODEL), D_ATTN ** -0.5 * DEEPNORM_BETA),
        "w_branch_rwkv": nrm((DEPTH_2, D_RWKV, D_MODEL), D_RWKV ** -0.5 * DEEPNORM_BETA),
        "w_out": nrm((DEPTH_2, D_MODEL, D_MODEL), D_MODEL ** -0.5 * DEEPNORM_BETA),
        "router_grp": nrm((DEPTH_2, D_MODEL, N_GROUPS), D_MODEL ** -0.5),
        "router_grp_bias": nrm((DEPTH_2, N_GROUPS), 0.01),
        "router_exp": nrm((DEPTH_2, D_MODEL, N_EXPERTS), D_MODEL ** -0.5),
        "router_exp_bias": nrm((DEPTH_2, N_EXPERTS), 0.01),
        "exp_gate": nrm((DEPTH_2, N_EXPERTS, D_MODEL, D_EXPERT), D_MODEL ** -0.5),
        "exp_up": nrm((DEPTH_2, N_EXPERTS, D_MODEL, D_EXPERT), D_MODEL ** -0.5),
        "exp_down": nrm((DEPTH_2, N_EXPERTS, D_EXPERT, D_MODEL), D_EXPERT ** -0.5 * DEEPNORM_BETA),
        "ple_proj": nrm((DEPTH_2, D_PLE, D_MODEL), D_PLE ** -0.5 * DEEPNORM_BETA),
        "ple_gate": nrm((DEPTH_2, D_MODEL, D_MODEL), D_MODEL ** -0.5),
        "ln_g": 1.0 + nrm((DEPTH_2, 3, D_MODEL), 0.02),
        "ln_b": nrm((DEPTH_2, 3, D_MODEL), 0.02),
    }

def second_block(x, p, ln_in_g, ln_in_b, rel_bias, w_in, tok_mix, decay_base, decay_up,
              aaa_base, aaa_up, gate_up, k_k, k_a, r_k, vres_base, vres_down, vres_up,
              gn_g, gn_b, w_branch_attn, w_branch_rwkv, w_out, router_grp, router_grp_bias,
              router_exp, router_exp_bias, exp_gate, exp_up, exp_down, ple_proj, ple_gate,
              ln_g, ln_b):
    x = layer_norm(x, ln_in_g, ln_in_b)
    v_first = None
    for i in range(DEPTH_2):
        proj = x @ w_in[i]
        y_attn = chunked_band_attention(proj[..., Q0:K0], proj[..., K0:V0], proj[..., V0:RW0], rel_bias)
        vres = None if i == 0 else (vres_base[i - 1], vres_down[i - 1], vres_up[i - 1])
        y_rwkv, v_first = rwkv7_time_mix(proj[..., RW0:GATE0], tok_mix[i], v_first, decay_base[i],
                                         decay_up[i], aaa_base[i], aaa_up[i], gate_up[i], k_k[i],
                                         k_a[i], r_k[i], gn_g[i], gn_b[i], vres)
        gate_a = jax.nn.sigmoid(proj[..., GATE0:GATE0 + D_MODEL])
        gate_b = jax.nn.sigmoid(proj[..., GATE0 + D_MODEL:])
        mixed = (gate_a * (y_attn @ w_branch_attn[i]) + gate_b * (y_rwkv @ w_branch_rwkv[i])) @ w_out[i]
        x = layer_norm(DEEPNORM_ALPHA * x + mixed, ln_g[i, 0], ln_b[i, 0])
        moe = hier_moe(x, router_grp[i], router_grp_bias[i], router_exp[i], router_exp_bias[i],
                       exp_gate[i], exp_up[i], exp_down[i])
        x = layer_norm(DEEPNORM_ALPHA * x + moe, ln_g[i, 1], ln_b[i, 1])
        ple = (p[i] @ ple_proj[i]) * jax.nn.sigmoid(x @ ple_gate[i])
        x = layer_norm(DEEPNORM_ALPHA * x + ple, ln_g[i, 2], ln_b[i, 2])
    return x


def setup_inputs(seed=0):
    out = dict(first_inputs(seed))
    for name, value in second_inputs(seed + 1).items():
        if name != "x":
            out[name + "_2"] = value
    return out


def reference(
    x, p, g_mix_norm, w_in, g_qa, g_ka, g_qb, g_kb, lam_q1, lam_k1, lam_q2, lam_k2, g_subln,
    w_branch_a, w_branch_b, w_out, g_ffn_norm, w_up, conv_w, conv_b, w_down, g_ple_norm,
    w_ple_gate, w_ple_proj, p_2, ln_in_g_2, ln_in_b_2, rel_bias_2, w_in_2, tok_mix_2,
    decay_base_2, decay_up_2, aaa_base_2, aaa_up_2, gate_up_2, k_k_2, k_a_2, r_k_2, vres_base_2,
    vres_down_2, vres_up_2, gn_g_2, gn_b_2, w_branch_attn_2, w_branch_rwkv_2, w_out_2,
    router_grp_2, router_grp_bias_2, router_exp_2, router_exp_bias_2, exp_gate_2, exp_up_2,
    exp_down_2, ple_proj_2, ple_gate_2, ln_g_2, ln_b_2,
):
    x = first_block(
        x, p, g_mix_norm, w_in, g_qa, g_ka, g_qb, g_kb, lam_q1, lam_k1, lam_q2, lam_k2, g_subln,
        w_branch_a, w_branch_b, w_out, g_ffn_norm, w_up, conv_w, conv_b, w_down, g_ple_norm,
        w_ple_gate, w_ple_proj,
    )
    return second_block(
        x, p_2, ln_in_g_2, ln_in_b_2, rel_bias_2, w_in_2, tok_mix_2, decay_base_2, decay_up_2,
        aaa_base_2, aaa_up_2, gate_up_2, k_k_2, k_a_2, r_k_2, vres_base_2, vres_down_2,
        vres_up_2, gn_g_2, gn_b_2, w_branch_attn_2, w_branch_rwkv_2, w_out_2, router_grp_2,
        router_grp_bias_2, router_exp_2, router_exp_bias_2, exp_gate_2, exp_up_2, exp_down_2,
        ple_proj_2, ple_gate_2, ln_g_2, ln_b_2,
    )


_drawn_inputs = setup_inputs


def setup_inputs(seed=0):
    import zlib

    import numpy as np

    out = dict(_drawn_inputs(seed))
    spreads = {}
    factors = {'g_qa': 5.098,
     'g_ka': 5.593,
     'lam_q1': 2.971,
     'lam_k2': 2.721,
     'g_ple_norm': 3.547,
     'rel_bias_2': 44.139,
     'decay_up_2': 6.228,
     'aaa_base_2': 8.0,
     'k_k_2': 200.0,
     'k_a_2': 8.0,
     'r_k_2': 3.493,
     'gn_g_2': 30.923,
     'gn_b_2': 78.153,
     'router_grp_bias_2': 6.672,
     'router_exp_bias_2': 22.042}
    for name, (base, spread) in spreads.items():
        noise = np.random.default_rng([zlib.crc32(name.encode()), seed]).standard_normal(out[name].shape)
        drawn = base * np.exp(spread * noise) if base else spread * noise
        out[name] = __import__('jax').numpy.asarray(drawn.astype(out[name].dtype))
    for name, factor in factors.items():
        out[name] = (out[name] * factor).astype(out[name].dtype)
    return out
```

```python
import math
from contextlib import ExitStack

import numpy as np

import concourse.bass as bass
from concourse import mybir

F32 = mybir.dt.float32
F32R = mybir.dt.float32r
ALU = mybir.AluOpType
ACT = mybir.ActivationFunctionType
AX = mybir.AxisListType

T = 512
D = 1024
KT = 8
NEG = -1.0e30
GONE = -3.0e38
EPS = 1e-6
LN_EPS = 1e-5
GN_EPS = 64e-5
ALPHA = 2.0 ** 0.25
BLK = 2048
FCH = [8, 8, 6]



def const_table():
    parts = {}
    out = []
    at = 0

    def put(name, a):
        nonlocal at
        a = np.asarray(a, np.float32).reshape(128, -1)
        parts[name] = (at, at + a.shape[1])
        at += a.shape[1]
        out.append(a)

    p = np.arange(128)
    put("ident", np.eye(128))
    put("ones", np.ones((128, 128)))
    put("blk", (p[:, None] // 64) == (p[None, :] // 64))
    swap = (p // 64) * 64 + (p % 64 + 32) % 64
    put("rot", (p[:, None] == swap[None, :]))
    inv = (np.float32(1) / np.power(np.float32(10000), np.arange(0, 64, 2, dtype=np.float32) / np.float32(64))).astype(np.float32)
    ang = (np.arange(T, dtype=np.float32)[:, None] * inv[None, :]).astype(np.float64).T
    cos, sin = np.cos(ang)[p % 32], np.sin(ang)[p % 32]
    put("cos", cos)
    put("sin", np.where((p % 64 < 32)[:, None], -sin, sin))
    x = np.arange(T)
    put("causal", np.where(x[None, :] - 384 <= p[:, None], 0.0, NEG))
    put("chunk", np.where(p[:, None] < 64, NEG, 0.0) * np.ones((1, 64)))
    s = (p % 64)[:, None]
    t = np.arange(64)[None, :]
    put("eye", s == t)
    put("tri", np.concatenate([s < t, s <= t], axis=1))
    put("lv1", (s // 2 == t // 2) & (s % 2 == 1) & (t % 2 == 0))
    for m in (1, 2, 4, 8, 16, 32):
        put(f"lt{m}", (s // (2 * m) == t // (2 * m)) & (s % (2 * m) < m) & (t % (2 * m) >= m))
    hs = np.zeros((128, 4, 8))
    hb = np.zeros((128, 4, 128))
    for j in range(4):
        for h in range(2):
            hs[64 * h:64 * h + 64, j, 2 * j + h] = 1
            hb[2 * j + h, j, 64 * h:64 * h + 64] = 1
    put("hsel", hs)
    put("hbr", hb)
    put("gidx", np.broadcast_to(8 - np.arange(4), (128, 4)))
    put("eidx", np.broadcast_to(64 - np.arange(32), (128, 32)))
    return np.concatenate(out, axis=1), parts


def small_columns():
    at = 0
    parts = {}
    for i in range(2):
        for name, n in (("gmix", 8), ("gqa", 1), ("gka", 1), ("gqb", 1), ("gkb", 1), ("gsub", 1), ("lam", 4),
                        ("gffn", 8), ("cw0", 44), ("cw1", 44), ("cw2", 44), ("cb", 44), ("gple", 8)):
            parts[f"{name}{i}"] = (at, at + n)
            at += n
    for name, n in (("lnig", 8), ("lnib", 8), ("mu", 15), ("dbase", 4), ("abase", 4), ("kk", 4), ("ka", 4),
                    ("rk", 4), ("gng", 4), ("gnb", 4), ("lng", 24), ("lnb", 24), ("rbias", 36), ("wrt", 288)):
        parts[name] = (at, at + n)
        at += n
    return parts, at


class Queue:

    def __init__(self, engine, sem, name):
        self.engine, self.sem, self.name = engine, sem, name
        self.count = 0
        self.seen = {}

    def w(self, *tickets):
        for t in tickets:
            if t is None:
                continue
            if isinstance(t, list):
                self.w(*t)
                continue
            sem, name, value = t
            if self.seen.get(name, 0) < value:
                self.engine.wait_ge(sem, value)
                self.seen[name] = value

    def inc(self, ins):
        self.count += 1
        ins.then_inc(self.sem, 1)
        return (self.sem, self.name, self.count)

    def last(self):
        return (self.sem, self.name, self.count) if self.count else None


class Slot:
    def __init__(self, ap):
        self.ap = ap
        self.free = []


class Pool:

    def __init__(self, aps):
        self.slots = [Slot(a) for a in aps]

    def get(self):
        assert self.slots, "no slot is free"
        return self.slots.pop(0)

    def put(self, slot, *tickets):
        slot.free = list(tickets)
        self.slots.append(slot)


def program(nc, A, out, sizes, cparts, stop=None, dbg=None):
    sp, n_small = small_columns()
    n_const = A["consts"].shape[1]
    ctx = ExitStack()
    with ctx:
        def sb(name, shape, dt=F32):
            return ctx.enter_context(nc.sbuf_tensor(name, shape, dt))

        def sem(name):
            return ctx.enter_context(nc.semaphore(name))

        pe, dve, act, pool, sync = nc.tensor, nc.vector, nc.scalar, nc.gpsimd, nc.sync
        P = Queue(pe, sem("s_pe"), "pe")
        V = Queue(dve, sem("s_dve"), "dve")
        S = Queue(act, sem("s_act"), "act")
        G = Queue(pool, sem("s_pool"), "pool")
        Y = Queue(sync, None, "sync")

        class Dma:

            def __init__(self, name):
                self.sem, self.name, self.n = sem(name), name, 0

            def start(self, queue, dst, src):
                self.n += 16
                queue.engine.dma_start(dst, src).then_inc(self.sem, 16)
                return (self.sem, self.name, self.n)

        hT = sb("hT", [128, KT, T])
        XH = sb("XH", [128, KT, T], F32R)
        XL = sb("XL", [128, KT, T], F32R)
        raw = sb("raw", [128, 2, BLK])
        wh = sb("wh", [128, 3, BLK], F32R)
        wl = sb("wl", [128, 3, BLK], F32R)
        cst = sb("cst", [128, n_const])
        sml = sb("sml", [128, n_small])
        NAR = 15120
        base = (nc.sbuf_base + 31) // 32 * 32
        ar = sb("arena", [128, NAR])
        rounded = nc.alloc_sbuf_tensor_at("arena_rounded", [128, NAR], F32R, offset=base)
        arr_r = rounded[:, :]
        scr = sb("scr", [128, 9, T])
        tiny = sb("tiny", [128, 256])

        def C(name):
            a, b = cparts[name]
            return cst[:, a:b]

        def K(name, j=None):
            a, b = sp[name]
            return sml[:, a:b] if j is None else sml[:, a + j:a + j + 1]

        banks = Pool([ctx.enter_context(nc.psum_tensor(f"bank{i}", [128, T], F32))[:, :] for i in range(8)])
        scratch = Pool([scr[:, i, :] for i in range(9)])

        def everything():
            return [P.last(), V.last(), S.last(), G.last()]

        d_c, d_s, d_x = Dma("d_c"), Dma("d_s"), Dma("d_x")
        t_c = d_c.start(Y, cst[:, :], A["consts"])
        t_s = d_s.start(Y, sml[:, :], A["small"])
        t_x = d_x.start(Y, hT[:, :, :], A["xT"])
        for q in (P, V, S, G):
            q.w(t_c, t_s, t_x)

        d_raw = [Dma(f"d_raw{i}") for i in range(2)]

        class Stream:
            def __init__(self):
                self.loaded = 0
                self.split = 0
                self.used = 0
                self.raw_t = []
                self.split_t = []
                self.done = {}

            def load(self):
                n = self.loaded
                if n >= len(sizes):
                    return
                if n >= 2:
                    Y.w(*self.split_t[n - 2])
                k = sizes[n]
                self.raw_t.append(d_raw[n % 2].start(Y, raw[:, n % 2, 0:k], A["W"][n, :, 0:k]))
                self.loaded += 1

            def cut(self):
                n = self.split
                if n >= len(sizes):
                    return
                k = sizes[n]
                r, h, l = raw[:, n % 2, 0:k], wh[:, n % 3, 0:k], wl[:, n % 3, 0:k]
                if n >= 3:
                    S.w(self.done[n - 3])
                    V.w(self.done[n - 3])
                S.w(self.raw_t[n])
                th = S.inc(act.activation(h, r, ACT.Copy))
                V.w(th, self.raw_t[n])
                tl = V.inc(dve.tensor_tensor(l, r, h.bitcast(F32), ALU.subtract))
                self.split_t.append((th, tl))
                self.split += 1
                self.load()

            def next(self, n_cols):
                n = self.used
                self.used += 1
                while self.split <= n:
                    self.cut()
                P.w(*self.split_t[n])
                k = sizes[n]
                return [x[:, n % 3, 0:k].rearrange("p (k n) -> p k n", n=n_cols) for x in (wh, wl)]

            def finished(self, ticket):
                self.done[self.used - 1] = ticket
                while self.split < self.used + 2:
                    if self.split >= len(sizes) or (self.split >= 3 and self.split - 3 not in self.done):
                        break
                    self.cut()

        stream = Stream()
        for _ in range(2):
            stream.load()

        bg = []

        def background(n):
            while n and bg:
                if next(bg[0], None) is None:
                    bg.pop(0)
                n -= 1

        later = []

        def settle(n):
            while n and later:
                if next(later[0], None) is None:
                    later.pop(0)
                n -= 1

        def units(jobs, every=1, fill=0):
            jobs, live, r = list(jobs), [], 0
            while jobs or live:
                if jobs and r % every == 0:
                    live.append(jobs.pop(0))
                r += 1
                live = [g for g in live if next(g, None) is not None]
                background(fill)

        def products(ps, w, x, ks, c0, c1, first, last):
            h, l = w
            n = len(ks)
            for i, (k, xh, xl) in enumerate(ks):
                a, z = first and i == 0, last and i == n - 1
                pe.matmul(ps, h[:, k, c0:c1], xh, start=a, stop=False)
                pe.matmul(ps, h[:, k, c0:c1], xl, start=False, stop=False)
                mm = pe.matmul(ps, l[:, k, c0:c1], xh, start=False, stop=z)
            return P.inc(mm)

        def linear(n_cols, ks, evac, step=3):
            w = stream.next(n_cols)
            got = []
            for i in range((n_cols + 127) // 128):
                m = min(128, n_cols - 128 * i)
                b = banks.get()
                P.w(*b.free)
                t = products(b.ap[0:m, :], w, None, ks, 128 * i, 128 * i + m, True, True)
                got.append((b, t))
            stream.finished(t)
            for i, (b, t) in enumerate(got):
                evac(i, b, t)
            settle(3)
            background(step)

        def natural(n_cols, evac):
            h, l = stream.next(n_cols)
            got = []
            for ti in range(4):
                b = banks.get()
                P.w(*b.free)
                tt = slice(128 * ti, 128 * ti + 128)
                for k in range(KT):
                    pe.matmul(b.ap[:, 0:n_cols], XH[:, k, tt], h[:, k, :], start=k == 0, stop=False)
                    pe.matmul(b.ap[:, 0:n_cols], XL[:, k, tt], h[:, k, :], start=False, stop=False)
                    mm = pe.matmul(b.ap[:, 0:n_cols], XH[:, k, tt], l[:, k, :], start=False, stop=k == KT - 1)
                got.append((b, P.inc(mm)))
            stream.finished(got[-1][1])
            for ti, (b, t) in enumerate(got):
                evac(ti, b, t)
            settle(3)
            background(3)

        xk = [(k, XH[:, k, :], XL[:, k, :]) for k in range(KT)]

        def square_sum(src, ready):
            acc, tmp = scratch.get(), scratch.get()
            t = None
            sq = [tmp, scratch.get()]
            free = [tmp.free, sq[1].free]
            S.w(*ready, *acc.free)
            t_acc = S.inc(act.activation(acc.ap, src(0), ACT.Square))
            for k in range(1, KT):
                s = sq[k % 2]
                S.w(*free[k % 2])
                t = S.inc(act.activation(s.ap, src(k), ACT.Square))
                V.w(t, t_acc)
                t_acc = V.inc(dve.tensor_tensor(acc.ap, acc.ap, s.ap, ALU.add))
                free[k % 2] = [t_acc]
            for s in sq:
                scratch.put(s, t_acc)
            return acc, t_acc

        def total(acc, t_acc, ones="ones"):
            b = banks.get()
            P.w(*b.free, t_acc)
            t = P.inc(pe.matmul(b.ap, C(ones), acc.ap, start=True, stop=True))
            scratch.put(acc, t)
            return b, t

        def inverse_root(b, t, scale, eps):
            r = scratch.get()
            V.w(t, *r.free)
            t1 = V.inc(dve.tensor_scalar(r.ap, b.ap, scale, eps, ALU.mult, ALU.add))
            banks.put(b, t1)
            S.w(t1)
            t2 = S.inc(act.activation(r.ap, r.ap, ACT.Sqrt))
            V.w(t2)
            t3 = V.inc(dve.reciprocal(r.ap, r.ap))
            return r, t3

        def split_x(dh, dl, src, *tickets):
            S.w(*tickets)
            th = S.inc(act.activation(dh, src, ACT.Copy))
            V.w(th, *tickets)
            return V.inc(dve.tensor_tensor(dl, src, dh.bitcast(F32), ALU.subtract))

        def rms(gain):
            fence = everything()
            acc, t = square_sum(lambda k: hT[:, k, :], fence)
            b, t = total(acc, t)
            r, t = inverse_root(b, t, 1.0 / D, EPS)
            V.w(*fence, t)
            for k in range(KT):
                u = scratch.get()
                V.w(*u.free)
                tu = V.inc(dve.scalar_tensor_tensor(out=u.ap, in0=hT[:, k, :], scalar=K(gain, k), in1=r.ap,
                                                    op0=ALU.mult, op1=ALU.mult))
                S.w(*fence)
                t = split_x(XH[:, k, :], XL[:, k, :], u.ap, tu)
                scratch.put(u, t, tu)
                P.w(t)
            scratch.put(r, t)

        def layer_norm(g, b_, j, split=True):
            fence = everything()
            s = scratch.get()
            V.w(*fence, *s.free)
            t = V.inc(dve.tensor_tensor(s.ap, hT[:, 0, :], hT[:, 1, :], ALU.add))
            for k in range(2, KT):
                V.w(t)
                t = V.inc(dve.tensor_tensor(s.ap, s.ap, hT[:, k, :], ALU.add))
            b, t = total(s, t)
            for k in range(KT):
                V.w(t)
                tk = V.inc(dve.scalar_tensor_tensor(out=hT[:, k, :], in0=b.ap, scalar=-1.0 / D, in1=hT[:, k, :],
                                                    op0=ALU.mult, op1=ALU.add))
            banks.put(b, tk)
            acc, t = square_sum(lambda k: hT[:, k, :], [tk])
            b, t = total(acc, t)
            r, t = inverse_root(b, t, 1.0 / D, LN_EPS)
            for k in range(KT):
                V.w(t)
                t1 = V.inc(dve.scalar_tensor_tensor(out=hT[:, k, :], in0=hT[:, k, :], scalar=K(g, j + k), in1=r.ap,
                                                    op0=ALU.mult, op1=ALU.mult))
                V.w(t1)
                t1 = V.inc(dve.tensor_scalar(hT[:, k, :], hT[:, k, :], K(b_, j + k), None, ALU.add))
                if split:
                    S.w(*fence)
                    t1 = split_x(XH[:, k, :], XL[:, k, :], hT[:, k, :], t1)
                    P.w(t1)
            scratch.put(r, t1)
            return t1

        def rope(dst, t_dst, scale=None):
            b = banks.get()
            P.w(*b.free, t_dst)
            t = P.inc(pe.matmul(b.ap, C("rot"), dst, start=True, stop=True))
            u = scratch.get()
            V.w(t, *u.free)
            t1 = V.inc(dve.tensor_tensor(u.ap, b.ap, C("sin"), ALU.mult))
            banks.put(b, t1)
            G.w(t_dst, t)
            t2 = G.inc(pool.tensor_tensor(dst, dst, C("cos"), ALU.mult))
            V.w(t1, t2)
            t3 = V.inc(dve.tensor_tensor(dst, dst, u.ap, ALU.add))
            scratch.put(u, t3)
            if scale is not None:
                sb_, ts = scale
                V.w(ts, t3)
                t3 = V.inc(dve.tensor_tensor(dst, dst, sb_.ap, ALU.mult))
                banks.put(sb_, t3)
            return t3

        class HeadNorm:

            def __init__(self, n):
                self.n = n
                self.b = banks.get()
                P.w(*self.b.free)
                self.tiles = []

            def add(self, dst, gain, b, t):
                j = len(self.tiles)
                s = scratch.get()
                S.w(t, *s.free)
                ts = S.inc(act.activation(s.ap, b.ap, ACT.Square))
                V.w(ts)
                td = V.inc(dve.tensor_scalar(dst, b.ap, K(gain, 0), None, ALU.mult))
                banks.put(b, ts, td)
                P.w(ts)
                a, _ = cparts["hsel"]
                self.tp = P.inc(pe.matmul(self.b.ap[0:8, :], cst[:, a + 8 * j:a + 8 * j + 8], s.ap,
                                          start=j == 0, stop=j == self.n - 1))
                scratch.put(s, self.tp)
                self.tiles.append((dst, td))

            def close(self, put):
                n = 2 * self.n
                r = scratch.get()
                V.w(self.tp, *r.free)
                t1 = V.inc(dve.tensor_scalar(r.ap[0:n, :], self.b.ap[0:n, :], 1.0 / 64, EPS, ALU.mult, ALU.add))
                banks.put(self.b, t1)
                S.w(t1)
                t2 = S.inc(act.activation(r.ap[0:n, :], r.ap[0:n, :], ACT.Sqrt))
                V.w(t2)
                t3 = V.inc(dve.reciprocal(r.ap[0:n, :], r.ap[0:n, :]))
                yield True
                a, _ = cparts["hbr"]
                for j, (dst, td) in enumerate(self.tiles):
                    b = banks.get()
                    P.w(*b.free, t3)
                    t = P.inc(pe.matmul(b.ap, cst[0:n, a + 128 * j:a + 128 * j + 128], r.ap[0:n, :],
                                        start=True, stop=True))
                    if j == self.n - 1:
                        scratch.put(r, t)
                    put(j, rope(dst, td, (b, t)))
                    yield True

        def tz(a, b=None):
            return tiny[:, a:a + 1] if b is None else tiny[:, a:b]

        cols = [0]

        def tiny4():
            cols[0] = (cols[0] + 1) % 16
            return 160 + 4 * cols[0]

        def probs(q, k, mask, n, scale, tq, got):
            b = banks.get()
            P.w(*b.free, *tq)
            t = P.inc(pe.matmul(b.ap[:, 0:n], q, k, start=True, stop=True))
            yield True
            s, c = scratch.get(), tiny4()
            V.w(t, *s.free, *tq)
            t1 = V.inc(dve.tensor_tensor_reduce(s.ap[:, 0:n], b.ap[:, 0:n], mask, scale, GONE, ALU.add, ALU.max, tz(c)))
            banks.put(b, t1)
            V.w(t1)
            t2 = V.inc(dve.tensor_scalar(tz(c + 1), tz(c), -1.0, None, ALU.mult))
            yield True
            S.w(t2)
            t3 = S.inc(act.activation(s.ap[:, 0:n], s.ap[:, 0:n], ACT.Exp, bias=tz(c + 1), accum_out=tz(c + 2)))
            yield True
            V.w(t3)
            t4 = V.inc(dve.reciprocal(tz(c + 3), tz(c + 2)))
            V.w(t4)
            got.append((s, c, t4))

        def turned(s, t, ti, got):
            n = 128 * (ti + 1)
            b = banks.get()
            P.w(*b.free, t)
            for j in range(ti + 1):
                mm = pe.transpose(b.ap[:, 128 * j:128 * j + 128], s.ap[:, 128 * j:128 * j + 128], C("ident"))
            tt = P.inc(mm)
            scratch.put(s, tt)
            yield True
            o = scratch.get()
            S.w(tt, *o.free)
            to = S.inc(act.activation(o.ap[:, 0:n], b.ap[:, 0:n], ACT.Copy))
            banks.put(b, to)
            yield True
            P.w(to)
            got.append(o)

        def attend(q, k, v, mask, ti, tq, acc, out_ap, first, finish):
            n = 128 * (ti + 1)
            got = []
            yield from probs(q, k, mask, n, 0.125, tq, got)
            s, c, t = got.pop()
            t = V.inc(dve.tensor_scalar(s.ap[:, 0:n], s.ap[:, 0:n], tz(c + 3), None, ALU.mult))
            yield True
            yield from turned(s, t, ti, got)
            o = got.pop()
            if first:
                acc.append(banks.get())
                P.w(*acc[0].free)
            for j in range(ti + 1):
                mm = pe.matmul(out_ap(acc[0]), v(j), o.ap[:, 128 * j:128 * j + 128], start=j == 0, stop=j == ti)
            t = P.inc(mm)
            scratch.put(o, t)
            yield True
            if finish:
                yield from finish(acc[0], t)

        def A_(off, n):
            return ar[:, off:off + n]

        def A3(off, k, n=T):
            return ar[:, off:off + k * n].rearrange("p (k n) -> p k n", n=n)

        def evac_add(n0):
            def f(i, b, t):
                V.w(t)
                banks.put(b, V.inc(dve.tensor_tensor(hT[:, n0 + i, :], b.ap, hT[:, n0 + i, :], ALU.add)))
            return f

        def dump(src, *tickets):
            d = Dma("d_dump")
            Y.w(*everything())
            t = d.start(Y, out, src)
            Y.w(t)

        def gated_branches(XA, XB, t_in, c0):
            mixf = A3(c0, 8)
            fence = everything()
            V.w(*fence)
            for j in range(4):
                sg = {}

                def gate(which):
                    def f(i, b, t):
                        s = scratch.get()
                        S.w(t, *s.free)
                        ts = S.inc(act.activation(s.ap, b.ap, ACT.Sigmoid))
                        banks.put(b, ts)
                        sg[which, i] = (s, ts)
                    return f
                linear(256, xk, gate(0))
                linear(256, xk, gate(1))
                w = stream.next(256)
                P.w(*t_in)
                done = []
                for i in range(2):
                    for which, X in ((0, XA), (1, XB)):
                        b = banks.get()
                        P.w(*b.free)
                        t = products(b.ap, w, None, [(4 * which + k, X[0][:, k, :], X[1][:, k, :]) for k in range(4)],
                                     128 * i, 128 * i + 128, True, True)
                        done.append((i, which, b, t))
                stream.finished(t)
                for i, which, b, t in done:
                    s, ts = sg[which, i]
                    o = mixf[:, 2 * j + i, :]
                    V.w(t, ts)
                    if which == 0:
                        t0 = V.inc(dve.tensor_tensor(o, b.ap, s.ap, ALU.mult))
                        banks.put(b, t0)
                        scratch.put(s, t0)
                    else:
                        t1 = V.inc(dve.tensor_tensor(s.ap, b.ap, s.ap, ALU.mult))
                        banks.put(b, t1)
                        V.w(t0, t1)
                        t2 = V.inc(dve.tensor_tensor(o, o, s.ap, ALU.add))
                        scratch.put(s, t2)
            fence = everything()
            for k in range(KT):
                S.w(*fence)
                V.w(*fence)
                P.w(split_x(XH[:, k, :], XL[:, k, :], mixf[:, k, :], t2))

        def first_layer(li):
            lam_init = 0.8 - 0.6 * math.exp(-0.3 * li)
            o = 0

            def take(n):
                nonlocal o
                o += n
                return o - n
            KI, QI = take(512), take(1024)
            o = 2048
            OBL = take(2048)
            KA, WV, QA, MB = take(512), take(4 * 68), take(2048), take(2048)
            QB, KB, VB = take(2048), take(2048), take(2048)
            assert o <= NAR
            rms(f"gmix{li}")
            fence = everything()
            for q in (V, S, P):
                q.w(*fence)
            ready = {}

            b = banks.get()
            t = None
            for j in range(2):
                t = V.inc(dve.tensor_tensor(tz(60 + j), K(f"lam{li}", 2 * j), K(f"lam{li}", 2 * j + 1), ALU.mult))
            P.w(*b.free, t)
            t = P.inc(pe.matmul(b.ap[:, 0:2], C("ones"), tz(60, 62), start=True, stop=True))
            S.w(t)
            t = S.inc(act.activation(tz(62, 64), b.ap[:, 0:2], ACT.Exp))
            banks.put(b, t)
            V.w(t)
            t = V.inc(dve.tensor_tensor(tz(64), tz(63), tz(62), ALU.subtract))
            V.w(t)
            t_lam = V.inc(dve.tensor_scalar(tz(65), tz(64), -lam_init, None, ALU.add))

            def keep(dst, name):
                def f(b, t):
                    V.w(t)
                    td = V.inc(dve.tensor_copy(dst, b.ap))
                    banks.put(b, td)

                    def turn():
                        ready[name] = rope(dst, td)
                        yield True
                    later.append(turn())
                return f

            hk = HeadNorm(1)
            linear(256, xk, lambda i, b, t: keep(A_(KI, 512), "ki")(b, t) if i == 0 else keep(A_(QI, 512), "qi0")(b, t))
            linear(256, xk, lambda i, b, t: keep(A_(QI + 512, 512), "qi1")(b, t) if i == 0
                   else hk.add(A_(KA, 512), f"gka{li}", b, t))
            wv = A3(WV, 4, 68)

            def evac_wv(ti, b, t):
                V.w(t)
                ready["wv", ti] = V.inc(dve.tensor_copy(wv[:, ti, :], b.ap[:, 0:68]))
                banks.put(b, ready["wv", ti])
            natural(68, evac_wv)
            later.append(hk.close(lambda j, t: ready.__setitem__("ka", t)))
            settle(3)

            mb = A3(MB, 4)
            t_mask = {0: None}

            def scores(ti):
                n = 128 * (ti + 1)
                t_prev = None
                V.w(ready["wv", ti])
                for h in range(4):
                    r0 = 64 * (h % 2)
                    b = banks.get()
                    P.w(*b.free, ready["ki"], ready[f"qi{h // 2}"])
                    t = P.inc(pe.matmul(b.ap[:, 0:n], A_(QI + 512 * (h // 2), 512)[r0:r0 + 64, 128 * ti:128 * ti + 128],
                                        A_(KI, 512)[r0:r0 + 64, 0:n], start=True, stop=True))
                    s = scratch.get()
                    S.w(t, *s.free)
                    t = S.inc(act.activation(s.ap[:, 0:n], b.ap[:, 0:n], ACT.Relu, scale=1.0 / 16))
                    banks.put(b, t)
                    w_ = wv[:, ti, 64 + h:65 + h]
                    V.w(t, t_prev)
                    if h == 0:
                        t_prev = V.inc(dve.tensor_scalar(mb[:, ti, 0:n], s.ap[:, 0:n], w_, None, ALU.mult))
                    else:
                        t_prev = V.inc(dve.scalar_tensor_tensor(out=mb[:, ti, 0:n], in0=s.ap[:, 0:n], scalar=w_,
                                                                in1=mb[:, ti, 0:n], op0=ALU.mult, op1=ALU.add))
                    scratch.put(s, t_prev)
                V.w(t_prev)
                return V.inc(dve.tensor_tensor(mb[:, ti, 0:n], mb[:, ti, 0:n], C("causal")[:, 512 - n:512], ALU.add))

            def choose(ti, t):
                n = 128 * (ti + 1)
                m = mb[:, ti, 0:n]
                top = tz(64 + 8 * ti, 72 + 8 * ti)
                for r in range(16):
                    V.w(t)
                    t = V.inc(dve.max(top, m))
                    yield t
                    V.w(t)
                    t = V.inc(dve.match_replace(m, top, m, GONE))
                    yield t
                V.w(t)
                t = V.inc(dve.tensor_scalar(m, m, -2.0e38, NEG, ALU.is_gt, ALU.mult))
                V.w(t)
                t_mask[ti] = V.inc(dve.tensor_tensor(m, m, C("causal")[:, 512 - n:512], ALU.add))
                yield t_mask[ti]

            for ti in (1, 2, 3):
                bg.append(choose(ti, scores(ti)))

            hn = HeadNorm(4)
            for j in range(2):
                linear(256, xk, lambda i, b, t, j=j: hn.add(A_(QA + 512 * (2 * j + i), 512), f"gqa{li}", b, t), 8)
            tqa, tqb, tkb = {}, {}, {}
            later.append(hn.close(tqa.__setitem__))
            hn = HeadNorm(4)
            for j in range(2):
                linear(256, xk, lambda i, b, t, j=j: hn.add(A_(QB + 512 * (2 * j + i), 512), f"gqb{li}", b, t), 8)
            later.append(hn.close(tqb.__setitem__))
            hn = HeadNorm(4)
            for j in range(2):
                linear(256, xk, lambda i, b, t, j=j: hn.add(A_(KB + 512 * (2 * j + i), 512), f"gkb{li}", b, t), 8)
            later.append(hn.close(tkb.__setitem__))
            vb = A3(VB, 4)
            tvb = []

            def evac_vb(c0):
                def f(ti, b, t):
                    V.w(t)
                    td = V.inc(dve.tensor_copy(vb[:, ti, c0:c0 + 256], b.ap[:, 0:256]))
                    banks.put(b, td)
                    tvb.append(td)
                return f
            natural(256, evac_vb(0))
            natural(256, evac_vb(256))

            obh = arr_r[:, 0:2048].rearrange("p (k n) -> p k n", n=T)
            obl = arr_r[:, OBL:OBL + 2048].rearrange("p (k n) -> p k n", n=T)
            fence = everything()
            S.w(*fence)
            V.w(*fence)
            settle(1000)
            P.w(*tvb)
            last = {}

            def diff_head(ti, h, acc):
                n = 128 * (ti + 1)
                cm = C("causal")[:, 512 - n:512]
                got = [[], []]
                two = []
                for e in range(2):
                    r0 = 64 * e
                    qt = A_(QB + 512 * h, 512)[r0:r0 + 64, 128 * ti:128 * ti + 128]
                    kt = A_(KB + 512 * h, 512)[r0:r0 + 64, 0:n]
                    two.append(probs(qt, kt, cm, n, 0.125, [tqb[h], tkb[h]], got[e]))
                while two:
                    two = [g for g in two if next(g, None) is not None]
                    last["qk"] = P.last()
                    if two:
                        yield True
                (s1, c1, u1), (s2, c2, u2) = got[0][0], got[1][0]
                V.w(t_lam, u2)
                t = V.inc(dve.tensor_scalar(s2.ap[:, 0:n], s2.ap[:, 0:n], tz(c2 + 3), tz(65), ALU.mult, ALU.mult))
                V.w(t, u1)
                t = V.inc(dve.scalar_tensor_tensor(out=s1.ap[:, 0:n], in0=s1.ap[:, 0:n], scalar=tz(c1 + 3),
                                                   in1=s2.ap[:, 0:n], op0=ALU.mult, op1=ALU.add))
                scratch.put(s2, t)
                yield True
                yield from turned(s1, t, ti, got[0])
                pt = got[0].pop()
                if h == 0:
                    acc.append(banks.get())
                    P.w(*acc[0].free)
                for j in range(ti + 1):
                    mm = pe.matmul(acc[0].ap[:, 128 * h:128 * h + 128], vb[:, j, 128 * h:128 * h + 128],
                                   pt.ap[:, 128 * j:128 * j + 128], start=j == 0, stop=j == ti)
                t = P.inc(mm)
                scratch.put(pt, t)
                yield True
                if h < 3:
                    return
                acc = acc[0]
                s, q = scratch.get(), scratch.get()
                S.w(t, *s.free, *q.free)
                ts = S.inc(act.activation(s.ap, acc.ap, ACT.Copy))
                tq = S.inc(act.activation(q.ap, acc.ap, ACT.Square))
                banks.put(acc, tq)
                yield True
                b, t = total(q, tq)
                yield True
                r, t = inverse_root(b, t, 1.0 / 128, EPS)
                V.w(t, ts)
                t = V.inc(dve.scalar_tensor_tensor(out=s.ap, in0=s.ap, scalar=K(f"gsub{li}", 0), in1=r.ap,
                                                   op0=ALU.mult, op1=ALU.mult))
                scratch.put(r, t)
                V.w(t)
                t = V.inc(dve.tensor_scalar(s.ap, s.ap, 1.0 - lam_init, None, ALU.mult))
                yield True
                s3 = s.ap.rearrange("p (h n) -> p h n", h=4)
                tt = slice(128 * ti, 128 * ti + 128)
                last["ob"] = split_x(obh[:, :, tt], obl[:, :, tt], s3, t)
                scratch.put(s, last["ob"])

            jobs = []
            for ti in range(4):
                acc = []
                jobs += [diff_head(ti, h, acc) for h in range(4)]
            units(jobs, every=2, fill=4)
            background(1000)

            oah = arr_r[:, QB:QB + 2048].rearrange("p (k n) -> p k n", n=T)
            oal = arr_r[:, KB:KB + 2048].rearrange("p (k n) -> p k n", n=T)
            S.w(last["qk"])
            V.w(last["qk"])
            P.w(ready["wv", 3])

            def keep_oa(ti):
                def f(acc, t):
                    a3 = acc.ap.rearrange("p (h n) -> p h n", h=4)
                    tt = slice(128 * ti, 128 * ti + 128)
                    last["oa"] = split_x(oah[:, :, tt], oal[:, :, tt], a3, t)
                    banks.put(acc, last["oa"])
                    yield True
                return f

            def out_of(h):
                r0 = 64 * (h % 2)
                return lambda b: b.ap[r0:r0 + 64, 128 * (h // 2):128 * (h // 2) + 128]

            jobs = []
            for ti in range(4):
                n = 128 * (ti + 1)
                mask = C("causal")[:, 512 - n:512] if ti == 0 else mb[:, ti, 0:n]
                acc = []
                for h in range(8):
                    r0 = 64 * (h % 2)
                    jobs.append(attend(A_(QA + 512 * (h // 2), 512)[r0:r0 + 64, 128 * ti:128 * ti + 128],
                                       A_(KA, 512)[r0:r0 + 64, 0:n], lambda j: wv[:, j, 0:64], mask, ti,
                                       [tqa[h // 2], ready["ka"], t_mask[ti]], acc, out_of(h), h == 0,
                                       keep_oa(ti) if h == 7 else None))
            units(jobs)
            t_oa, t_ob = last["oa"], last["ob"]

            gated_branches((oah, oal), (obh, obl), [t_oa, t_ob], 4096)
            for j in range(4):
                linear(256, xk, evac_add(2 * j))

            if stop == f"mix{li}":
                return
            rms(f"gffn{li}")
            fence = everything()
            S.w(*fence)
            V.w(*fence)
            f0 = 0
            for c in FCH:
                uh = arr_r[:, 0:4096].rearrange("p (k n) -> p k n", n=T)
                ul = arr_r[:, 4096:8192].rearrange("p (k n) -> p k n", n=T)
                fence = [P.last()]
                S.w(*fence)
                V.w(*fence)
                for j in range(0, c, 2):
                    conv = {}

                    def evac_conv(which, j=j):
                        def f(i, b, t):
                            fi = f0 + j + i + 22 * which
                            s = scratch.get()
                            S.w(t, *s.free)
                            t0 = S.inc(act.activation(s.ap, b.ap, ACT.Identity, scale=K(f"cw2{li}", fi),
                                                      bias=K(f"cb{li}", fi)))
                            V.w(t0, t)
                            t1 = V.inc(dve.scalar_tensor_tensor(out=s.ap[:, 1:T], in0=b.ap[:, 0:T - 1],
                                                                scalar=K(f"cw1{li}", fi), in1=s.ap[:, 1:T],
                                                                op0=ALU.mult, op1=ALU.add))
                            V.w(t1)
                            t2 = V.inc(dve.scalar_tensor_tensor(out=s.ap[:, 2:T], in0=b.ap[:, 0:T - 2],
                                                                scalar=K(f"cw0{li}", fi), in1=s.ap[:, 2:T],
                                                                op0=ALU.mult, op1=ALU.add))
                            banks.put(b, t0, t2)
                            if which == 0:
                                S.w(t2)
                                t2 = S.inc(act.activation(s.ap, s.ap, ACT.Gelu_apprx_tanh))
                                conv[i] = (s, t2)
                            else:
                                g, tg = conv[i]
                                V.w(t2, tg)
                                t3 = V.inc(dve.tensor_tensor(s.ap, s.ap, g.ap, ALU.mult))
                                scratch.put(g, t3)
                                t4 = split_x(uh[:, j + i, :], ul[:, j + i, :], s.ap, t3)
                                scratch.put(s, t4)
                                P.w()
                                conv["t", i] = t4
                        return f
                    linear(256, xk, evac_conv(0))
                    linear(256, xk, evac_conv(1))
                P.w(conv["t", 0], conv["t", 1])
                ku = [(k, uh[:, k, :], ul[:, k, :]) for k in range(c)]
                for j in range(4):
                    linear(256, ku, evac_add(2 * j))
                f0 += c

            if stop == f"ffn{li}":
                return
            rms(f"gple{li}")
            fence = everything()
            S.w(*fence)
            V.w(*fence)
            Y.w(*fence)
            pt = A3(0, 2)
            ph = arr_r[:, 1024:2048].rearrange("p (k n) -> p k n", n=T)
            pl = arr_r[:, 2048:3072].rearrange("p (k n) -> p k n", n=T)
            pp = A3(4096, 8)
            t = d_p.start(Y, pt, A["pT"][li])
            for k in range(2):
                t1 = split_x(ph[:, k, :], pl[:, k, :], pt[:, k, :], t)
            P.w(t1)
            embed(ph, pl, pp)
            for j in range(4):
                def f(i, b, t, j=j):
                    s = scratch.get()
                    S.w(t, *s.free)
                    ts = S.inc(act.activation(s.ap, b.ap, ACT.Sigmoid))
                    banks.put(b, ts)
                    V.w(ts)
                    t1 = V.inc(dve.tensor_tensor(s.ap, s.ap, pp[:, 2 * j + i, :], ALU.mult))
                    V.w(t1)
                    t1 = V.inc(dve.tensor_tensor(hT[:, 2 * j + i, :], hT[:, 2 * j + i, :], s.ap, ALU.add))
                    scratch.put(s, t1)
                linear(256, xk, f)

        def embed(ph, pl, pp):
            w = stream.next(1024)
            for i in range(8):
                b = banks.get()
                P.w(*b.free)
                t = products(b.ap, w, None, [(k, ph[:, k, :], pl[:, k, :]) for k in range(2)],
                             128 * i, 128 * i + 128, True, True)
                if i == 7:
                    stream.finished(t)
                S.w(t)
                tc = S.inc(act.activation(pp[:, i, :], b.ap, ACT.Copy))
                banks.put(b, tc)
            V.w(tc)
            return tc

        d_p = Dma("d_p")

        for li in range(2):
            first_layer(li)
            if stop in (f"layer{li}", f"mix{li}", f"ffn{li}"):
                dump(hT[:, :, :])
                return
        def bc(ap, shape):
            return ap.to_broadcast(shape)

        layer_norm("lnig", "lnib", 0)
        if stop == "ln2":
            dump(hT[:, :, :])
            return
        fence = everything()
        for q in (V, S, P, Y):
            q.w(*fence)
        YA, YR, QO, KO, VO, BI = 0, 2048, 2048, 4096, 6144, 8192
        bias = A3(BI, 8)
        d_b = Dma("d_b")
        t_b = d_b.start(Y, ar[:, BI:BI + 4096], A["bias"])
        V.w(t_b)
        t_b = V.inc(dve.tensor_scalar(ar[:, BI:BI + 4096], ar[:, BI:BI + 4096], 8.0, None, ALU.mult))
        V.w(t_b)
        for h in range(8):
            t_b = V.inc(dve.tensor_tensor(bias[:, h, 448:512], bias[:, h, 448:512], C("chunk"), ALU.add))
        rdy = {}

        def evac_to(dst, name):
            def f(i, b, t):
                S.w(t)
                rdy[name, i] = S.inc(act.activation(dst(i), b.ap, ACT.Copy))
                banks.put(b, rdy[name, i])
            return f

        for name, off in (("q", QO), ("k", KO)):
            for j in range(2):
                linear(256, xk, evac_to(lambda i, off=off, j=j: A_(off + 512 * (2 * j + i), 512), (name, j)))
        vn = A3(VO, 4)

        def evac_vn(c0):
            def f(ti, b, t):
                S.w(t)
                rdy["v"] = S.inc(act.activation(vn[:, ti, c0:c0 + 256], b.ap[:, 0:256], ACT.Copy))
                banks.put(b, rdy["v"])
            return f
        natural(256, evac_vn(0))
        natural(256, evac_vn(256))
        ya = A3(YA, 4)
        P.w(rdy["v"])
        V.w(t_b)
        last = {}

        def keep_ya(ti):
            def f(acc, t):
                S.w(t)
                last["ya"] = S.inc(act.activation(ya[:, :, 128 * ti:128 * ti + 128],
                                                  acc.ap.rearrange("p (h n) -> p h n", h=4), ACT.Copy))
                banks.put(acc, last["ya"])
                yield True
            return f

        def out_of(h):
            r0 = 64 * (h % 2)
            return lambda b: b.ap[r0:r0 + 64, 128 * (h // 2):128 * (h // 2) + 128]

        jobs = []
        for ti in range(4):
            n = 128 * (ti + 1)
            acc = []
            for h in range(8):
                r0 = 64 * (h % 2)
                j, i = divmod(h // 2, 2)
                jobs.append(attend(A_(QO + 512 * (h // 2), 512)[r0:r0 + 64, 128 * ti:128 * ti + 128],
                                   A_(KO + 512 * (h // 2), 512)[r0:r0 + 64, 0:n],
                                   lambda j, h=h: vn[:, j, 64 * h:64 * h + 64], bias[:, h, 512 - n:512], ti,
                                   [rdy[("q", j), i], rdy[("k", j), i]], acc, out_of(h), h == 0,
                                   keep_ya(ti) if h == 7 else None))
        units(jobs)
        t_ya = last["ya"]

        fence = everything()
        for q in (V, S, P):
            q.w(*fence)
        yr = A3(YR, 4)
        WD, GD = A_(4096, 512), A3(4608, 2)
        omu = tz(128, 143)
        V.w()
        t_omu = V.inc(dve.tensor_scalar(omu, K("mu"), -1.0, 1.0, ALU.mult, ALU.add))
        S.w(t_omu)

        def mixed(dst, b, t, col, rows=128):
            S.w(t)
            t0 = S.inc(act.activation(dst, b.ap[0:rows, :], ACT.Identity, scale=tz(128 + col)[0:rows, :]))
            V.w(t0)
            t1 = V.inc(dve.scalar_tensor_tensor(out=dst[:, 1:T], in0=b.ap[0:rows, 0:T - 1], scalar=K("mu", col)[0:rows, :],
                                                in1=dst[:, 1:T], op0=ALU.mult, op1=ALU.add))
            banks.put(b, t1)
            return t1

        def evac_lo(i, b, t):
            if i == 0:
                t = mixed(WD, b, t, 12)
                S.w(t)
                rdy["wd"] = S.inc(act.activation(WD[0:64, :], WD[0:64, :], ACT.Tanh))
            else:
                t = mixed(GD[:, 0, :], b, t, 13)
                S.w(t)
                rdy["gd"] = S.inc(act.activation(GD[:, 0, :], GD[:, 0, :], ACT.Sigmoid))

        def evac_g1(i, b, t):
            t = mixed(GD[0:32, 1, :], b, t, 14, 32)
            S.w(t)
            rdy["gd"] = S.inc(act.activation(GD[0:32, 1, :], GD[0:32, 1, :], ACT.Sigmoid))
        linear(256, xk, evac_lo)
        linear(32, xk, evac_g1)
        P.w(rdy["wd"], rdy["gd"])

        AR = ar[:, 5632:6656]
        AR4 = AR.rearrange("p (c w t) -> p c w t", c=8, w=2)
        Bt, Kt, Bn, Kn, Vn, BV, YT = (A_(6656 + 512 * i, 512) for i in range(7))
        LR, MK = ar[:, 10752:11776], ar[:, 11776:12800]
        X, XT, T1, Lm = (A_(12800 + 512 * i, 512) for i in range(4))
        rT, kT, vT, lw, cc, aT, kkT, tm = (A_(10752 + 512 * i, 512) for i in range(8))
        STs = [A_(14848 + 128 * i, 128) for i in range(2)]
        Bz, Kz = (Bt, T1), (Kt, Lm)
        hm = (C("blk")[:, 0:1], C("blk")[:, 64:65])

        def c8(ap):
            return ap.rearrange("p (c t) -> p c t", c=8)

        d_l = Dma("d_l")
        for i in range(2):
            t = V.inc(dve.memset(STs[i], 0.0))
        V.w(t)
        for j in range(4):
            fence = everything()
            for q in (V, S, P):
                q.w(*fence)
            lora = scratch.get()
            Y.w(*lora.free)
            t_l = d_l.start(Y, lora.ap[:, 0:384], A["lora"][j])
            P.w(t_l)
            rk = {}

            def evac_rk(i, b, t):
                rk[i] = mixed((rT, kT)[i], b, t, 4 * i + j)
            linear(256, xk, evac_rk)
            linear(128, xk, lambda i, b, t: rk.__setitem__(2, mixed(vT, b, t, 8 + j)))

            def low_rank(r0, r1, dst, base):
                b = banks.get()
                P.w(*b.free)
                t = P.inc(pe.matmul(b.ap, lora.ap[r0:r1, 0:128], WD[r0:r1, :], start=True, stop=True))
                S.w(t)
                t = S.inc(act.activation(dst, b.ap, ACT.Sigmoid, bias=K(base, j)))
                banks.put(b, t)
                return t
            t = low_rank(0, 64, lw, "dbase")
            V.w(t)
            t_lw = V.inc(dve.tensor_scalar(lw, lw, -math.exp(-0.5), None, ALU.mult))
            t_a = low_rank(64, 128, aT, "abase")

            t, src = t_lw, lw
            w2 = scratch.get()
            V.w(*w2.free)
            S.w(*w2.free)
            for n_, sh in enumerate((1, 2, 4, 8, 16, 32)):
                dst = cc if n_ % 2 else w2.ap
                V.w(t)
                S.w(t)
                t1 = V.inc(dve.tensor_tensor(c8(dst)[:, :, sh:64], c8(src)[:, :, sh:64], c8(src)[:, :, 0:64 - sh], ALU.add))
                t2 = S.inc(act.activation(c8(dst)[:, :, 0:sh], c8(src)[:, :, 0:sh], ACT.Copy))
                V.w(t2)
                S.w(t1)
                t, src = [t1, t2], dst
            t_c = t
            scratch.put(w2, *t_c)

            V.w(rk[1], rk[0], rk[2])
            tk = V.inc(dve.tensor_scalar(kkT, kT, K("kk", j), None, ALU.mult))
            s = scratch.get()
            S.w(tk, *s.free)
            ts = S.inc(act.activation(s.ap, kkT, ACT.Square))
            b, t = total(s, ts, "blk")
            r = scratch.get()
            V.w(t, *r.free)
            t = V.inc(dve.tensor_scalar(r.ap, b.ap, 1e-24, None, ALU.max))
            banks.put(b, t)
            S.w(t)
            t = S.inc(act.activation(r.ap, r.ap, ACT.Sqrt))
            V.w(t)
            t = V.inc(dve.reciprocal(r.ap, r.ap))
            V.w(t)
            tk = V.inc(dve.tensor_tensor(kkT, kkT, r.ap, ALU.mult))
            scratch.put(r, tk)
            V.w(t_a)
            t = V.inc(dve.tensor_scalar(tm, aT, -1.0, K("ka", j), ALU.add, ALU.mult))
            V.w(t)
            t_k = V.inc(dve.scalar_tensor_tensor(out=kT, in0=tm, scalar=1.0, in1=kT, op0=ALU.add, op1=ALU.mult))
            V.w(tk)
            t_a = V.inc(dve.tensor_tensor(aT, aT, kkT, ALU.mult))

            s = scratch.get()
            V.w(t_k, *s.free)
            t = V.inc(dve.scalar_tensor_tensor(out=s.ap, in0=rT, scalar=K("rk", j), in1=kT, op0=ALU.mult, op1=ALU.mult))
            b, t = total(s, t, "blk")
            V.w(t)
            t = V.inc(dve.tensor_tensor(BV, b.ap, vT, ALU.mult))
            banks.put(b, t)

            e = scratch.get()
            S.w(t_c, *e.free)
            t = S.inc(act.activation(e.ap, cc, ACT.Exp))
            V.w(t)
            PC = tz(144, 152)
            t_pc = V.inc(dve.tensor_copy(PC, c8(e.ap)[:, :, 63]))
            t_R = V.inc(dve.tensor_tensor(AR4[:, :, 1, :], c8(rT), c8(e.ap), ALU.mult))
            scratch.put(e, t_R)
            V.w(t_c)
            t = V.inc(dve.tensor_tensor(tm, cc, lw, ALU.subtract))
            S.w(t)
            t = S.inc(act.activation(tm, tm, ACT.Exp))
            V.w(t)
            t_A = V.inc(dve.scalar_tensor_tensor(out=AR4[:, :, 0, :], in0=c8(kkT), scalar=-1.0, in1=c8(tm),
                                                 op0=ALU.mult, op1=ALU.mult))
            e = scratch.get()
            S.w(*e.free)
            t = S.inc(act.activation(e.ap, cc, ACT.Exp, scale=-1.0))
            V.w(t, t_a, t_pc)
            V.w(t_A)
            for src, dst in ((aT, Bz), (kT, Kz)):
                for h in range(2):
                    t_BK = V.inc(dve.scalar_tensor_tensor(out=dst[h], in0=src, scalar=hm[h], in1=e.ap,
                                                          op0=ALU.mult, op1=ALU.mult))
            V.w(t_BK)
            t = V.inc(dve.tensor_tensor(c8(e.ap), c8(e.ap), bc(PC.unsqueeze(2), [128, 8, 64]), ALU.mult))
            V.w(t)
            V.inc(dve.tensor_tensor(aT, aT, e.ap, ALU.mult))
            t = V.inc(dve.tensor_tensor(kT, kT, e.ap, ALU.mult))
            scratch.put(e, t)
            P.w(t, rk[2])
            for src, dst in ((aT, Bn), (kT, Kn), (vT, Vn)):
                b = banks.get()
                P.w(*b.free)
                for i in range(4):
                    mm = pe.transpose(b.ap[:, 128 * i:128 * i + 128], src[:, 128 * i:128 * i + 128], C("ident"))
                t = P.inc(mm)
                S.w(t)
                t_n = S.inc(act.activation(dst, b.ap, ACT.Copy))
                banks.put(b, t_n)

            P.w(t_R, t_A, t_BK)
            tri = C("tri").unsqueeze(1)
            V.w(t_n)
            for lhs, dst in ((Bz, LR), (Kz, MK)):
                for half in range(2):
                    b = banks.get()
                    P.w(*b.free)
                    for c in range(4 * half, 4 * half + 4):
                        for h in range(2):
                            pr = 64 * (c % 2)
                            col = 128 * (2 * (c // 2 - 2 * half) + h)
                            mm = pe.matmul(b.ap[pr:pr + 64, col:col + 128], lhs[h][:, 64 * c:64 * c + 64],
                                           AR[:, 128 * c:128 * c + 128], start=True, stop=True)
                    t = P.inc(mm)
                    V.w(t)
                    t_m = V.inc(dve.tensor_tensor(dst[:, 512 * half:512 * half + 512].rearrange("p (g n) -> p g n", g=4),
                                                  b.ap.rearrange("p (g n) -> p g n", g=4), bc(tri, [128, 4, 128]), ALU.mult))
                    banks.put(b, t_m)
            b = banks.get()
            P.w(*b.free)
            for c in range(8):
                for h in range(2):
                    pr = 64 * (c % 2)
                    col = 64 * (2 * (c // 2) + h)
                    mm = pe.matmul(b.ap[pr:pr + 64, col:col + 64], AR4[:, c, 0, :],
                                   Bz[h][:, 64 * c:64 * c + 64], start=True, stop=True)
            t = P.inc(mm)
            LT = LR.rearrange("p (g w n) -> p g w n", g=8, w=2)[:, :, 0, :]

            def m8(name):
                return bc(C(name).unsqueeze(1), [128, 8, 64])
            V.w(t)
            t = V.inc(dve.tensor_tensor(c8(X), c8(b.ap), m8("lv1"), ALU.mult))
            banks.put(b, t)
            V.w(t)
            t_X = V.inc(dve.tensor_tensor(c8(X), c8(X), m8("eye"), ALU.add))
            V.w(t_m)
            t = V.inc(dve.tensor_tensor(c8(XT), LT, m8("lt1"), ALU.mult))
            V.w(t)
            t_X = V.inc(dve.tensor_tensor(c8(XT), c8(XT), m8("eye"), ALU.add))

            def small(lhs, rhs):
                b = banks.get()
                P.w(*b.free)
                for c in range(8):
                    for h in range(2):
                        pr = 64 * (c % 2)
                        col = 64 * (2 * (c // 2) + h)
                        mm = pe.matmul(b.ap[pr:pr + 64, col:col + 64], lhs[pr:pr + 64, col:col + 64],
                                       rhs[pr:pr + 64, col:col + 64], start=True, stop=True)
                return b, P.inc(mm)

            t = None
            for m in (2, 4, 8, 16, 32):
                V.w(t)
                t = V.inc(dve.tensor_tensor(c8(Lm), LT, m8(f"lt{m}"), ALU.mult))
                P.w(t, t_X)
                b, t = small(Lm, X)
                S.w(t)
                t = S.inc(act.activation(T1, b.ap, ACT.Copy))
                banks.put(b, t)
                P.w(t)
                if m < 32:
                    b1, u1 = small(XT, T1)
                b2, t = small(T1, XT)
                V.w(t)
                if m < 32:
                    t_x1 = V.inc(dve.tensor_tensor(X, X, b1.ap, ALU.add))
                    banks.put(b1, t_x1)
                t_X = V.inc(dve.tensor_tensor(XT, XT, b2.ap, ALU.add))
                banks.put(b2, t_X)

            P.w(t_X)
            yb = banks.get()
            P.w(*yb.free)
            gu = scratch.get()
            V.w(*gu.free)
            t_S = None
            for c in range(8):
                pr = 64 * (c % 2)
                cp = c // 2
                S0, S1 = STs[c % 2], STs[(c + 1) % 2]
                b = banks.get()
                P.w(*b.free, t_S)
                o = b.ap[pr:pr + 64, 0:128]
                if c:
                    pe.matmul(o, AR4[:, c, 0, :], S0, start=True, stop=False, skip_group_check=True)
                for h in range(2):
                    hr = 64 * h
                    col = 128 * (2 * cp + h)
                    mm = pe.matmul(o[:, hr:hr + 64], MK[pr:pr + 64, col:col + 64],
                                   Vn[pr:pr + 64, 128 * cp + hr:128 * cp + hr + 64], start=c == 0, stop=True,
                                   skip_group_check=True)
                t = P.inc(mm)
                V.w(t)
                t = V.inc(dve.tensor_copy(gu.ap[pr:pr + 64, 0:128], o))
                P.w(t)
                for h in range(2):
                    col = 64 * (2 * cp + h)
                    mm = pe.matmul(b.ap[pr:pr + 64, 128 + 64 * h:192 + 64 * h], XT[pr:pr + 64, col:col + 64],
                                   gu.ap[pr:pr + 64, 64 * h:64 * h + 64], start=True, stop=True)
                t = P.inc(mm)
                V.w(t)
                t = V.inc(dve.tensor_copy(gu.ap[pr:pr + 64, 128:256], b.ap[pr:pr + 64, 128:256]))
                P.w(t)
                u = gu.ap[pr:pr + 64, 128:256]
                v_ = Vn[pr:pr + 64, 128 * cp:128 * cp + 128]
                o = b.ap[:, 256:384]
                pe.matmul(o, Bn[pr:pr + 64, 128 * cp:128 * cp + 128], u, start=True, stop=False)
                t = P.inc(pe.matmul(o, Kn[pr:pr + 64, 128 * cp:128 * cp + 128], v_, start=False, stop=True))
                if c:
                    pe.matmul(yb.ap[:, 64 * c:64 * c + 64], S0, AR4[:, c, 1, :], start=True, stop=False,
                              skip_group_check=True)
                for h in range(2):
                    hr = 64 * h
                    o = yb.ap[hr:hr + 64, 64 * c:64 * c + 64]
                    col = 128 * (2 * cp + h)
                    pe.matmul(o, u[:, hr:hr + 64], LR[pr:pr + 64, col + 64:col + 128], start=c == 0, stop=False,
                              skip_group_check=True)
                    mm = pe.matmul(o, v_[:, hr:hr + 64], MK[pr:pr + 64, col + 64:col + 128], start=False, stop=True,
                                   skip_group_check=True)
                t_Y = P.inc(mm)
                V.w(t)
                for h in range(2):
                    hr = 64 * h
                    d = (slice(hr, hr + 64), slice(hr, hr + 64))
                    ps = b.ap[hr:hr + 64, 256 + hr:320 + hr]
                    if c:
                        t_S = V.inc(dve.scalar_tensor_tensor(out=S1[d], in0=S0[d], scalar=PC[hr:hr + 64, c:c + 1],
                                                             in1=ps, op0=ALU.mult, op1=ALU.add))
                    else:
                        t_S = V.inc(dve.tensor_copy(S1[d], ps))
                V.w(t_S, t_Y)
                banks.put(b, t_S)
            scratch.put(gu, t_Y)
            S.w(t_Y)
            t = S.inc(act.activation(YT, yb.ap, ACT.Copy))
            banks.put(yb, t)

            b = banks.get()
            P.w(*b.free, t)
            t = P.inc(pe.matmul(b.ap, C("blk"), YT, start=True, stop=True))
            V.w(t)
            t = V.inc(dve.scalar_tensor_tensor(out=YT, in0=b.ap, scalar=-1.0 / 64, in1=YT, op0=ALU.mult, op1=ALU.add))
            banks.put(b, t)
            s = scratch.get()
            S.w(t, *s.free)
            ts = S.inc(act.activation(s.ap, YT, ACT.Square))
            b, t = total(s, ts, "blk")
            r, t = inverse_root(b, t, 1.0 / 64, GN_EPS)
            V.w(t)
            t = V.inc(dve.scalar_tensor_tensor(out=YT, in0=YT, scalar=K("gng", j), in1=r.ap, op0=ALU.mult, op1=ALU.mult))
            scratch.put(r, t)
            V.w(t)
            t = V.inc(dve.scalar_tensor_tensor(out=YT, in0=YT, scalar=K("gnb", j), in1=BV, op0=ALU.add, op1=ALU.add))
            b = banks.get()
            P.w(*b.free)
            pe.matmul(b.ap, lora.ap[:, 128:256], GD[:, 0, :], start=True, stop=False)
            tg = P.inc(pe.matmul(b.ap, lora.ap[0:32, 256:384], GD[0:32, 1, :], start=False, stop=True))
            scratch.put(lora, tg)
            V.w(tg, t)
            t_yr = V.inc(dve.tensor_tensor(yr[:, j, :], b.ap, YT, ALU.mult))
            banks.put(b, t_yr)

        if stop in ("rwkv", "attn2"):
            V.w(t_yr)
            t = V.inc(dve.memset(hT[:, 0:4, :], 0.0))
            V.w(t)
            V.w(t_ya)
            V.inc(dve.tensor_copy(hT[:, 0:4, :], ya))
            V.inc(dve.tensor_copy(hT[:, 4:8, :], yr))
            dump(hT[:, :, :])
            return

        fence = everything()
        for q in (V, S):
            q.w(*fence)
        XA = [arr_r[:, o:o + 2048].rearrange("p (k n) -> p k n", n=T) for o in (4096, 6144)]
        XB = [arr_r[:, o:o + 2048].rearrange("p (k n) -> p k n", n=T) for o in (8192, 10240)]
        t1 = split_x(XA[0], XA[1], ya)
        t2 = split_x(XB[0], XB[1], yr)
        gated_branches(XA, XB, [t1, t2], 0)

        def evac_alpha(n0):
            def f(i, b, t):
                V.w(t)
                banks.put(b, V.inc(dve.scalar_tensor_tensor(out=hT[:, n0 + i, :], in0=hT[:, n0 + i, :], scalar=ALPHA,
                                                            in1=b.ap, op0=ALU.mult, op1=ALU.add)))
            return f
        for j in range(4):
            linear(256, xk, evac_alpha(2 * j))
        t = layer_norm("lng", "lnb", 0)
        if stop == "ln3":
            dump(hT[:, :, :])
            return

        fence = everything()
        for q in (V, S, P):
            q.w(*fence)
        RO = ar[:, 14000:15100]

        def R(a, n, *dims):
            v = RO[:, a:a + n]
            if len(dims) == 2:
                return v.rearrange("p (x y) -> p x y", x=dims[0])
            return v
        lg = R(0, 144, 4, 36)
        wrt = K("wrt").rearrange("p (k n) -> p k n", n=36)
        b = banks.get()
        P.w(*b.free)
        for ti in range(4):
            for k in range(KT):
                mm = pe.matmul(b.ap[:, 36 * ti:36 * ti + 36], hT[:, k, 128 * ti:128 * ti + 128], wrt[:, k, :],
                               start=k == 0, stop=k == KT - 1)
        t = P.inc(mm)

        def vv(ins):
            V.w(V.inc(ins))
        V.w(t)
        vv(dve.tensor_tensor(lg, b.ap[:, 0:144].rearrange("p (x y) -> p x y", x=4),
                             bc(K("rbias").unsqueeze(1), [128, 4, 36]), ALU.add))
        banks.put(b, V.last())
        gl, el = lg[:, :, 0:4], lg[:, :, 4:36]
        gm, gs = R(144, 4), R(148, 4)
        gd, oh, eq = R(152, 16, 4, 4), R(168, 16, 4, 4), R(184, 16, 4, 4)
        mx = R(200, 4)
        m1, m2, w1, w2_, dd = R(204, 4), R(208, 4), R(212, 4), R(216, 4), R(220, 4)
        me, oa, ob, qq = R(224, 128, 4, 32), R(352, 128, 4, 32), R(480, 128, 4, 32), R(608, 128, 4, 32)
        comb = R(736, 128, 4, 32)

        def w4(v, n):
            return bc(v.unsqueeze(2), [128, 4, n])
        vv(dve.tensor_reduce(gm, gl, AX.X, ALU.max))
        vv(dve.tensor_tensor(gd, gl, w4(gm, 4), ALU.subtract))
        vv(dve.tensor_scalar(oh, gd, 0.0, None, ALU.is_equal))
        S.w(V.last())
        V.w(S.inc(act.activation(gd, gd, ACT.Exp)))
        vv(dve.tensor_reduce(gs, gd, AX.X, ALU.add))
        vv(dve.reciprocal(gs, gs))
        vv(dve.tensor_tensor(eq, oh, bc(C("gidx").unsqueeze(1), [128, 4, 4]), ALU.mult))
        vv(dve.tensor_reduce(mx, eq, AX.X, ALU.max))
        vv(dve.tensor_tensor(oh, eq, w4(mx, 4), ALU.is_equal))
        vv(dve.tensor_scalar(oh, oh, -1.0, 1.0e30, ALU.add, ALU.mult))
        for g in range(4):
            vv(dve.tensor_tensor(me[:, :, 8 * g:8 * g + 8], el[:, :, 8 * g:8 * g + 8],
                                 w4(oh[:, :, g], 8), ALU.add))

        def first_of(dst, v, m):
            vv(dve.tensor_reduce(m, v, AX.X, ALU.max))
            vv(dve.tensor_tensor(qq, v, w4(m, 32), ALU.is_equal))
            vv(dve.tensor_tensor(qq, qq, bc(C("eidx").unsqueeze(1), [128, 4, 32]), ALU.mult))
            vv(dve.tensor_reduce(mx, qq, AX.X, ALU.max))
            vv(dve.tensor_tensor(dst, qq, w4(mx, 32), ALU.is_equal))
        first_of(oa, me, m1)
        vv(dve.scalar_tensor_tensor(out=me, in0=oa, scalar=-2.0e30, in1=me, op0=ALU.mult, op1=ALU.add))
        first_of(ob, me, m2)
        vv(dve.tensor_tensor(dd, m2, m1, ALU.subtract))
        S.w(V.last())
        V.w(S.inc(act.activation(dd, dd, ACT.Exp)))
        vv(dve.tensor_scalar(w1, dd, 1.0, None, ALU.add))
        vv(dve.reciprocal(w1, w1))
        vv(dve.tensor_tensor(w1, w1, gs, ALU.mult))
        vv(dve.tensor_tensor(w2_, w1, dd, ALU.mult))
        vv(dve.tensor_tensor(oa, oa, w4(w1, 32), ALU.mult))
        vv(dve.tensor_tensor(ob, ob, w4(w2_, 32), ALU.mult))
        vv(dve.tensor_tensor(comb, oa, ob, ALU.add))
        b = banks.get()
        P.w(*b.free, V.last())
        for ti in range(4):
            mm = pe.transpose(b.ap[0:32, 128 * ti:128 * ti + 128], comb[:, ti, :], C("ident"))
        t = P.inc(mm)
        cT = ar[0:32, 13000:13512]
        S.w(t)
        t = S.inc(act.activation(cT, b.ap[0:32, :], ACT.Copy))
        banks.put(b, t)
        P.w(t)

        for k in range(KT):
            t = V.inc(dve.tensor_scalar(hT[:, k, :], hT[:, k, :], ALPHA, None, ALU.mult))
        V.w(t)
        uh = arr_r[:, 0:4096].rearrange("p (k n) -> p k n", n=T)
        ul = arr_r[:, 4096:8192].rearrange("p (k n) -> p k n", n=T)
        for g4 in range(8):
            fence = [P.last()]
            S.w(*fence)
            V.w(*fence)
            for e4 in range(4):
                e = 4 * g4 + e4
                cb = scratch.get()
                b = banks.get()
                P.w(*b.free)
                t = P.inc(pe.matmul(b.ap, C("ident")[0:32, e:e + 1].to_broadcast([32, 128]), cT, start=True, stop=True))
                S.w(t, *cb.free)
                t_cb = S.inc(act.activation(cb.ap, b.ap, ACT.Copy))
                banks.put(b, t_cb)
                sg = {}

                def f_gate(i, b, t):
                    s = scratch.get()
                    S.w(t, *s.free)
                    ts = S.inc(act.activation(s.ap, b.ap, ACT.Silu))
                    banks.put(b, ts)
                    V.w(ts, t_cb)
                    sg[i] = (s, V.inc(dve.tensor_tensor(s.ap, s.ap, cb.ap, ALU.mult)))

                def f_up(i, b, t):
                    s, ts = sg[i]
                    V.w(t, ts)
                    t1 = V.inc(dve.tensor_tensor(s.ap, b.ap, s.ap, ALU.mult))
                    banks.put(b, t1)
                    sg["t"] = split_x(uh[:, 2 * e4 + i, :], ul[:, 2 * e4 + i, :], s.ap, t1)
                    scratch.put(s, sg["t"])
                linear(256, xk, f_gate)
                linear(256, xk, f_up)
                scratch.put(cb, sg["t"])
            P.w(sg["t"])
            ku = [(k, uh[:, k, :], ul[:, k, :]) for k in range(8)]
            for j in range(4):
                linear(256, ku, evac_add(2 * j))
        layer_norm("lng", "lnb", 8)
        if stop == "ln4":
            dump(hT[:, :, :])
            return

        fence = everything()
        for q in (V, S, Y):
            q.w(*fence)
        pt = A3(0, 2)
        ph = arr_r[:, 1024:2048].rearrange("p (k n) -> p k n", n=T)
        pl = arr_r[:, 2048:3072].rearrange("p (k n) -> p k n", n=T)
        pp = A3(4096, 8)
        t = d_p.start(Y, pt, A["pT"][2])
        for k in range(2):
            t1 = split_x(ph[:, k, :], pl[:, k, :], pt[:, k, :], t)
        P.w(t1)
        embed(ph, pl, pp)
        for j in range(4):
            def f_e(i, b, t, j=j):
                s = scratch.get()
                S.w(t, *s.free)
                ts = S.inc(act.activation(s.ap, b.ap, ACT.Sigmoid))
                banks.put(b, ts)
                V.w(ts)
                t1 = V.inc(dve.tensor_tensor(s.ap, s.ap, pp[:, 2 * j + i, :], ALU.mult))
                V.w(t1)
                t1 = V.inc(dve.scalar_tensor_tensor(out=hT[:, 2 * j + i, :], in0=hT[:, 2 * j + i, :], scalar=ALPHA,
                                                    in1=s.ap, op0=ALU.mult, op1=ALU.add))
                scratch.put(s, t1)
            linear(256, xk, f_e)
        t = layer_norm("lng", "lnb", 16, split=False)
        Y.w(t)
        d_o = Dma("d_o")
        Y.w(d_o.start(Y, out, hT[:, :, :]))




def weight_blocks(W):
    blocks = []

    def cols(w, idx, k0=0, k1=None):
        w = w[128 * k0:(128 * k1 if k1 else None)]
        k = w.shape[0] // 128
        return w.reshape(k, 128, w.shape[1])[:, :, idx].transpose(1, 0, 2).reshape(128, -1)

    r = np.arange
    for i in range(2):
        w = W["w_in"][i]
        ka, ki = r(512, 576), r(896, 960)
        qa, qi, qb, kb, vb = r(0, 512), r(640, 896), r(964, 1476), r(1476, 1988), r(1988, 2500)
        blocks.append(cols(w, np.concatenate([ki, ki, qi[:128]])))
        blocks.append(cols(w, np.concatenate([qi[128:], ka, ka])))
        blocks.append(cols(w, np.concatenate([r(576, 640), r(960, 964)])))
        for c in (qa, qb, kb, vb):
            blocks += [cols(w, c[:256]), cols(w, c[256:])]
        for j in range(4):
            s = r(256 * j, 256 * j + 256)
            blocks += [cols(w, 2500 + s), cols(w, 3524 + s)]
            blocks.append(np.concatenate([cols(W["w_branch_a"][i], s), cols(W["w_branch_b"][i], s)], axis=1))
        for j in range(4):
            blocks.append(cols(W["w_out"][i], r(256 * j, 256 * j + 256)))
        f0 = 0
        for c in FCH:
            for j in range(0, c, 2):
                s = r(128 * (f0 + j), 128 * (f0 + j) + 256)
                blocks += [cols(W["w_up"][i], s), cols(W["w_up"][i], 2816 + s)]
            for j in range(4):
                blocks.append(cols(W["w_down"][i], r(256 * j, 256 * j + 256), f0, f0 + c))
            f0 += c
        blocks.append(cols(W["w_ple_proj"][i], r(1024)))
        for j in range(4):
            blocks.append(cols(W["w_ple_gate"][i], r(256 * j, 256 * j + 256)))
    w = W["w_in_2"][0]
    for c in (r(0, 512), r(512, 1024), r(1024, 1536)):
        blocks += [cols(w, c[:256]), cols(w, c[256:])]
    RW = 1536
    blocks.append(cols(w, r(RW + 1536, RW + 1792)))
    blocks.append(cols(w, r(RW + 1792, RW + 1824)))
    for j in range(4):
        s = r(RW + 128 * j, RW + 128 * j + 128)
        blocks += [cols(w, np.concatenate([s, 512 + s])), cols(w, 1024 + s)]
    for j in range(4):
        s = r(256 * j, 256 * j + 256)
        blocks += [cols(w, 3360 + s), cols(w, 4384 + s)]
        blocks.append(np.concatenate([cols(W["w_branch_attn_2"][0], s), cols(W["w_branch_rwkv_2"][0], s)], axis=1))
    for j in range(4):
        blocks.append(cols(W["w_out_2"][0], r(256 * j, 256 * j + 256)))
    for g4 in range(8):
        for e in range(4 * g4, 4 * g4 + 4):
            blocks += [cols(W["exp_gate_2"][0, e], r(256)), cols(W["exp_up_2"][0, e], r(256))]
        down = W["exp_down_2"][0, 4 * g4:4 * g4 + 4].reshape(1024, 1024)
        for j in range(4):
            blocks.append(cols(down, r(256 * j, 256 * j + 256)))
    blocks.append(cols(W["ple_proj_2"][0], r(1024)))
    for j in range(4):
        blocks.append(cols(W["ple_gate_2"][0], r(256 * j, 256 * j + 256)))
    return blocks


def columns(v):
    return np.asarray(v).reshape(-1, 128).T


def lay_out(inp):
    W = {k: np.asarray(v) for k, v in inp.items()}
    consts, cparts = const_table()
    parts, n_small = small_columns()
    small = np.zeros((128, n_small), np.float32)

    def put(name, a):
        x, y = parts[name]
        small[:, x:y] = a

    def twice(v):
        return np.concatenate([v, v])[:, None]

    for i in range(2):
        put(f"gmix{i}", columns(W["g_mix_norm"][i]))
        for n, s in (("gqa", "g_qa"), ("gka", "g_ka"), ("gqb", "g_qb"), ("gkb", "g_kb")):
            put(f"{n}{i}", twice(W[s][i]))
        put(f"gsub{i}", W["g_subln"][i][:, None])
        a, _ = parts[f"lam{i}"]
        for j, s in enumerate(("lam_q1", "lam_k1", "lam_q2", "lam_k2")):
            small[0:64, a + j] = W[s][i]
        put(f"gffn{i}", columns(W["g_ffn_norm"][i]))
        for j in range(3):
            put(f"cw{j}{i}", columns(W["conv_w"][i, j]))
        put(f"cb{i}", columns(W["conv_b"][i]))
        put(f"gple{i}", columns(W["g_ple_norm"][i]))
    put("lnig", columns(W["ln_in_g_2"]))
    put("lnib", columns(W["ln_in_b_2"]))
    a, _ = parts["mu"]
    mu = W["tok_mix_2"][0]
    small[:, a:a + 14] = columns(mu[:1792])
    small[0:32, a + 14] = mu[1792:]
    for n, s in (("dbase", "decay_base_2"), ("abase", "aaa_base_2"), ("kk", "k_k_2"), ("ka", "k_a_2"),
                 ("gng", "gn_g_2"), ("gnb", "gn_b_2")):
        put(n, columns(W[s][0]))
    put("rk", columns(W["r_k_2"][0].reshape(-1)))
    put("lng", columns(W["ln_g_2"][0].reshape(-1)))
    put("lnb", columns(W["ln_b_2"][0].reshape(-1)))
    put("rbias", np.concatenate([W["router_grp_bias_2"][0], W["router_exp_bias_2"][0]])[None, :])
    wr = np.concatenate([W["router_grp_2"][0], W["router_exp_2"][0]], axis=1)
    put("wrt", wr.reshape(8, 128, 36).transpose(1, 0, 2).reshape(128, -1))
    lora = np.zeros((4, 128, 384), np.float32)
    for j in range(4):
        c = slice(128 * j, 128 * j + 128)
        lora[j, 0:64, 0:128] = W["decay_up_2"][0][:, c]
        lora[j, 64:128, 0:128] = W["aaa_up_2"][0][:, c]
        lora[j, :, 128:256] = W["gate_up_2"][0][0:128, c]
        lora[j, 0:32, 256:384] = W["gate_up_2"][0][128:160, c]
    dist = 384 + np.arange(128)[:, None] - np.arange(512)[None, :]
    bias = W["rel_bias_2"][:, np.clip(dist, -128, 128) + 128]
    p_all = np.concatenate([W["p"][:, 0], W["p_2"][:, 0]])
    tiles = {
        "lora": lora,
        "bias": np.ascontiguousarray(bias.transpose(1, 0, 2).reshape(128, -1)),
        "consts": consts,
        "small": small,
        "xT": np.ascontiguousarray(W["x"][0].T.reshape(8, 128, 512).transpose(1, 0, 2)),
        "pT": np.ascontiguousarray(p_all.transpose(0, 2, 1).reshape(3, 2, 128, 512).transpose(0, 2, 1, 3)),
    }
    blocks = weight_blocks(W)
    sizes = [b.shape[1] for b in blocks]
    big = np.zeros((len(blocks), 128, BLK), np.float32)
    for i, b in enumerate(blocks):
        big[i, :, :b.shape[1]] = b
    tiles["W"] = big
    return tiles, sizes, cparts


def kernel(**inputs):
    import concourse.bacc as _bacc
    from concourse.bass_utils import run_bass_kernel_spmd as _run

    tiles, sizes, cparts = lay_out(inputs)
    nc = _bacc.Bacc("TRN2", target_bir_lowering=False, num_devices=1)
    arrays, args = {}, {}
    for name, a in tiles.items():
        arrays[f"in_{name}"] = a
        args[name] = nc.dram_tensor(f"in_{name}", a.shape, mybir.dt.from_np(a.dtype), kind="ExternalInput").ap()
    out = nc.dram_tensor("out_y", (128, 8, 512), F32, kind="ExternalOutput").ap()
    program(nc, args, out, sizes, cparts)
    r = _run(nc, [arrays], core_ids=[0])
    y = np.asarray(r.results[0]["out_y"])
    return y.transpose(1, 0, 2).reshape(1024, 512).T.reshape(1, 512, 1024)
```

```python
import math
from contextlib import ExitStack

import numpy as np

import concourse.bass as bass
from concourse import mybir

F32 = mybir.dt.float32
F32R = mybir.dt.float32r
ALU = mybir.AluOpType
ACT = mybir.ActivationFunctionType
AX = mybir.AxisListType

T = 512
D = 1024
KT = 8
NEG = -1.0e30
GONE = -3.0e38
EPS = 1e-6
LN_EPS = 1e-5
GN_EPS = 64e-5
ALPHA = 2.0 ** 0.25
BLK = 2048
FCH = [8, 8, 6]
NT = 39
MOEC = 13624
POOL_CUTS = (2, 5)



def const_table():
    parts = {}
    out = []
    at = 0

    def put(name, a):
        nonlocal at
        a = np.asarray(a, np.float32).reshape(128, -1)
        parts[name] = (at, at + a.shape[1])
        at += a.shape[1]
        out.append(a)

    p = np.arange(128)
    put("ident", np.eye(128))
    put("ones", np.ones((128, 128)))
    put("blk", (p[:, None] // 64) == (p[None, :] // 64))
    swap = (p // 64) * 64 + (p % 64 + 32) % 64
    put("rot", (p[:, None] == swap[None, :]))
    inv = (np.float32(1) / np.power(np.float32(10000), np.arange(0, 64, 2, dtype=np.float32) / np.float32(64))).astype(np.float32)
    ang = (np.arange(T, dtype=np.float32)[:, None] * inv[None, :]).astype(np.float64).T
    cos, sin = np.cos(ang)[p % 32], np.sin(ang)[p % 32]
    put("cos", cos)
    put("sin", np.where((p % 64 < 32)[:, None], -sin, sin))
    x = np.arange(T)
    put("causal", np.where(x[None, :] - 384 <= p[:, None], 0.0, NEG))
    put("chunk", np.where(p[:, None] < 64, NEG, 0.0) * np.ones((1, 64)))
    s = (p % 64)[:, None]
    t = np.arange(64)[None, :]
    put("eye", s == t)
    put("tri", np.concatenate([s < t, s <= t], axis=1))
    put("lv1", (s // 2 == t // 2) & (s % 2 == 1) & (t % 2 == 0))
    for m in (1, 2, 4, 8, 16, 32):
        put(f"lt{m}", (s // (2 * m) == t // (2 * m)) & (s % (2 * m) < m) & (t % (2 * m) >= m))
    hs = np.zeros((128, 4, 8))
    hb = np.zeros((128, 4, 128))
    for j in range(4):
        for h in range(2):
            hs[64 * h:64 * h + 64, j, 2 * j + h] = 1
            hb[2 * j + h, j, 64 * h:64 * h + 64] = 1
    put("hsel", hs)
    put("hbr", hb)
    put("gidx", np.broadcast_to(8 - np.arange(4), (128, 4)))
    put("eidx", np.broadcast_to(64 - np.arange(32), (128, 32)))
    return np.concatenate(out, axis=1), parts


def small_columns():
    at = 0
    parts = {}
    for i in range(2):
        for name, n in (("gmix", 8), ("gqa", 1), ("gka", 1), ("gqb", 1), ("gkb", 1), ("gsub", 1), ("lam", 4),
                        ("gffn", 8), ("cw0", 44), ("cw1", 44), ("cw2", 44), ("cb", 44), ("gple", 8)):
            parts[f"{name}{i}"] = (at, at + n)
            at += n
    for name, n in (("lnig", 8), ("lnib", 8), ("mu", 15), ("dbase", 4), ("abase", 4), ("kk", 4), ("ka", 4),
                    ("rk", 4), ("gng", 4), ("gnb", 4), ("lng", 24), ("lnb", 24), ("rbias", 36), ("wrt", 288)):
        parts[name] = (at, at + n)
        at += n
    return parts, at


class Queue:

    def __init__(self, engine, sem, name):
        self.engine, self.sem, self.name = engine, sem, name
        self.count = 0
        self.seen = {}

    def w(self, *tickets):
        for t in tickets:
            if t is None:
                continue
            if isinstance(t, list):
                self.w(*t)
                continue
            sem, name, value = t
            if self.seen.get(name, 0) < value:
                self.engine.wait_ge(sem, value)
                self.seen[name] = value

    def inc(self, ins):
        self.count += 1
        ins.then_inc(self.sem, 1)
        return (self.sem, self.name, self.count)

    def last(self):
        return (self.sem, self.name, self.count) if self.count else None


class Slot:
    def __init__(self, ap):
        self.ap = ap
        self.free = []


class Pool:

    def __init__(self, aps):
        self.slots = [Slot(a) for a in aps]

    def get(self):
        assert self.slots, "no slot is free"
        return self.slots.pop(0)

    def put(self, slot, *tickets):
        slot.free = list(tickets)
        self.slots.append(slot)


def program(nc, A, out, sizes, cparts, stop=None, dbg=None):
    sp, n_small = small_columns()
    n_const = A["consts"].shape[1]
    ctx = ExitStack()
    with ctx:
        def sb(name, shape, dt=F32):
            return ctx.enter_context(nc.sbuf_tensor(name, shape, dt))

        def sem(name):
            return ctx.enter_context(nc.semaphore(name))

        pe, dve, act, pool, sync = nc.tensor, nc.vector, nc.scalar, nc.gpsimd, nc.sync
        P = Queue(pe, sem("s_pe"), "pe")
        V = Queue(dve, sem("s_dve"), "dve")
        S = Queue(act, sem("s_act"), "act")
        G = Queue(pool, sem("s_pool"), "pool")
        Y = Queue(sync, None, "sync")

        class Dma:

            def __init__(self, name):
                self.sem, self.name, self.n = sem(name), name, 0

            def start(self, queue, dst, src):
                self.n += 16
                queue.engine.dma_start(dst, src).then_inc(self.sem, 16)
                return (self.sem, self.name, self.n)

        hT = sb("hT", [128, KT, T])
        XH = sb("XH", [128, KT, T], F32R)
        XL = sb("XL", [128, KT, T], F32R)
        raw = sb("raw", [128, 2, BLK])
        wh = sb("wh", [128, 3, BLK], F32R)
        wl = sb("wl", [128, 3, BLK], F32R)
        cst = sb("cst", [128, n_const])
        sml = sb("sml", [128, n_small])
        NAR = 15120
        base = (nc.sbuf_base + 31) // 32 * 32
        ar = sb("arena", [128, NAR])
        rounded = nc.alloc_sbuf_tensor_at("arena_rounded", [128, NAR], F32R, offset=base)
        arr_r = rounded[:, :]
        slots = sb("slots", [128, 2, NT], mybir.dt.int32)
        owner = sb("owner", [1, 128], mybir.dt.int32)
        xtok = nc.dram_tensor("xtok", (T, D), F32, kind="Internal").ap()
        ytok = nc.dram_tensor("ytok", (2 * T, D), F32, kind="Internal").ap()
        scr = sb("scr", [128, 9, T])
        tiny = sb("tiny", [128, 256])
        weight = tiny[:, 0:8]

        def C(name):
            a, b = cparts[name]
            return cst[:, a:b]

        def K(name, j=None):
            a, b = sp[name]
            return sml[:, a:b] if j is None else sml[:, a + j:a + j + 1]

        banks = Pool([ctx.enter_context(nc.psum_tensor(f"bank{i}", [128, T], F32))[:, :] for i in range(8)])
        scratch = Pool([scr[:, i, :] for i in range(9)])

        def everything():
            return [P.last(), V.last(), S.last(), G.last()]

        d_c, d_s, d_x = Dma("d_c"), Dma("d_s"), Dma("d_x")
        t_c = d_c.start(Y, cst[:, :], A["consts"])
        t_s = d_s.start(Y, sml[:, :], A["small"])
        t_x = d_x.start(Y, hT[:, :, :], A["xT"])
        for q in (P, V, S, G):
            q.w(t_c, t_s, t_x)

        d_raw = [Dma(f"d_raw{i}") for i in range(2)]

        class Stream:
            def __init__(self):
                self.loaded = 0
                self.split = 0
                self.used = 0
                self.raw_t = []
                self.split_t = []
                self.done = {}

            def load(self):
                n = self.loaded
                if n >= len(sizes):
                    return
                if n >= 2:
                    Y.w(*self.split_t[n - 2])
                k = sizes[n]
                self.raw_t.append(d_raw[n % 2].start(Y, raw[:, n % 2, 0:k], A["W"][n, :, 0:k]))
                self.loaded += 1

            def cut(self):
                n = self.split
                if n >= len(sizes):
                    return
                k = sizes[n]
                r, h, l = raw[:, n % 2, 0:k], wh[:, n % 3, 0:k], wl[:, n % 3, 0:k]
                if n >= 3:
                    S.w(self.done[n - 3])
                    V.w(self.done[n - 3])
                S.w(self.raw_t[n])
                th = S.inc(act.activation(h, r, ACT.Copy))
                V.w(th, self.raw_t[n])
                tl = V.inc(dve.tensor_tensor(l, r, h.bitcast(F32), ALU.subtract))
                self.split_t.append((th, tl))
                self.split += 1
                self.load()

            def next(self, n_cols):
                n = self.used
                self.used += 1
                while self.split <= n:
                    self.cut()
                P.w(*self.split_t[n])
                k = sizes[n]
                return [x[:, n % 3, 0:k].rearrange("p (k n) -> p k n", n=n_cols) for x in (wh, wl)]

            def finished(self, ticket):
                self.done[self.used - 1] = ticket
                while self.split < self.used + 2:
                    if self.split >= len(sizes) or (self.split >= 3 and self.split - 3 not in self.done):
                        break
                    self.cut()

        stream = Stream()
        for _ in range(2):
            stream.load()

        bg = []

        def background(n):
            while n and bg:
                if next(bg[0], None) is None:
                    bg.pop(0)
                n -= 1

        later = []

        def settle(n):
            while n and later:
                if next(later[0], None) is None:
                    later.pop(0)
                n -= 1

        def units(jobs, every=1, fill=0):
            jobs, live, r = list(jobs), [], 0
            while jobs or live:
                if jobs and r % every == 0:
                    live.append(jobs.pop(0))
                r += 1
                live = [g for g in live if next(g, None) is not None]
                background(fill)

        def products(ps, w, x, ks, c0, c1, first, last):
            h, l = w
            n = len(ks)
            for i, (k, xh, xl) in enumerate(ks):
                a, z = first and i == 0, last and i == n - 1
                pe.matmul(ps, h[:, k, c0:c1], xh, start=a, stop=False)
                pe.matmul(ps, h[:, k, c0:c1], xl, start=False, stop=False)
                mm = pe.matmul(ps, l[:, k, c0:c1], xh, start=False, stop=z)
            return P.inc(mm)

        def linear(n_cols, ks, evac, step=3):
            w = stream.next(n_cols)
            got = []
            for i in range((n_cols + 127) // 128):
                m = min(128, n_cols - 128 * i)
                b = banks.get()
                P.w(*b.free)
                t = products(b.ap[0:m, :], w, None, ks, 128 * i, 128 * i + m, True, True)
                got.append((b, t))
            stream.finished(t)
            for i, (b, t) in enumerate(got):
                evac(i, b, t)
            settle(3)
            background(step)

        def natural(n_cols, evac):
            h, l = stream.next(n_cols)
            got = []
            for ti in range(4):
                b = banks.get()
                P.w(*b.free)
                tt = slice(128 * ti, 128 * ti + 128)
                for k in range(KT):
                    pe.matmul(b.ap[:, 0:n_cols], XH[:, k, tt], h[:, k, :], start=k == 0, stop=False)
                    pe.matmul(b.ap[:, 0:n_cols], XL[:, k, tt], h[:, k, :], start=False, stop=False)
                    mm = pe.matmul(b.ap[:, 0:n_cols], XH[:, k, tt], l[:, k, :], start=False, stop=k == KT - 1)
                got.append((b, P.inc(mm)))
            stream.finished(got[-1][1])
            for ti, (b, t) in enumerate(got):
                evac(ti, b, t)
            settle(3)
            background(3)

        xk = [(k, XH[:, k, :], XL[:, k, :]) for k in range(KT)]

        def square_sum(src, ready):
            acc, tmp = scratch.get(), scratch.get()
            t = None
            sq = [tmp, scratch.get()]
            free = [tmp.free, sq[1].free]
            S.w(*ready, *acc.free)
            t_acc = S.inc(act.activation(acc.ap, src(0), ACT.Square))
            for k in range(1, KT):
                s = sq[k % 2]
                S.w(*free[k % 2])
                t = S.inc(act.activation(s.ap, src(k), ACT.Square))
                V.w(t, t_acc)
                t_acc = V.inc(dve.tensor_tensor(acc.ap, acc.ap, s.ap, ALU.add))
                free[k % 2] = [t_acc]
            for s in sq:
                scratch.put(s, t_acc)
            return acc, t_acc

        def total(acc, t_acc, ones="ones"):
            b = banks.get()
            P.w(*b.free, t_acc)
            t = P.inc(pe.matmul(b.ap, C(ones), acc.ap, start=True, stop=True))
            scratch.put(acc, t)
            return b, t

        def inverse_root(b, t, scale, eps):
            r = scratch.get()
            V.w(t, *r.free)
            t1 = V.inc(dve.tensor_scalar(r.ap, b.ap, scale, eps, ALU.mult, ALU.add))
            banks.put(b, t1)
            S.w(t1)
            t2 = S.inc(act.activation(r.ap, r.ap, ACT.Sqrt))
            V.w(t2)
            t3 = V.inc(dve.reciprocal(r.ap, r.ap))
            return r, t3

        def split_x(dh, dl, src, *tickets):
            S.w(*tickets)
            th = S.inc(act.activation(dh, src, ACT.Copy))
            V.w(th, *tickets)
            return V.inc(dve.tensor_tensor(dl, src, dh.bitcast(F32), ALU.subtract))

        def rms(gain):
            fence = everything()
            acc, t = square_sum(lambda k: hT[:, k, :], fence)
            b, t = total(acc, t)
            r, t = inverse_root(b, t, 1.0 / D, EPS)
            V.w(*fence, t)
            for k in range(KT):
                u = scratch.get()
                V.w(*u.free)
                tu = V.inc(dve.scalar_tensor_tensor(out=u.ap, in0=hT[:, k, :], scalar=K(gain, k), in1=r.ap,
                                                    op0=ALU.mult, op1=ALU.mult))
                S.w(*fence)
                t = split_x(XH[:, k, :], XL[:, k, :], u.ap, tu)
                scratch.put(u, t, tu)
                P.w(t)
            scratch.put(r, t)

        def layer_norm(g, b_, j, split=True):
            fence = everything()
            s = scratch.get()
            V.w(*fence, *s.free)
            t = V.inc(dve.tensor_tensor(s.ap, hT[:, 0, :], hT[:, 1, :], ALU.add))
            for k in range(2, KT):
                V.w(t)
                t = V.inc(dve.tensor_tensor(s.ap, s.ap, hT[:, k, :], ALU.add))
            b, t = total(s, t)
            for k in range(KT):
                V.w(t)
                tk = V.inc(dve.scalar_tensor_tensor(out=hT[:, k, :], in0=b.ap, scalar=-1.0 / D, in1=hT[:, k, :],
                                                    op0=ALU.mult, op1=ALU.add))
            banks.put(b, tk)
            acc, t = square_sum(lambda k: hT[:, k, :], [tk])
            b, t = total(acc, t)
            r, t = inverse_root(b, t, 1.0 / D, LN_EPS)
            for k in range(KT):
                V.w(t)
                t1 = V.inc(dve.scalar_tensor_tensor(out=hT[:, k, :], in0=hT[:, k, :], scalar=K(g, j + k), in1=r.ap,
                                                    op0=ALU.mult, op1=ALU.mult))
                V.w(t1)
                t1 = V.inc(dve.tensor_scalar(hT[:, k, :], hT[:, k, :], K(b_, j + k), None, ALU.add))
                if split:
                    S.w(*fence)
                    t1 = split_x(XH[:, k, :], XL[:, k, :], hT[:, k, :], t1)
                    P.w(t1)
            scratch.put(r, t1)
            return t1

        def rope(dst, t_dst, scale=None):
            b = banks.get()
            P.w(*b.free, t_dst)
            t = P.inc(pe.matmul(b.ap, C("rot"), dst, start=True, stop=True))
            u = scratch.get()
            V.w(t, *u.free)
            t1 = V.inc(dve.tensor_tensor(u.ap, b.ap, C("sin"), ALU.mult))
            banks.put(b, t1)
            G.w(t_dst, t)
            t2 = G.inc(pool.tensor_tensor(dst, dst, C("cos"), ALU.mult))
            V.w(t1, t2)
            t3 = V.inc(dve.tensor_tensor(dst, dst, u.ap, ALU.add))
            scratch.put(u, t3)
            if scale is not None:
                sb_, ts = scale
                V.w(ts, t3)
                t3 = V.inc(dve.tensor_tensor(dst, dst, sb_.ap, ALU.mult))
                banks.put(sb_, t3)
            return t3

        class HeadNorm:

            def __init__(self, n):
                self.n = n
                self.b = banks.get()
                P.w(*self.b.free)
                self.tiles = []

            def add(self, dst, gain, b, t):
                j = len(self.tiles)
                s = scratch.get()
                S.w(t, *s.free)
                ts = S.inc(act.activation(s.ap, b.ap, ACT.Square))
                V.w(ts)
                td = V.inc(dve.tensor_scalar(dst, b.ap, K(gain, 0), None, ALU.mult))
                banks.put(b, ts, td)
                P.w(ts)
                a, _ = cparts["hsel"]
                self.tp = P.inc(pe.matmul(self.b.ap[0:8, :], cst[:, a + 8 * j:a + 8 * j + 8], s.ap,
                                          start=j == 0, stop=j == self.n - 1))
                scratch.put(s, self.tp)
                self.tiles.append((dst, td))

            def close(self, put):
                n = 2 * self.n
                r = scratch.get()
                V.w(self.tp, *r.free)
                t1 = V.inc(dve.tensor_scalar(r.ap[0:n, :], self.b.ap[0:n, :], 1.0 / 64, EPS, ALU.mult, ALU.add))
                banks.put(self.b, t1)
                S.w(t1)
                t2 = S.inc(act.activation(r.ap[0:n, :], r.ap[0:n, :], ACT.Sqrt))
                V.w(t2)
                t3 = V.inc(dve.reciprocal(r.ap[0:n, :], r.ap[0:n, :]))
                yield True
                a, _ = cparts["hbr"]
                for j, (dst, td) in enumerate(self.tiles):
                    b = banks.get()
                    P.w(*b.free, t3)
                    t = P.inc(pe.matmul(b.ap, cst[0:n, a + 128 * j:a + 128 * j + 128], r.ap[0:n, :],
                                        start=True, stop=True))
                    if j == self.n - 1:
                        scratch.put(r, t)
                    put(j, rope(dst, td, (b, t)))
                    yield True

        def tz(a, b=None):
            return tiny[:, a:a + 1] if b is None else tiny[:, a:b]

        cols = [0]

        def tiny4():
            cols[0] = (cols[0] + 1) % 16
            return 160 + 4 * cols[0]

        def probs(q, k, mask, n, scale, tq, got):
            b = banks.get()
            P.w(*b.free, *tq)
            t = P.inc(pe.matmul(b.ap[:, 0:n], q, k, start=True, stop=True))
            yield True
            s, c = scratch.get(), tiny4()
            V.w(t, *s.free, *tq)
            t1 = V.inc(dve.tensor_tensor_reduce(s.ap[:, 0:n], b.ap[:, 0:n], mask, scale, GONE, ALU.add, ALU.max, tz(c)))
            banks.put(b, t1)
            V.w(t1)
            t2 = V.inc(dve.tensor_scalar(tz(c + 1), tz(c), -1.0, None, ALU.mult))
            yield True
            S.w(t2)
            t3 = S.inc(act.activation(s.ap[:, 0:n], s.ap[:, 0:n], ACT.Exp, bias=tz(c + 1), accum_out=tz(c + 2)))
            yield True
            V.w(t3)
            t4 = V.inc(dve.reciprocal(tz(c + 3), tz(c + 2)))
            V.w(t4)
            got.append((s, c, t4))

        def turned(s, t, ti, got):
            n = 128 * (ti + 1)
            b = banks.get()
            P.w(*b.free, t)
            for j in range(ti + 1):
                mm = pe.transpose(b.ap[:, 128 * j:128 * j + 128], s.ap[:, 128 * j:128 * j + 128], C("ident"))
            tt = P.inc(mm)
            scratch.put(s, tt)
            yield True
            o = scratch.get()
            S.w(tt, *o.free)
            to = S.inc(act.activation(o.ap[:, 0:n], b.ap[:, 0:n], ACT.Copy))
            banks.put(b, to)
            yield True
            P.w(to)
            got.append(o)

        def attend(q, k, v, mask, ti, tq, acc, out_ap, first, finish):
            n = 128 * (ti + 1)
            got = []
            yield from probs(q, k, mask, n, 0.125, tq, got)
            s, c, t = got.pop()
            t = V.inc(dve.tensor_scalar(s.ap[:, 0:n], s.ap[:, 0:n], tz(c + 3), None, ALU.mult))
            yield True
            yield from turned(s, t, ti, got)
            o = got.pop()
            if first:
                acc.append(banks.get())
                P.w(*acc[0].free)
            for j in range(ti + 1):
                mm = pe.matmul(out_ap(acc[0]), v(j), o.ap[:, 128 * j:128 * j + 128], start=j == 0, stop=j == ti)
            t = P.inc(mm)
            scratch.put(o, t)
            yield True
            if finish:
                yield from finish(acc[0], t)

        def A_(off, n):
            return ar[:, off:off + n]

        def A3(off, k, n=T):
            return ar[:, off:off + k * n].rearrange("p (k n) -> p k n", n=n)

        def evac_add(n0):
            def f(i, b, t):
                V.w(t)
                banks.put(b, V.inc(dve.tensor_tensor(hT[:, n0 + i, :], b.ap, hT[:, n0 + i, :], ALU.add)))
            return f

        def dump(src, *tickets):
            d = Dma("d_dump")
            Y.w(*everything())
            t = d.start(Y, out, src)
            Y.w(t)

        def gated_branches(XA, XB, t_in, c0):
            mixf = A3(c0, 8)
            fence = everything()
            V.w(*fence)
            for j in range(4):
                sg = {}

                def gate(which):
                    def f(i, b, t):
                        s = scratch.get()
                        S.w(t, *s.free)
                        ts = S.inc(act.activation(s.ap, b.ap, ACT.Sigmoid))
                        banks.put(b, ts)
                        sg[which, i] = (s, ts)
                    return f
                linear(256, xk, gate(0))
                linear(256, xk, gate(1))
                w = stream.next(256)
                P.w(*t_in)
                done = []
                for i in range(2):
                    for which, X in ((0, XA), (1, XB)):
                        b = banks.get()
                        P.w(*b.free)
                        t = products(b.ap, w, None, [(4 * which + k, X[0][:, k, :], X[1][:, k, :]) for k in range(4)],
                                     128 * i, 128 * i + 128, True, True)
                        done.append((i, which, b, t))
                stream.finished(t)
                for i, which, b, t in done:
                    s, ts = sg[which, i]
                    o = mixf[:, 2 * j + i, :]
                    V.w(t, ts)
                    if which == 0:
                        t0 = V.inc(dve.tensor_tensor(o, b.ap, s.ap, ALU.mult))
                        banks.put(b, t0)
                        scratch.put(s, t0)
                    else:
                        t1 = V.inc(dve.tensor_tensor(s.ap, b.ap, s.ap, ALU.mult))
                        banks.put(b, t1)
                        V.w(t0, t1)
                        t2 = V.inc(dve.tensor_tensor(o, o, s.ap, ALU.add))
                        scratch.put(s, t2)
            fence = everything()
            for k in range(KT):
                S.w(*fence)
                V.w(*fence)
                P.w(split_x(XH[:, k, :], XL[:, k, :], mixf[:, k, :], t2))

        def first_layer(li):
            lam_init = 0.8 - 0.6 * math.exp(-0.3 * li)
            o = 0

            def take(n):
                nonlocal o
                o += n
                return o - n
            KI, QI = take(512), take(1024)
            o = 2048
            OBL = take(2048)
            KA, WV, QA, MB = take(512), take(4 * 68), take(2048), take(2048)
            QB, KB, VB = take(2048), take(2048), take(2048)
            assert o <= NAR
            rms(f"gmix{li}")
            fence = everything()
            for q in (V, S, P):
                q.w(*fence)
            ready = {}

            b = banks.get()
            t = None
            for j in range(2):
                t = V.inc(dve.tensor_tensor(tz(60 + j), K(f"lam{li}", 2 * j), K(f"lam{li}", 2 * j + 1), ALU.mult))
            P.w(*b.free, t)
            t = P.inc(pe.matmul(b.ap[:, 0:2], C("ones"), tz(60, 62), start=True, stop=True))
            S.w(t)
            t = S.inc(act.activation(tz(62, 64), b.ap[:, 0:2], ACT.Exp))
            banks.put(b, t)
            V.w(t)
            t = V.inc(dve.tensor_tensor(tz(64), tz(63), tz(62), ALU.subtract))
            V.w(t)
            t_lam = V.inc(dve.tensor_scalar(tz(65), tz(64), -lam_init, None, ALU.add))

            def keep(dst, name):
                def f(b, t):
                    V.w(t)
                    td = V.inc(dve.tensor_copy(dst, b.ap))
                    banks.put(b, td)

                    def turn():
                        ready[name] = rope(dst, td)
                        yield True
                    later.append(turn())
                return f

            hk = HeadNorm(1)
            linear(256, xk, lambda i, b, t: keep(A_(KI, 512), "ki")(b, t) if i == 0 else keep(A_(QI, 512), "qi0")(b, t))
            linear(256, xk, lambda i, b, t: keep(A_(QI + 512, 512), "qi1")(b, t) if i == 0
                   else hk.add(A_(KA, 512), f"gka{li}", b, t))
            wv = A3(WV, 4, 68)

            def evac_wv(ti, b, t):
                V.w(t)
                ready["wv", ti] = V.inc(dve.tensor_copy(wv[:, ti, :], b.ap[:, 0:68]))
                banks.put(b, ready["wv", ti])
            natural(68, evac_wv)
            later.append(hk.close(lambda j, t: ready.__setitem__("ka", t)))
            settle(3)

            mb = A3(MB, 4)
            t_mask = {0: None}

            def scores(ti):
                n = 128 * (ti + 1)
                t_prev = None
                V.w(ready["wv", ti])
                for h in range(4):
                    r0 = 64 * (h % 2)
                    b = banks.get()
                    P.w(*b.free, ready["ki"], ready[f"qi{h // 2}"])
                    t = P.inc(pe.matmul(b.ap[:, 0:n], A_(QI + 512 * (h // 2), 512)[r0:r0 + 64, 128 * ti:128 * ti + 128],
                                        A_(KI, 512)[r0:r0 + 64, 0:n], start=True, stop=True))
                    s = scratch.get()
                    S.w(t, *s.free)
                    t = S.inc(act.activation(s.ap[:, 0:n], b.ap[:, 0:n], ACT.Relu, scale=1.0 / 16))
                    banks.put(b, t)
                    w_ = wv[:, ti, 64 + h:65 + h]
                    V.w(t, t_prev)
                    if h == 0:
                        t_prev = V.inc(dve.tensor_scalar(mb[:, ti, 0:n], s.ap[:, 0:n], w_, None, ALU.mult))
                    else:
                        t_prev = V.inc(dve.scalar_tensor_tensor(out=mb[:, ti, 0:n], in0=s.ap[:, 0:n], scalar=w_,
                                                                in1=mb[:, ti, 0:n], op0=ALU.mult, op1=ALU.add))
                    scratch.put(s, t_prev)
                V.w(t_prev)
                return V.inc(dve.tensor_tensor(mb[:, ti, 0:n], mb[:, ti, 0:n], C("causal")[:, 512 - n:512], ALU.add))

            def choose(ti, t):
                n = 128 * (ti + 1)
                m = mb[:, ti, 0:n]
                top = tz(64 + 8 * ti, 72 + 8 * ti)
                for r in range(16):
                    V.w(t)
                    t = V.inc(dve.max(top, m))
                    yield t
                    V.w(t)
                    t = V.inc(dve.match_replace(m, top, m, GONE))
                    yield t
                V.w(t)
                t = V.inc(dve.tensor_scalar(m, m, -2.0e38, NEG, ALU.is_gt, ALU.mult))
                V.w(t)
                t_mask[ti] = V.inc(dve.tensor_tensor(m, m, C("causal")[:, 512 - n:512], ALU.add))
                yield t_mask[ti]

            for ti in (1, 2, 3):
                bg.append(choose(ti, scores(ti)))

            hn = HeadNorm(4)
            for j in range(2):
                linear(256, xk, lambda i, b, t, j=j: hn.add(A_(QA + 512 * (2 * j + i), 512), f"gqa{li}", b, t), 8)
            tqa, tqb, tkb = {}, {}, {}
            later.append(hn.close(tqa.__setitem__))
            hn = HeadNorm(4)
            for j in range(2):
                linear(256, xk, lambda i, b, t, j=j: hn.add(A_(QB + 512 * (2 * j + i), 512), f"gqb{li}", b, t), 8)
            later.append(hn.close(tqb.__setitem__))
            hn = HeadNorm(4)
            for j in range(2):
                linear(256, xk, lambda i, b, t, j=j: hn.add(A_(KB + 512 * (2 * j + i), 512), f"gkb{li}", b, t), 8)
            later.append(hn.close(tkb.__setitem__))
            vb = A3(VB, 4)
            tvb = []

            def evac_vb(c0):
                def f(ti, b, t):
                    V.w(t)
                    td = V.inc(dve.tensor_copy(vb[:, ti, c0:c0 + 256], b.ap[:, 0:256]))
                    banks.put(b, td)
                    tvb.append(td)
                return f
            natural(256, evac_vb(0))
            natural(256, evac_vb(256))

            obh = arr_r[:, 0:2048].rearrange("p (k n) -> p k n", n=T)
            obl = arr_r[:, OBL:OBL + 2048].rearrange("p (k n) -> p k n", n=T)
            fence = everything()
            S.w(*fence)
            V.w(*fence)
            settle(1000)
            P.w(*tvb)
            last = {}

            def diff_head(ti, h, acc):
                n = 128 * (ti + 1)
                cm = C("causal")[:, 512 - n:512]
                got = [[], []]
                two = []
                for e in range(2):
                    r0 = 64 * e
                    qt = A_(QB + 512 * h, 512)[r0:r0 + 64, 128 * ti:128 * ti + 128]
                    kt = A_(KB + 512 * h, 512)[r0:r0 + 64, 0:n]
                    two.append(probs(qt, kt, cm, n, 0.125, [tqb[h], tkb[h]], got[e]))
                while two:
                    two = [g for g in two if next(g, None) is not None]
                    last["qk"] = P.last()
                    if two:
                        yield True
                (s1, c1, u1), (s2, c2, u2) = got[0][0], got[1][0]
                V.w(t_lam, u2)
                t = V.inc(dve.tensor_scalar(s2.ap[:, 0:n], s2.ap[:, 0:n], tz(c2 + 3), tz(65), ALU.mult, ALU.mult))
                V.w(t, u1)
                t = V.inc(dve.scalar_tensor_tensor(out=s1.ap[:, 0:n], in0=s1.ap[:, 0:n], scalar=tz(c1 + 3),
                                                   in1=s2.ap[:, 0:n], op0=ALU.mult, op1=ALU.add))
                scratch.put(s2, t)
                yield True
                yield from turned(s1, t, ti, got[0])
                pt = got[0].pop()
                if h == 0:
                    acc.append(banks.get())
                    P.w(*acc[0].free)
                for j in range(ti + 1):
                    mm = pe.matmul(acc[0].ap[:, 128 * h:128 * h + 128], vb[:, j, 128 * h:128 * h + 128],
                                   pt.ap[:, 128 * j:128 * j + 128], start=j == 0, stop=j == ti)
                t = P.inc(mm)
                scratch.put(pt, t)
                yield True
                if h < 3:
                    return
                acc = acc[0]
                s, q = scratch.get(), scratch.get()
                S.w(t, *s.free, *q.free)
                ts = S.inc(act.activation(s.ap, acc.ap, ACT.Copy))
                tq = S.inc(act.activation(q.ap, acc.ap, ACT.Square))
                banks.put(acc, tq)
                yield True
                b, t = total(q, tq)
                yield True
                r, t = inverse_root(b, t, 1.0 / 128, EPS)
                V.w(t, ts)
                t = V.inc(dve.scalar_tensor_tensor(out=s.ap, in0=s.ap, scalar=K(f"gsub{li}", 0), in1=r.ap,
                                                   op0=ALU.mult, op1=ALU.mult))
                scratch.put(r, t)
                V.w(t)
                t = V.inc(dve.tensor_scalar(s.ap, s.ap, 1.0 - lam_init, None, ALU.mult))
                yield True
                s3 = s.ap.rearrange("p (h n) -> p h n", h=4)
                tt = slice(128 * ti, 128 * ti + 128)
                last["ob"] = split_x(obh[:, :, tt], obl[:, :, tt], s3, t)
                scratch.put(s, last["ob"])

            jobs = []
            for ti in range(4):
                acc = []
                jobs += [diff_head(ti, h, acc) for h in range(4)]
            units(jobs, every=2, fill=4)
            background(1000)

            oah = arr_r[:, QB:QB + 2048].rearrange("p (k n) -> p k n", n=T)
            oal = arr_r[:, KB:KB + 2048].rearrange("p (k n) -> p k n", n=T)
            S.w(last["qk"])
            V.w(last["qk"])
            P.w(ready["wv", 3])

            def keep_oa(ti):
                def f(acc, t):
                    a3 = acc.ap.rearrange("p (h n) -> p h n", h=4)
                    tt = slice(128 * ti, 128 * ti + 128)
                    last["oa"] = split_x(oah[:, :, tt], oal[:, :, tt], a3, t)
                    banks.put(acc, last["oa"])
                    yield True
                return f

            def out_of(h):
                r0 = 64 * (h % 2)
                return lambda b: b.ap[r0:r0 + 64, 128 * (h // 2):128 * (h // 2) + 128]

            jobs = []
            for ti in range(4):
                n = 128 * (ti + 1)
                mask = C("causal")[:, 512 - n:512] if ti == 0 else mb[:, ti, 0:n]
                acc = []
                for h in range(8):
                    r0 = 64 * (h % 2)
                    jobs.append(attend(A_(QA + 512 * (h // 2), 512)[r0:r0 + 64, 128 * ti:128 * ti + 128],
                                       A_(KA, 512)[r0:r0 + 64, 0:n], lambda j: wv[:, j, 0:64], mask, ti,
                                       [tqa[h // 2], ready["ka"], t_mask[ti]], acc, out_of(h), h == 0,
                                       keep_oa(ti) if h == 7 else None))
            units(jobs)
            t_oa, t_ob = last["oa"], last["ob"]

            gated_branches((oah, oal), (obh, obl), [t_oa, t_ob], 4096)
            for j in range(4):
                linear(256, xk, evac_add(2 * j))

            if stop == f"mix{li}":
                return
            rms(f"gffn{li}")
            fence = everything()
            S.w(*fence)
            V.w(*fence)
            f0 = 0
            for c in FCH:
                uh = arr_r[:, 0:4096].rearrange("p (k n) -> p k n", n=T)
                ul = arr_r[:, 4096:8192].rearrange("p (k n) -> p k n", n=T)
                fence = [P.last()]
                S.w(*fence)
                V.w(*fence)
                for j in range(0, c, 2):
                    conv = {}

                    def evac_conv(which, j=j):
                        def f(i, b, t):
                            fi = f0 + j + i + 22 * which
                            s = scratch.get()
                            S.w(t, *s.free)
                            t0 = S.inc(act.activation(s.ap, b.ap, ACT.Identity, scale=K(f"cw2{li}", fi),
                                                      bias=K(f"cb{li}", fi)))
                            V.w(t0, t)
                            t1 = V.inc(dve.scalar_tensor_tensor(out=s.ap[:, 1:T], in0=b.ap[:, 0:T - 1],
                                                                scalar=K(f"cw1{li}", fi), in1=s.ap[:, 1:T],
                                                                op0=ALU.mult, op1=ALU.add))
                            V.w(t1)
                            t2 = V.inc(dve.scalar_tensor_tensor(out=s.ap[:, 2:T], in0=b.ap[:, 0:T - 2],
                                                                scalar=K(f"cw0{li}", fi), in1=s.ap[:, 2:T],
                                                                op0=ALU.mult, op1=ALU.add))
                            banks.put(b, t0, t2)
                            if which == 0:
                                S.w(t2)
                                t2 = S.inc(act.activation(s.ap, s.ap, ACT.Gelu_apprx_tanh))
                                conv[i] = (s, t2)
                            else:
                                g, tg = conv[i]
                                V.w(t2, tg)
                                t3 = V.inc(dve.tensor_tensor(s.ap, s.ap, g.ap, ALU.mult))
                                scratch.put(g, t3)
                                t4 = split_x(uh[:, j + i, :], ul[:, j + i, :], s.ap, t3)
                                scratch.put(s, t4)
                                P.w()
                                conv["t", i] = t4
                        return f
                    linear(256, xk, evac_conv(0))
                    linear(256, xk, evac_conv(1))
                P.w(conv["t", 0], conv["t", 1])
                ku = [(k, uh[:, k, :], ul[:, k, :]) for k in range(c)]
                for j in range(4):
                    linear(256, ku, evac_add(2 * j))
                f0 += c

            if stop == f"ffn{li}":
                return
            rms(f"gple{li}")
            fence = everything()
            S.w(*fence)
            V.w(*fence)
            Y.w(*fence)
            pt = A3(0, 2)
            ph = arr_r[:, 1024:2048].rearrange("p (k n) -> p k n", n=T)
            pl = arr_r[:, 2048:3072].rearrange("p (k n) -> p k n", n=T)
            pp = A3(4096, 8)
            t = d_p.start(Y, pt, A["pT"][li])
            for k in range(2):
                t1 = split_x(ph[:, k, :], pl[:, k, :], pt[:, k, :], t)
            P.w(t1)
            embed(ph, pl, pp)
            for j in range(4):
                def f(i, b, t, j=j):
                    s = scratch.get()
                    S.w(t, *s.free)
                    ts = S.inc(act.activation(s.ap, b.ap, ACT.Sigmoid))
                    banks.put(b, ts)
                    V.w(ts)
                    t1 = V.inc(dve.tensor_tensor(s.ap, s.ap, pp[:, 2 * j + i, :], ALU.mult))
                    V.w(t1)
                    t1 = V.inc(dve.tensor_tensor(hT[:, 2 * j + i, :], hT[:, 2 * j + i, :], s.ap, ALU.add))
                    scratch.put(s, t1)
                linear(256, xk, f)

        def embed(ph, pl, pp):
            w = stream.next(1024)
            for i in range(8):
                b = banks.get()
                P.w(*b.free)
                t = products(b.ap, w, None, [(k, ph[:, k, :], pl[:, k, :]) for k in range(2)],
                             128 * i, 128 * i + 128, True, True)
                if i == 7:
                    stream.finished(t)
                S.w(t)
                tc = S.inc(act.activation(pp[:, i, :], b.ap, ACT.Copy))
                banks.put(b, tc)
            V.w(tc)
            return tc

        d_p = Dma("d_p")

        for li in range(2):
            first_layer(li)
            if stop in (f"layer{li}", f"mix{li}", f"ffn{li}"):
                dump(hT[:, :, :])
                return
        def bc(ap, shape):
            return ap.to_broadcast(shape)

        layer_norm("lnig", "lnib", 0)
        if stop == "ln2":
            dump(hT[:, :, :])
            return
        fence = everything()
        for q in (V, S, P, Y):
            q.w(*fence)
        YA, YR, QO, KO, VO, BI = 0, 2048, 2048, 4096, 6144, 8192
        bias = A3(BI, 8)
        d_b = Dma("d_b")
        t_b = d_b.start(Y, ar[:, BI:BI + 4096], A["bias"])
        V.w(t_b)
        t_b = V.inc(dve.tensor_scalar(ar[:, BI:BI + 4096], ar[:, BI:BI + 4096], 8.0, None, ALU.mult))
        V.w(t_b)
        for h in range(8):
            t_b = V.inc(dve.tensor_tensor(bias[:, h, 448:512], bias[:, h, 448:512], C("chunk"), ALU.add))
        rdy = {}

        def evac_to(dst, name):
            def f(i, b, t):
                S.w(t)
                rdy[name, i] = S.inc(act.activation(dst(i), b.ap, ACT.Copy))
                banks.put(b, rdy[name, i])
            return f

        for name, off in (("q", QO), ("k", KO)):
            for j in range(2):
                linear(256, xk, evac_to(lambda i, off=off, j=j: A_(off + 512 * (2 * j + i), 512), (name, j)))
        vn = A3(VO, 4)

        def evac_vn(c0):
            def f(ti, b, t):
                S.w(t)
                rdy["v"] = S.inc(act.activation(vn[:, ti, c0:c0 + 256], b.ap[:, 0:256], ACT.Copy))
                banks.put(b, rdy["v"])
            return f
        natural(256, evac_vn(0))
        natural(256, evac_vn(256))
        ya = A3(YA, 4)
        P.w(rdy["v"])
        V.w(t_b)
        last = {}

        def keep_ya(ti):
            def f(acc, t):
                S.w(t)
                last["ya"] = S.inc(act.activation(ya[:, :, 128 * ti:128 * ti + 128],
                                                  acc.ap.rearrange("p (h n) -> p h n", h=4), ACT.Copy))
                banks.put(acc, last["ya"])
                yield True
            return f

        def out_of(h):
            r0 = 64 * (h % 2)
            return lambda b: b.ap[r0:r0 + 64, 128 * (h // 2):128 * (h // 2) + 128]

        jobs = []
        for ti in range(4):
            n = 128 * (ti + 1)
            acc = []
            for h in range(8):
                r0 = 64 * (h % 2)
                j, i = divmod(h // 2, 2)
                jobs.append(attend(A_(QO + 512 * (h // 2), 512)[r0:r0 + 64, 128 * ti:128 * ti + 128],
                                   A_(KO + 512 * (h // 2), 512)[r0:r0 + 64, 0:n],
                                   lambda j, h=h: vn[:, j, 64 * h:64 * h + 64], bias[:, h, 512 - n:512], ti,
                                   [rdy[("q", j), i], rdy[("k", j), i]], acc, out_of(h), h == 0,
                                   keep_ya(ti) if h == 7 else None))
        units(jobs)
        t_ya = last["ya"]

        fence = everything()
        for q in (V, S, P):
            q.w(*fence)
        yr = A3(YR, 4)
        WD, GD = A_(4096, 512), A3(4608, 2)
        omu = tz(128, 143)
        V.w()
        t_omu = V.inc(dve.tensor_scalar(omu, K("mu"), -1.0, 1.0, ALU.mult, ALU.add))
        S.w(t_omu)

        def mixed(dst, b, t, col, rows=128):
            S.w(t)
            t0 = S.inc(act.activation(dst, b.ap[0:rows, :], ACT.Identity, scale=tz(128 + col)[0:rows, :]))
            V.w(t0)
            t1 = V.inc(dve.scalar_tensor_tensor(out=dst[:, 1:T], in0=b.ap[0:rows, 0:T - 1], scalar=K("mu", col)[0:rows, :],
                                                in1=dst[:, 1:T], op0=ALU.mult, op1=ALU.add))
            banks.put(b, t1)
            return t1

        def evac_lo(i, b, t):
            if i == 0:
                t = mixed(WD, b, t, 12)
                S.w(t)
                rdy["wd"] = S.inc(act.activation(WD[0:64, :], WD[0:64, :], ACT.Tanh))
            else:
                t = mixed(GD[:, 0, :], b, t, 13)
                S.w(t)
                rdy["gd"] = S.inc(act.activation(GD[:, 0, :], GD[:, 0, :], ACT.Sigmoid))

        def evac_g1(i, b, t):
            t = mixed(GD[0:32, 1, :], b, t, 14, 32)
            S.w(t)
            rdy["gd"] = S.inc(act.activation(GD[0:32, 1, :], GD[0:32, 1, :], ACT.Sigmoid))
        linear(256, xk, evac_lo)
        linear(32, xk, evac_g1)
        P.w(rdy["wd"], rdy["gd"])

        AR = ar[:, 5632:6656]
        AR4 = AR.rearrange("p (c w t) -> p c w t", c=8, w=2)
        Bt, Kt, Bn, Kn, Vn, BV, YT = (A_(6656 + 512 * i, 512) for i in range(7))
        LR, MK = ar[:, 10752:11776], ar[:, 11776:12800]
        X, XT, T1, Lm = (A_(12800 + 512 * i, 512) for i in range(4))
        rT, kT, vT, lw, cc, aT, kkT, tm = (A_(10752 + 512 * i, 512) for i in range(8))
        STs = [A_(14848 + 128 * i, 128) for i in range(2)]
        Bz, Kz = (Bt, T1), (Kt, Lm)
        hm = (C("blk")[:, 0:1], C("blk")[:, 64:65])

        def c8(ap):
            return ap.rearrange("p (c t) -> p c t", c=8)

        d_l = Dma("d_l")
        for i in range(2):
            t = V.inc(dve.memset(STs[i], 0.0))
        V.w(t)
        for j in range(4):
            fence = everything()
            for q in (V, S, P):
                q.w(*fence)
            lora = scratch.get()
            Y.w(*lora.free)
            t_l = d_l.start(Y, lora.ap[:, 0:384], A["lora"][j])
            P.w(t_l)
            rk = {}

            def evac_rk(i, b, t):
                rk[i] = mixed((rT, kT)[i], b, t, 4 * i + j)
            linear(256, xk, evac_rk)
            linear(128, xk, lambda i, b, t: rk.__setitem__(2, mixed(vT, b, t, 8 + j)))

            def low_rank(r0, r1, dst, base):
                b = banks.get()
                P.w(*b.free)
                t = P.inc(pe.matmul(b.ap, lora.ap[r0:r1, 0:128], WD[r0:r1, :], start=True, stop=True))
                S.w(t)
                t = S.inc(act.activation(dst, b.ap, ACT.Sigmoid, bias=K(base, j)))
                banks.put(b, t)
                return t
            t = low_rank(0, 64, lw, "dbase")
            V.w(t)
            t_lw = V.inc(dve.tensor_scalar(lw, lw, -math.exp(-0.5), None, ALU.mult))
            t_a = low_rank(64, 128, aT, "abase")

            t, src = t_lw, lw
            w2 = scratch.get()
            V.w(*w2.free)
            S.w(*w2.free)
            for n_, sh in enumerate((1, 2, 4, 8, 16, 32)):
                dst = cc if n_ % 2 else w2.ap
                V.w(t)
                S.w(t)
                t1 = V.inc(dve.tensor_tensor(c8(dst)[:, :, sh:64], c8(src)[:, :, sh:64], c8(src)[:, :, 0:64 - sh], ALU.add))
                t2 = S.inc(act.activation(c8(dst)[:, :, 0:sh], c8(src)[:, :, 0:sh], ACT.Copy))
                V.w(t2)
                S.w(t1)
                t, src = [t1, t2], dst
            t_c = t
            scratch.put(w2, *t_c)

            V.w(rk[1], rk[0], rk[2])
            tk = V.inc(dve.tensor_scalar(kkT, kT, K("kk", j), None, ALU.mult))
            s = scratch.get()
            S.w(tk, *s.free)
            ts = S.inc(act.activation(s.ap, kkT, ACT.Square))
            b, t = total(s, ts, "blk")
            r = scratch.get()
            V.w(t, *r.free)
            t = V.inc(dve.tensor_scalar(r.ap, b.ap, 1e-24, None, ALU.max))
            banks.put(b, t)
            S.w(t)
            t = S.inc(act.activation(r.ap, r.ap, ACT.Sqrt))
            V.w(t)
            t = V.inc(dve.reciprocal(r.ap, r.ap))
            V.w(t)
            tk = V.inc(dve.tensor_tensor(kkT, kkT, r.ap, ALU.mult))
            scratch.put(r, tk)
            V.w(t_a)
            t = V.inc(dve.tensor_scalar(tm, aT, -1.0, K("ka", j), ALU.add, ALU.mult))
            V.w(t)
            t_k = V.inc(dve.scalar_tensor_tensor(out=kT, in0=tm, scalar=1.0, in1=kT, op0=ALU.add, op1=ALU.mult))
            V.w(tk)
            t_a = V.inc(dve.tensor_tensor(aT, aT, kkT, ALU.mult))

            s = scratch.get()
            V.w(t_k, *s.free)
            t = V.inc(dve.scalar_tensor_tensor(out=s.ap, in0=rT, scalar=K("rk", j), in1=kT, op0=ALU.mult, op1=ALU.mult))
            b, t = total(s, t, "blk")
            V.w(t)
            t = V.inc(dve.tensor_tensor(BV, b.ap, vT, ALU.mult))
            banks.put(b, t)

            e = scratch.get()
            S.w(t_c, *e.free)
            t = S.inc(act.activation(e.ap, cc, ACT.Exp))
            V.w(t)
            PC = tz(144, 152)
            t_pc = V.inc(dve.tensor_copy(PC, c8(e.ap)[:, :, 63]))
            t_R = V.inc(dve.tensor_tensor(AR4[:, :, 1, :], c8(rT), c8(e.ap), ALU.mult))
            scratch.put(e, t_R)
            V.w(t_c)
            t = V.inc(dve.tensor_tensor(tm, cc, lw, ALU.subtract))
            S.w(t)
            t = S.inc(act.activation(tm, tm, ACT.Exp))
            V.w(t)
            t_A = V.inc(dve.scalar_tensor_tensor(out=AR4[:, :, 0, :], in0=c8(kkT), scalar=-1.0, in1=c8(tm),
                                                 op0=ALU.mult, op1=ALU.mult))
            e = scratch.get()
            S.w(*e.free)
            t = S.inc(act.activation(e.ap, cc, ACT.Exp, scale=-1.0))
            V.w(t, t_a, t_pc)
            V.w(t_A)
            for src, dst in ((aT, Bz), (kT, Kz)):
                for h in range(2):
                    t_BK = V.inc(dve.scalar_tensor_tensor(out=dst[h], in0=src, scalar=hm[h], in1=e.ap,
                                                          op0=ALU.mult, op1=ALU.mult))
            V.w(t_BK)
            t = V.inc(dve.tensor_tensor(c8(e.ap), c8(e.ap), bc(PC.unsqueeze(2), [128, 8, 64]), ALU.mult))
            V.w(t)
            V.inc(dve.tensor_tensor(aT, aT, e.ap, ALU.mult))
            t = V.inc(dve.tensor_tensor(kT, kT, e.ap, ALU.mult))
            scratch.put(e, t)
            P.w(t, rk[2])
            for src, dst in ((aT, Bn), (kT, Kn), (vT, Vn)):
                b = banks.get()
                P.w(*b.free)
                for i in range(4):
                    mm = pe.transpose(b.ap[:, 128 * i:128 * i + 128], src[:, 128 * i:128 * i + 128], C("ident"))
                t = P.inc(mm)
                S.w(t)
                t_n = S.inc(act.activation(dst, b.ap, ACT.Copy))
                banks.put(b, t_n)

            P.w(t_R, t_A, t_BK)
            tri = C("tri").unsqueeze(1)
            V.w(t_n)
            for lhs, dst in ((Bz, LR), (Kz, MK)):
                for half in range(2):
                    b = banks.get()
                    P.w(*b.free)
                    for c in range(4 * half, 4 * half + 4):
                        for h in range(2):
                            pr = 64 * (c % 2)
                            col = 128 * (2 * (c // 2 - 2 * half) + h)
                            mm = pe.matmul(b.ap[pr:pr + 64, col:col + 128], lhs[h][:, 64 * c:64 * c + 64],
                                           AR[:, 128 * c:128 * c + 128], start=True, stop=True)
                    t = P.inc(mm)
                    V.w(t)
                    t_m = V.inc(dve.tensor_tensor(dst[:, 512 * half:512 * half + 512].rearrange("p (g n) -> p g n", g=4),
                                                  b.ap.rearrange("p (g n) -> p g n", g=4), bc(tri, [128, 4, 128]), ALU.mult))
                    banks.put(b, t_m)
            b = banks.get()
            P.w(*b.free)
            for c in range(8):
                for h in range(2):
                    pr = 64 * (c % 2)
                    col = 64 * (2 * (c // 2) + h)
                    mm = pe.matmul(b.ap[pr:pr + 64, col:col + 64], AR4[:, c, 0, :],
                                   Bz[h][:, 64 * c:64 * c + 64], start=True, stop=True)
            t = P.inc(mm)
            LT = LR.rearrange("p (g w n) -> p g w n", g=8, w=2)[:, :, 0, :]

            def m8(name):
                return bc(C(name).unsqueeze(1), [128, 8, 64])
            V.w(t)
            t = V.inc(dve.tensor_tensor(c8(X), c8(b.ap), m8("lv1"), ALU.mult))
            banks.put(b, t)
            V.w(t)
            t_X = V.inc(dve.tensor_tensor(c8(X), c8(X), m8("eye"), ALU.add))
            V.w(t_m)
            t = V.inc(dve.tensor_tensor(c8(XT), LT, m8("lt1"), ALU.mult))
            V.w(t)
            t_X = V.inc(dve.tensor_tensor(c8(XT), c8(XT), m8("eye"), ALU.add))

            def small(lhs, rhs):
                b = banks.get()
                P.w(*b.free)
                for c in range(8):
                    for h in range(2):
                        pr = 64 * (c % 2)
                        col = 64 * (2 * (c // 2) + h)
                        mm = pe.matmul(b.ap[pr:pr + 64, col:col + 64], lhs[pr:pr + 64, col:col + 64],
                                       rhs[pr:pr + 64, col:col + 64], start=True, stop=True)
                return b, P.inc(mm)

            t = None
            for m in (2, 4, 8, 16, 32):
                V.w(t)
                t = V.inc(dve.tensor_tensor(c8(Lm), LT, m8(f"lt{m}"), ALU.mult))
                P.w(t, t_X)
                b, t = small(Lm, X)
                S.w(t)
                t = S.inc(act.activation(T1, b.ap, ACT.Copy))
                banks.put(b, t)
                P.w(t)
                if m < 32:
                    b1, u1 = small(XT, T1)
                b2, t = small(T1, XT)
                V.w(t)
                if m < 32:
                    t_x1 = V.inc(dve.tensor_tensor(X, X, b1.ap, ALU.add))
                    banks.put(b1, t_x1)
                t_X = V.inc(dve.tensor_tensor(XT, XT, b2.ap, ALU.add))
                banks.put(b2, t_X)

            P.w(t_X)
            yb = banks.get()
            P.w(*yb.free)
            gu = scratch.get()
            V.w(*gu.free)
            t_S = None
            for c in range(8):
                pr = 64 * (c % 2)
                cp = c // 2
                S0, S1 = STs[c % 2], STs[(c + 1) % 2]
                b = banks.get()
                P.w(*b.free, t_S)
                o = b.ap[pr:pr + 64, 0:128]
                if c:
                    pe.matmul(o, AR4[:, c, 0, :], S0, start=True, stop=False, skip_group_check=True)
                for h in range(2):
                    hr = 64 * h
                    col = 128 * (2 * cp + h)
                    mm = pe.matmul(o[:, hr:hr + 64], MK[pr:pr + 64, col:col + 64],
                                   Vn[pr:pr + 64, 128 * cp + hr:128 * cp + hr + 64], start=c == 0, stop=True,
                                   skip_group_check=True)
                t = P.inc(mm)
                V.w(t)
                t = V.inc(dve.tensor_copy(gu.ap[pr:pr + 64, 0:128], o))
                P.w(t)
                for h in range(2):
                    col = 64 * (2 * cp + h)
                    mm = pe.matmul(b.ap[pr:pr + 64, 128 + 64 * h:192 + 64 * h], XT[pr:pr + 64, col:col + 64],
                                   gu.ap[pr:pr + 64, 64 * h:64 * h + 64], start=True, stop=True)
                t = P.inc(mm)
                V.w(t)
                t = V.inc(dve.tensor_copy(gu.ap[pr:pr + 64, 128:256], b.ap[pr:pr + 64, 128:256]))
                P.w(t)
                u = gu.ap[pr:pr + 64, 128:256]
                v_ = Vn[pr:pr + 64, 128 * cp:128 * cp + 128]
                o = b.ap[:, 256:384]
                pe.matmul(o, Bn[pr:pr + 64, 128 * cp:128 * cp + 128], u, start=True, stop=False)
                t = P.inc(pe.matmul(o, Kn[pr:pr + 64, 128 * cp:128 * cp + 128], v_, start=False, stop=True))
                if c:
                    pe.matmul(yb.ap[:, 64 * c:64 * c + 64], S0, AR4[:, c, 1, :], start=True, stop=False,
                              skip_group_check=True)
                for h in range(2):
                    hr = 64 * h
                    o = yb.ap[hr:hr + 64, 64 * c:64 * c + 64]
                    col = 128 * (2 * cp + h)
                    pe.matmul(o, u[:, hr:hr + 64], LR[pr:pr + 64, col + 64:col + 128], start=c == 0, stop=False,
                              skip_group_check=True)
                    mm = pe.matmul(o, v_[:, hr:hr + 64], MK[pr:pr + 64, col + 64:col + 128], start=False, stop=True,
                                   skip_group_check=True)
                t_Y = P.inc(mm)
                V.w(t)
                for h in range(2):
                    hr = 64 * h
                    d = (slice(hr, hr + 64), slice(hr, hr + 64))
                    ps = b.ap[hr:hr + 64, 256 + hr:320 + hr]
                    if c:
                        t_S = V.inc(dve.scalar_tensor_tensor(out=S1[d], in0=S0[d], scalar=PC[hr:hr + 64, c:c + 1],
                                                             in1=ps, op0=ALU.mult, op1=ALU.add))
                    else:
                        t_S = V.inc(dve.tensor_copy(S1[d], ps))
                V.w(t_S, t_Y)
                banks.put(b, t_S)
            scratch.put(gu, t_Y)
            S.w(t_Y)
            t = S.inc(act.activation(YT, yb.ap, ACT.Copy))
            banks.put(yb, t)

            b = banks.get()
            P.w(*b.free, t)
            t = P.inc(pe.matmul(b.ap, C("blk"), YT, start=True, stop=True))
            V.w(t)
            t = V.inc(dve.scalar_tensor_tensor(out=YT, in0=b.ap, scalar=-1.0 / 64, in1=YT, op0=ALU.mult, op1=ALU.add))
            banks.put(b, t)
            s = scratch.get()
            S.w(t, *s.free)
            ts = S.inc(act.activation(s.ap, YT, ACT.Square))
            b, t = total(s, ts, "blk")
            r, t = inverse_root(b, t, 1.0 / 64, GN_EPS)
            V.w(t)
            t = V.inc(dve.scalar_tensor_tensor(out=YT, in0=YT, scalar=K("gng", j), in1=r.ap, op0=ALU.mult, op1=ALU.mult))
            scratch.put(r, t)
            V.w(t)
            t = V.inc(dve.scalar_tensor_tensor(out=YT, in0=YT, scalar=K("gnb", j), in1=BV, op0=ALU.add, op1=ALU.add))
            b = banks.get()
            P.w(*b.free)
            pe.matmul(b.ap, lora.ap[:, 128:256], GD[:, 0, :], start=True, stop=False)
            tg = P.inc(pe.matmul(b.ap, lora.ap[0:32, 256:384], GD[0:32, 1, :], start=False, stop=True))
            scratch.put(lora, tg)
            V.w(tg, t)
            t_yr = V.inc(dve.tensor_tensor(yr[:, j, :], b.ap, YT, ALU.mult))
            banks.put(b, t_yr)

        if stop in ("rwkv", "attn2"):
            V.w(t_yr)
            t = V.inc(dve.memset(hT[:, 0:4, :], 0.0))
            V.w(t)
            V.w(t_ya)
            V.inc(dve.tensor_copy(hT[:, 0:4, :], ya))
            V.inc(dve.tensor_copy(hT[:, 4:8, :], yr))
            dump(hT[:, :, :])
            return

        fence = everything()
        for q in (V, S):
            q.w(*fence)
        XA = [arr_r[:, o:o + 2048].rearrange("p (k n) -> p k n", n=T) for o in (4096, 6144)]
        XB = [arr_r[:, o:o + 2048].rearrange("p (k n) -> p k n", n=T) for o in (8192, 10240)]
        t1 = split_x(XA[0], XA[1], ya)
        t2 = split_x(XB[0], XB[1], yr)
        gated_branches(XA, XB, [t1, t2], 0)

        def evac_alpha(n0):
            def f(i, b, t):
                V.w(t)
                banks.put(b, V.inc(dve.scalar_tensor_tensor(out=hT[:, n0 + i, :], in0=hT[:, n0 + i, :], scalar=ALPHA,
                                                            in1=b.ap, op0=ALU.mult, op1=ALU.add)))
            return f
        for j in range(4):
            linear(256, xk, evac_alpha(2 * j))
        t = layer_norm("lng", "lnb", 0)
        if stop == "ln3":
            dump(hT[:, :, :])
            return

        fence = everything()
        for q in (V, S, P):
            q.w(*fence)
        RO = ar[:, 14000:15100]

        def R(a, n, *dims):
            v = RO[:, a:a + n]
            if len(dims) == 2:
                return v.rearrange("p (x y) -> p x y", x=dims[0])
            return v
        d_m = Dma("d_m")
        Y.w(*fence)
        t_cm = d_m.start(Y, A_(MOEC, A["moec"].shape[1]), A["moec"])
        lg = R(0, 144, 4, 36)
        wrt = K("wrt").rearrange("p (k n) -> p k n", n=36)
        b = banks.get()
        P.w(*b.free)
        for ti in range(4):
            for k in range(KT):
                mm = pe.matmul(b.ap[:, 36 * ti:36 * ti + 36], hT[:, k, 128 * ti:128 * ti + 128], wrt[:, k, :],
                               start=k == 0, stop=k == KT - 1)
        t = P.inc(mm)

        xn = A3(8192, 4, 1024)
        d_t = Dma("d_t")
        for ti in range(4):
            for half in range(2):
                b1 = banks.get()
                P.w(*b1.free)
                for k in range(4):
                    mm = pe.transpose(b1.ap[:, 128 * k:128 * k + 128],
                                      hT[:, 4 * half + k, 128 * ti:128 * ti + 128], C("ident"))
                t1 = P.inc(mm)
                S.w(t1)
                t1 = S.inc(act.activation(xn[:, ti, 512 * half:512 * half + 512], b1.ap, ACT.Copy))
                banks.put(b1, t1)
            Y.w(t1)
            t_tok = d_t.start(Y, xtok[128 * ti:128 * ti + 128, :], xn[:, ti, :])

        def vv(ins):
            V.w(V.inc(ins))
        V.w(t)
        vv(dve.tensor_tensor(lg, b.ap[:, 0:144].rearrange("p (x y) -> p x y", x=4),
                             bc(K("rbias").unsqueeze(1), [128, 4, 36]), ALU.add))
        banks.put(b, V.last())
        gl, el = lg[:, :, 0:4], lg[:, :, 4:36]
        gm, gs = R(144, 4), R(148, 4)
        gd, oh, eq = R(152, 16, 4, 4), R(168, 16, 4, 4), R(184, 16, 4, 4)
        mx = R(200, 4)
        m1, m2, w1, w2_, dd = R(204, 4), R(208, 4), R(212, 4), R(216, 4), R(220, 4)
        me, oa, ob, qq = R(224, 128, 4, 32), R(352, 128, 4, 32), R(480, 128, 4, 32), R(608, 128, 4, 32)
        comb = R(736, 128, 4, 32)

        def w4(v, n):
            return bc(v.unsqueeze(2), [128, 4, n])
        vv(dve.tensor_reduce(gm, gl, AX.X, ALU.max))
        vv(dve.tensor_tensor(gd, gl, w4(gm, 4), ALU.subtract))
        vv(dve.tensor_scalar(oh, gd, 0.0, None, ALU.is_equal))
        S.w(V.last())
        V.w(S.inc(act.activation(gd, gd, ACT.Exp)))
        vv(dve.tensor_reduce(gs, gd, AX.X, ALU.add))
        vv(dve.reciprocal(gs, gs))
        vv(dve.tensor_tensor(eq, oh, bc(C("gidx").unsqueeze(1), [128, 4, 4]), ALU.mult))
        vv(dve.tensor_reduce(mx, eq, AX.X, ALU.max))
        vv(dve.tensor_tensor(oh, eq, w4(mx, 4), ALU.is_equal))
        vv(dve.tensor_scalar(oh, oh, -1.0, 1.0e30, ALU.add, ALU.mult))
        for g in range(4):
            vv(dve.tensor_tensor(me[:, :, 8 * g:8 * g + 8], el[:, :, 8 * g:8 * g + 8],
                                 w4(oh[:, :, g], 8), ALU.add))

        def first_of(dst, v, m):
            vv(dve.tensor_reduce(m, v, AX.X, ALU.max))
            vv(dve.tensor_tensor(qq, v, w4(m, 32), ALU.is_equal))
            vv(dve.tensor_tensor(qq, qq, bc(C("eidx").unsqueeze(1), [128, 4, 32]), ALU.mult))
            vv(dve.tensor_reduce(mx, qq, AX.X, ALU.max))
            vv(dve.tensor_tensor(dst, qq, w4(mx, 32), ALU.is_equal))
        first_of(oa, me, m1)
        vv(dve.scalar_tensor_tensor(out=me, in0=oa, scalar=-2.0e30, in1=me, op0=ALU.mult, op1=ALU.add))
        first_of(ob, me, m2)
        vv(dve.tensor_tensor(dd, m2, m1, ALU.subtract))
        S.w(V.last())
        V.w(S.inc(act.activation(dd, dd, ACT.Exp)))
        vv(dve.tensor_scalar(w1, dd, 1.0, None, ALU.add))
        vv(dve.reciprocal(w1, w1))
        vv(dve.tensor_tensor(w1, w1, gs, ALU.mult))
        vv(dve.tensor_tensor(w2_, w1, dd, ALU.mult))
        cm = A_(MOEC, A["moec"].shape[1])
        V.w(t_cm)
        P.w(t_cm)
        before, count_to = cm[:, 0:128], cm[:, 128:256]
        tile_to, pair, upto, part = cm[:, 256:256 + NT], cm[:, 256 + NT:264 + NT], cm[0:32, 264 + NT:328 + NT], \
            cm[:, 328 + NT:329 + NT]
        onehot_p, onehot_t = A3(12288, 8, 128), A3(12288 + 1024, 8, NT)
        oab, rank, owned, basis = qq, R(224, 128, 4, 32), R(736, 8), R(744, 64)
        prod = R(808, 128, 4, 32)
        place, tile_, over = R(936, 8), R(944, 8), R(952, 8)
        fidx, gidx_ = R(960, NT), R(1000, NT)
        vv(dve.tensor_copy(weight[:, 0:4], w1))
        vv(dve.tensor_copy(weight[:, 4:8], w2_))
        vv(dve.tensor_tensor(oab, oa, ob, ALU.add))
        b, b2 = banks.get(), banks.get()
        P.w(*b.free, *b2.free, V.last())
        for ti in range(4):
            for tj in range(ti):
                pe.matmul(b.ap[:, 32 * ti:32 * ti + 32], C("ones"), oab[:, tj, :], start=tj == 0, stop=False)
            mm = pe.matmul(b.ap[:, 32 * ti:32 * ti + 32], before, oab[:, ti, :], start=ti == 0, stop=True)
        t = P.inc(mm)
        for ti in range(4):
            mm = pe.matmul(b2.ap[0:32, 0:1], oab[:, ti, :], C("ones")[:, 0:1], start=ti == 0, stop=ti == 3)
        t2 = P.inc(mm)
        V.w(t2)
        vv(dve.tensor_scalar(owned[0:32, 0:1], b2.ap[0:32, 0:1], 0.0, None, ALU.is_gt))
        for j in (1, 2, 3):
            vv(dve.scalar_tensor_tensor(out=owned[0:32, 0:1], in0=b2.ap[0:32, 0:1], scalar=128.0 * j,
                                        in1=owned[0:32, 0:1], op0=ALU.is_gt, op1=ALU.add))
        banks.put(b2, V.last())
        b2 = banks.get()
        P.w(*b2.free, V.last())
        t2 = P.inc(pe.matmul(b2.ap[:, 0:64], owned[0:32, 0:1].to_broadcast([32, 128]), upto, start=True, stop=True))
        V.w(t)
        vv(dve.tensor_copy(rank, b.ap[:, 0:128].rearrange("p (x y) -> p x y", x=4)))
        banks.put(b, V.last())
        V.w(t2)
        vv(dve.tensor_copy(basis, b2.ap[:, 0:64]))
        banks.put(b2, V.last())
        vv(dve.tensor_scalar(prod[:, 0, :], basis[:, 32:64], part, None, ALU.is_le))
        vv(dve.tensor_reduce(owned[:, 1:2], prod[:, 0, :], AX.X, ALU.add))
        vv(dve.tensor_scalar(owned[:, 1:2], owned[:, 1:2], 31.0, None, ALU.min))
        b = banks.get()
        P.w(*b.free, V.last())
        t_own = P.inc(pe.matmul(b.ap[0:1, 0:128], owned[:, 1:2], C("ident"), start=True, stop=True))
        V.w(t_own)
        vv(dve.tensor_copy(owner[0:1, :], b.ap[0:1, 0:128]))
        banks.put(b, V.last())
        Y.w(V.last())
        for c_, one in ((0, oa), (1, ob)):
            vv(dve.tensor_tensor(prod, one, rank, ALU.mult))
            vv(dve.tensor_reduce(place[:, 4 * c_:4 * c_ + 4], prod, AX.X, ALU.add))
            vv(dve.tensor_tensor(prod, one, bc(basis[:, 0:32].unsqueeze(1), [128, 4, 32]), ALU.mult))
            vv(dve.tensor_reduce(tile_[:, 4 * c_:4 * c_ + 4], prod, AX.X, ALU.add))
        vv(dve.tensor_scalar(over, place, 128.0, None, ALU.is_ge))
        for j in (2, 3):
            vv(dve.scalar_tensor_tensor(out=over, in0=place, scalar=128.0 * j, in1=over, op0=ALU.is_ge, op1=ALU.add))
        vv(dve.tensor_tensor(tile_, tile_, over, ALU.add))
        vv(dve.scalar_tensor_tensor(out=place, in0=over, scalar=-128.0, in1=place, op0=ALU.mult, op1=ALU.add))
        for x in range(8):
            V.inc(dve.tensor_scalar(onehot_p[:, x, :], count_to, place[:, x:x + 1], None, ALU.is_equal))
            t = V.inc(dve.tensor_scalar(onehot_t[:, x, :], tile_to, tile_[:, x:x + 1], pair[:, x:x + 1],
                                        ALU.is_equal, ALU.mult))
        b = banks.get()
        P.w(*b.free, t)
        for x in range(8):
            mm = pe.matmul(b.ap[:, 0:NT], onehot_p[:, x, :], onehot_t[:, x, :], start=x == 0, stop=x == 7)
        V.w(P.inc(mm))
        vv(dve.tensor_scalar(fidx, b.ap[:, 0:NT], 4096.0, None, ALU.add))
        banks.put(b, V.last())
        vv(dve.tensor_copy(slots[:, 1, :], fidx))
        vv(dve.tensor_scalar(gidx_, fidx, 512.0, -512.0, ALU.is_ge, ALU.mult))
        vv(dve.tensor_tensor(gidx_, gidx_, fidx, ALU.add))
        vv(dve.tensor_copy(slots[:, 0, :], gidx_))

        assert len(scratch.slots) == 9
        fence = everything() + [t_tok]
        for q in (V, S, P, G, Y):
            q.w(*fence)
        flat = "p a b -> p (a b)"
        xe = [scr[:, 2 * i:2 * i + 2, :].rearrange(flat) for i in range(3)]
        act_ = [scr[:, 6 + i, 0:256] for i in range(2)]
        ye = [A_(8192 + 1024 * i, 1024) for i in range(2)]
        xs = [[arr_r[:, 10240 + 2048 * w_ + 1024 * i:11264 + 2048 * w_ + 1024 * i].rearrange("p (k n) -> p k n", n=128)
               for w_ in range(2)] for i in range(2)]
        hs = [arr_r[:, 14336 + 256 * w_:14592 + 256 * w_].rearrange("p (k n) -> p k n", n=128) for w_ in range(2)]
        for i in range(3):
            t = V.inc(dve.memset(xe[i], 0.0))
        G.w(t)

        order = []
        for i in range(NT):
            order += [(i, 0), (i, 1)] + ([(i - 1, 2)] if i else [])
        order.append((NT - 1, 2))
        d_e = [Dma(f"d_e{i}") for i in range(4)]

        class Experts:

            def __init__(self):
                self.loaded = self.split = self.used = 0
                self.raw_t, self.split_t, self.done = [], [], []
                for _ in range(4):
                    self.load()

            def load(self):
                n = self.loaded
                if n >= len(order):
                    return
                if n >= 4:
                    Y.w(*self.split_t[2 * (n - 4)], *self.split_t[2 * (n - 4) + 1])
                i, part_ = order[n]
                e = nc.values_load(owner[0:1, i:i + 1], engines=[mybir.EngineType.SP], min_val=0, max_val=31)
                src = A["WE"][bass.ds(e, 1), part_, :, :].rearrange("o p n -> p (o n)")
                self.raw_t.append(d_e[n % 4].start(Y, A_(2048 * (n % 4), 2048), src))
                self.loaded += 1

            def cut(self):
                n = self.split
                if n >= 2 * len(order):
                    return
                r = A_(2048 * (n // 2 % 4) + 1024 * (n % 2), 1024)
                s_ = n % 4
                h, l = (x[:, 2 * s_:2 * s_ + 2, :].rearrange(flat) for x in (XH, XL))
                free = self.done[n - 4] if n >= 4 else None
                Q, eng = (G, pool) if n % 6 in POOL_CUTS else (V, dve)
                S.w(free, self.raw_t[n // 2])
                th = S.inc(act.activation(h, r, ACT.Copy))
                Q.w(free, th, self.raw_t[n // 2])
                tl = Q.inc(eng.tensor_tensor(l, r, h.bitcast(F32), ALU.subtract))
                self.split_t.append((th, tl))
                self.split += 1
                if n % 2:
                    self.load()

            def next(self, n_cols):
                n = self.used
                self.used += 1
                while self.split <= n:
                    self.cut()
                P.w(*self.split_t[n])
                s_ = n % 4
                return [x[:, 2 * s_:2 * s_ + 2, :].rearrange(flat).rearrange("p (k n) -> p k n", n=n_cols)
                        for x in (XH, XL)]

            def finished(self, ticket):
                self.done.append(ticket)
                while self.split < min(self.used + 3, 2 * len(order)):
                    self.cut()

        experts = Experts()
        d_g = [Dma(f"d_g{i}") for i in range(3)]
        d_y = [Dma(f"d_y{i}") for i in range(2)]
        t_gather, t_scatter, turned_t, xs_t, xs_read = {}, {}, {}, {}, {}

        def gather(i):
            if i >= NT:
                return
            G.w(turned_t.get(i - 3))
            d = d_g[i % 3]
            d.n += 16
            pool.indirect_dma_start(xe[i % 3], None, xtok, bass.IndirectOffsetOnAxis(ap=slots[:, 0, i:i + 1], axis=0),
                                    bounds_check=T - 1, oob_is_err=False).then_inc(d.sem, 16)
            t_gather[i] = (d.sem, d.name, d.n)

        def tokens(i):
            if i >= NT:
                return
            P.w(t_gather[i])
            two = []
            for half in range(2):
                b = banks.get()
                P.w(*b.free)
                for k in range(4):
                    kk = 4 * half + k
                    mm = pe.transpose(b.ap[:, 128 * k:128 * k + 128], xe[i % 3][:, 128 * kk:128 * kk + 128], C("ident"))
                two.append((b, P.inc(mm)))
            turned_t[i] = two[1][1]
            for half, (b, t) in enumerate(two):
                src = b.ap.rearrange("p (k n) -> p k n", n=128)
                kk = slice(4 * half, 4 * half + 4)
                xs_t[i] = split_x(xs[i % 2][0][:, kk, :], xs[i % 2][1][:, kk, :], src, t, xs_read.get(i - 2))
                banks.put(b, xs_t[i])
            gather(i + 3)

        def hidden(i):
            b = banks.get()
            P.w(*b.free, xs_t[i])
            xh, xl = xs[i % 2]
            for q in range(4):
                h, l = experts.next(512)
                for kk in range(2):
                    k = 2 * q + kk
                    pe.matmul(b.ap, xh[:, k, :], h[:, kk, :], start=k == 0, stop=False)
                    pe.matmul(b.ap, xl[:, k, :], h[:, kk, :], start=False, stop=False)
                    mm = pe.matmul(b.ap, xh[:, k, :], l[:, kk, :], start=False, stop=k == 7)
                t = P.inc(mm)
                experts.finished(t)
            xs_read[i] = t
            s = act_[i % 2]
            S.w(t, hid_t.get(i - 2))
            ts = S.inc(act.activation(s, b.ap[:, 0:256], ACT.Silu))
            V.w(ts)
            t1 = V.inc(dve.tensor_tensor(s, s, b.ap[:, 256:512], ALU.mult))
            banks.put(b, t1)
            return s, t1

        hid_t = {}

        def turn_hidden(i, s, t1):
            b = banks.get()
            P.w(*b.free, t1)
            for k in range(2):
                mm = pe.transpose(b.ap[:, 128 * k:128 * k + 128], s[:, 128 * k:128 * k + 128], C("ident"))
            hid_t[i] = P.inc(mm)
            hid_t["x"] = split_x(hs[0], hs[1], b.ap[:, 0:256].rearrange("p (k n) -> p k n", n=128), hid_t[i])
            banks.put(b, hid_t["x"])

        def down(i):
            two = [banks.get(), banks.get()]
            P.w(*two[0].free, *two[1].free, hid_t["x"])
            for kt in range(2):
                h, l = experts.next(512)
                for half in range(2):
                    o = two[half].ap
                    pe.matmul(o, hs[0][:, kt, :], h[:, half, :], start=kt == 0, stop=False)
                    pe.matmul(o, hs[1][:, kt, :], h[:, half, :], start=False, stop=False)
                    mm = pe.matmul(o, hs[0][:, kt, :], l[:, half, :], start=False, stop=kt == 1)
                t = P.inc(mm)
                experts.finished(t)
            y_ = ye[i % 2]
            S.w(t, t_scatter.get(i - 2))
            ta = S.inc(act.activation(y_[:, 0:512], two[0].ap, ACT.Copy))
            banks.put(two[0], ta)
            V.w(t, t_scatter.get(i - 2))
            tb = V.inc(dve.tensor_copy(y_[:, 512:1024], two[1].ap))
            banks.put(two[1], tb)
            G.w(ta, tb)
            d = d_y[i % 2]
            d.n += 16
            pool.indirect_dma_start(ytok, bass.IndirectOffsetOnAxis(ap=slots[:, 1, i:i + 1], axis=0), y_, None,
                                    bounds_check=2 * T - 1, oob_is_err=False).then_inc(d.sem, 16)
            t_scatter[i] = (d.sem, d.name, d.n)

        for i in range(3):
            gather(i)
        tokens(0)
        for i in range(NT):
            s, t1 = hidden(i)
            tokens(i + 1)
            if i:
                down(i - 1)
            turn_hidden(i, s, t1)
        down(NT - 1)

        fence = everything() + [t_scatter[NT - 1], t_scatter[NT - 2]]
        for q in (V, S, P, G, Y):
            q.w(*fence)
        y2 = [A3(4096 * c_, 4, 1024) for c_ in range(2)]
        d_r = [Dma(f"d_r{i}") for i in range(4)]
        got = []
        for ti in range(4):
            for c_ in range(2):
                r0 = T * c_ + 128 * ti
                t = d_r[ti].start(Y, y2[c_][:, ti, :], ytok[r0:r0 + 128, :])
            got.append(t)
        eight = [banks.get() for _ in range(8)]
        for b in eight:
            P.w(*b.free)
        for ti in range(4):
            S.w(got[ti])
            t = S.inc(act.activation(y2[0][:, ti, :], y2[0][:, ti, :], ACT.Copy, scale=weight[:, ti:ti + 1]))
            V.w(t, got[ti])
            t = V.inc(dve.scalar_tensor_tensor(out=y2[0][:, ti, :], in0=y2[1][:, ti, :], scalar=weight[:, 4 + ti:5 + ti],
                                               in1=y2[0][:, ti, :], op0=ALU.mult, op1=ALU.add))
            P.w(t)
            for k in range(KT):
                t = P.inc(pe.transpose(eight[k].ap[:, 128 * ti:128 * ti + 128],
                                       y2[0][:, ti, 128 * k:128 * k + 128], C("ident")))
                if ti == 3:
                    V.w(t)
                    banks.put(eight[k], V.inc(dve.scalar_tensor_tensor(
                        out=hT[:, k, :], in0=hT[:, k, :], scalar=ALPHA, in1=eight[k].ap, op0=ALU.mult, op1=ALU.add)))
        layer_norm("lng", "lnb", 8)
        if stop == "ln4":
            dump(hT[:, :, :])
            return

        fence = everything()
        for q in (V, S, Y):
            q.w(*fence)
        pt = A3(0, 2)
        ph = arr_r[:, 1024:2048].rearrange("p (k n) -> p k n", n=T)
        pl = arr_r[:, 2048:3072].rearrange("p (k n) -> p k n", n=T)
        pp = A3(4096, 8)
        t = d_p.start(Y, pt, A["pT"][2])
        for k in range(2):
            t1 = split_x(ph[:, k, :], pl[:, k, :], pt[:, k, :], t)
        P.w(t1)
        embed(ph, pl, pp)
        for j in range(4):
            def f_e(i, b, t, j=j):
                s = scratch.get()
                S.w(t, *s.free)
                ts = S.inc(act.activation(s.ap, b.ap, ACT.Sigmoid))
                banks.put(b, ts)
                V.w(ts)
                t1 = V.inc(dve.tensor_tensor(s.ap, s.ap, pp[:, 2 * j + i, :], ALU.mult))
                V.w(t1)
                t1 = V.inc(dve.scalar_tensor_tensor(out=hT[:, 2 * j + i, :], in0=hT[:, 2 * j + i, :], scalar=ALPHA,
                                                    in1=s.ap, op0=ALU.mult, op1=ALU.add))
                scratch.put(s, t1)
            linear(256, xk, f_e)
        t = layer_norm("lng", "lnb", 16, split=False)
        Y.w(t)
        d_o = Dma("d_o")
        Y.w(d_o.start(Y, out, hT[:, :, :]))




def weight_blocks(W):
    blocks = []

    def cols(w, idx, k0=0, k1=None):
        w = w[128 * k0:(128 * k1 if k1 else None)]
        k = w.shape[0] // 128
        return w.reshape(k, 128, w.shape[1])[:, :, idx].transpose(1, 0, 2).reshape(128, -1)

    r = np.arange
    for i in range(2):
        w = W["w_in"][i]
        ka, ki = r(512, 576), r(896, 960)
        qa, qi, qb, kb, vb = r(0, 512), r(640, 896), r(964, 1476), r(1476, 1988), r(1988, 2500)
        blocks.append(cols(w, np.concatenate([ki, ki, qi[:128]])))
        blocks.append(cols(w, np.concatenate([qi[128:], ka, ka])))
        blocks.append(cols(w, np.concatenate([r(576, 640), r(960, 964)])))
        for c in (qa, qb, kb, vb):
            blocks += [cols(w, c[:256]), cols(w, c[256:])]
        for j in range(4):
            s = r(256 * j, 256 * j + 256)
            blocks += [cols(w, 2500 + s), cols(w, 3524 + s)]
            blocks.append(np.concatenate([cols(W["w_branch_a"][i], s), cols(W["w_branch_b"][i], s)], axis=1))
        for j in range(4):
            blocks.append(cols(W["w_out"][i], r(256 * j, 256 * j + 256)))
        f0 = 0
        for c in FCH:
            for j in range(0, c, 2):
                s = r(128 * (f0 + j), 128 * (f0 + j) + 256)
                blocks += [cols(W["w_up"][i], s), cols(W["w_up"][i], 2816 + s)]
            for j in range(4):
                blocks.append(cols(W["w_down"][i], r(256 * j, 256 * j + 256), f0, f0 + c))
            f0 += c
        blocks.append(cols(W["w_ple_proj"][i], r(1024)))
        for j in range(4):
            blocks.append(cols(W["w_ple_gate"][i], r(256 * j, 256 * j + 256)))
    w = W["w_in_2"][0]
    for c in (r(0, 512), r(512, 1024), r(1024, 1536)):
        blocks += [cols(w, c[:256]), cols(w, c[256:])]
    RW = 1536
    blocks.append(cols(w, r(RW + 1536, RW + 1792)))
    blocks.append(cols(w, r(RW + 1792, RW + 1824)))
    for j in range(4):
        s = r(RW + 128 * j, RW + 128 * j + 128)
        blocks += [cols(w, np.concatenate([s, 512 + s])), cols(w, 1024 + s)]
    for j in range(4):
        s = r(256 * j, 256 * j + 256)
        blocks += [cols(w, 3360 + s), cols(w, 4384 + s)]
        blocks.append(np.concatenate([cols(W["w_branch_attn_2"][0], s), cols(W["w_branch_rwkv_2"][0], s)], axis=1))
    for j in range(4):
        blocks.append(cols(W["w_out_2"][0], r(256 * j, 256 * j + 256)))
    blocks.append(cols(W["ple_proj_2"][0], r(1024)))
    for j in range(4):
        blocks.append(cols(W["ple_gate_2"][0], r(256 * j, 256 * j + 256)))
    return blocks


def expert_weights(W):
    gu = np.concatenate([W["exp_gate_2"][0], W["exp_up_2"][0]], axis=2)
    gu = gu.reshape(32, 2, 4, 128, 512).transpose(0, 1, 3, 2, 4).reshape(32, 2, 128, BLK)
    dn = W["exp_down_2"][0].reshape(32, 2, 128, 1024).transpose(0, 2, 1, 3).reshape(32, 1, 128, BLK)
    return np.ascontiguousarray(np.concatenate([gu, dn], axis=1))


def slot_consts():
    p = np.arange(128)[:, None]
    x = np.arange(8)[None, :]
    upto = np.zeros((128, 64))
    e = np.arange(32)
    upto[0:32, 0:32] = e[:, None] < e[None, :]
    upto[0:32, 32:64] = e[:, None] <= e[None, :]
    parts = [p < np.arange(128)[None, :], np.arange(128)[None, :] + 0 * p, np.arange(NT)[None, :] + 0 * p,
             128 * x + p - 4096, upto, p]
    return np.concatenate([np.asarray(a, np.float32) for a in parts], axis=1)


def columns(v):
    return np.asarray(v).reshape(-1, 128).T


def lay_out(inp):
    W = {k: np.asarray(v) for k, v in inp.items()}
    consts, cparts = const_table()
    parts, n_small = small_columns()
    small = np.zeros((128, n_small), np.float32)

    def put(name, a):
        x, y = parts[name]
        small[:, x:y] = a

    def twice(v):
        return np.concatenate([v, v])[:, None]

    for i in range(2):
        put(f"gmix{i}", columns(W["g_mix_norm"][i]))
        for n, s in (("gqa", "g_qa"), ("gka", "g_ka"), ("gqb", "g_qb"), ("gkb", "g_kb")):
            put(f"{n}{i}", twice(W[s][i]))
        put(f"gsub{i}", W["g_subln"][i][:, None])
        a, _ = parts[f"lam{i}"]
        for j, s in enumerate(("lam_q1", "lam_k1", "lam_q2", "lam_k2")):
            small[0:64, a + j] = W[s][i]
        put(f"gffn{i}", columns(W["g_ffn_norm"][i]))
        for j in range(3):
            put(f"cw{j}{i}", columns(W["conv_w"][i, j]))
        put(f"cb{i}", columns(W["conv_b"][i]))
        put(f"gple{i}", columns(W["g_ple_norm"][i]))
    put("lnig", columns(W["ln_in_g_2"]))
    put("lnib", columns(W["ln_in_b_2"]))
    a, _ = parts["mu"]
    mu = W["tok_mix_2"][0]
    small[:, a:a + 14] = columns(mu[:1792])
    small[0:32, a + 14] = mu[1792:]
    for n, s in (("dbase", "decay_base_2"), ("abase", "aaa_base_2"), ("kk", "k_k_2"), ("ka", "k_a_2"),
                 ("gng", "gn_g_2"), ("gnb", "gn_b_2")):
        put(n, columns(W[s][0]))
    put("rk", columns(W["r_k_2"][0].reshape(-1)))
    put("lng", columns(W["ln_g_2"][0].reshape(-1)))
    put("lnb", columns(W["ln_b_2"][0].reshape(-1)))
    put("rbias", np.concatenate([W["router_grp_bias_2"][0], W["router_exp_bias_2"][0]])[None, :])
    wr = np.concatenate([W["router_grp_2"][0], W["router_exp_2"][0]], axis=1)
    put("wrt", wr.reshape(8, 128, 36).transpose(1, 0, 2).reshape(128, -1))
    lora = np.zeros((4, 128, 384), np.float32)
    for j in range(4):
        c = slice(128 * j, 128 * j + 128)
        lora[j, 0:64, 0:128] = W["decay_up_2"][0][:, c]
        lora[j, 64:128, 0:128] = W["aaa_up_2"][0][:, c]
        lora[j, :, 128:256] = W["gate_up_2"][0][0:128, c]
        lora[j, 0:32, 256:384] = W["gate_up_2"][0][128:160, c]
    dist = 384 + np.arange(128)[:, None] - np.arange(512)[None, :]
    bias = W["rel_bias_2"][:, np.clip(dist, -128, 128) + 128]
    p_all = np.concatenate([W["p"][:, 0], W["p_2"][:, 0]])
    tiles = {
        "lora": lora,
        "bias": np.ascontiguousarray(bias.transpose(1, 0, 2).reshape(128, -1)),
        "consts": consts,
        "small": small,
        "xT": np.ascontiguousarray(W["x"][0].T.reshape(8, 128, 512).transpose(1, 0, 2)),
        "pT": np.ascontiguousarray(p_all.transpose(0, 2, 1).reshape(3, 2, 128, 512).transpose(0, 2, 1, 3)),
    }
    blocks = weight_blocks(W)
    sizes = [b.shape[1] for b in blocks]
    big = np.zeros((len(blocks), 128, BLK), np.float32)
    for i, b in enumerate(blocks):
        big[i, :, :b.shape[1]] = b
    tiles["W"] = big
    tiles["WE"] = expert_weights(W)
    tiles["moec"] = slot_consts()
    return tiles, sizes, cparts


def kernel(**inputs):
    import concourse.bacc as _bacc
    from concourse.bass_utils import run_bass_kernel_spmd as _run

    tiles, sizes, cparts = lay_out(inputs)
    nc = _bacc.Bacc("TRN2", target_bir_lowering=False, num_devices=1)
    arrays, args = {}, {}
    for name, a in tiles.items():
        arrays[f"in_{name}"] = a
        args[name] = nc.dram_tensor(f"in_{name}", a.shape, mybir.dt.from_np(a.dtype), kind="ExternalInput").ap()
    out = nc.dram_tensor("out_y", (128, 8, 512), F32, kind="ExternalOutput").ap()
    program(nc, args, out, sizes, cparts)
    r = _run(nc, [arrays], core_ids=[0])
    y = np.asarray(r.results[0]["out_y"])
    return y.transpose(1, 0, 2).reshape(1024, 512).T.reshape(1, 512, 1024)
```

```python
import math
from contextlib import ExitStack

import numpy as np

import concourse.bass as bass
from concourse import mybir

F32 = mybir.dt.float32
F32R = mybir.dt.float32r
ALU = mybir.AluOpType
ACT = mybir.ActivationFunctionType
AX = mybir.AxisListType

T = 512
D = 1024
KT = 8
NEG = -1.0e30
GONE = -3.0e38
EPS = 1e-6
LN_EPS = 1e-5
GN_EPS = 64e-5
ALPHA = 2.0 ** 0.25
BLK = 2048
FCH = [8, 8, 6]
NT = 39
NT_1 = 32
LAG = 55
SETTLE = 6
GATE_STEPS = (1, 2)
MOEC = 13624
POOL_CUTS = (2, 5)



def const_table():
    parts = {}
    out = []
    at = 0

    def put(name, a):
        nonlocal at
        a = np.asarray(a, np.float32).reshape(128, -1)
        parts[name] = (at, at + a.shape[1])
        at += a.shape[1]
        out.append(a)

    p = np.arange(128)
    put("ident", np.eye(128))
    put("ones", np.ones((128, 128)))
    put("blk", (p[:, None] // 64) == (p[None, :] // 64))
    swap = (p // 64) * 64 + (p % 64 + 32) % 64
    put("rot", (p[:, None] == swap[None, :]))
    inv = (np.float32(1) / np.power(np.float32(10000), np.arange(0, 64, 2, dtype=np.float32) / np.float32(64))).astype(np.float32)
    ang = (np.arange(T, dtype=np.float32)[:, None] * inv[None, :]).astype(np.float64).T
    cos, sin = np.cos(ang)[p % 32], np.sin(ang)[p % 32]
    put("cos", cos)
    put("sin", np.where((p % 64 < 32)[:, None], -sin, sin))
    x = np.arange(T)
    put("causal", np.where(x[None, :] - 384 <= p[:, None], 0.0, NEG))
    put("chunk", np.where(p[:, None] < 64, NEG, 0.0) * np.ones((1, 64)))
    s = (p % 64)[:, None]
    t = np.arange(64)[None, :]
    put("eye", s == t)
    put("tri", np.concatenate([s < t, s <= t], axis=1))
    put("lv1", (s // 2 == t // 2) & (s % 2 == 1) & (t % 2 == 0))
    for m in (1, 2, 4, 8, 16, 32):
        put(f"lt{m}", (s // (2 * m) == t // (2 * m)) & (s % (2 * m) < m) & (t % (2 * m) >= m))
    hs = np.zeros((128, 4, 8))
    hb = np.zeros((128, 4, 128))
    for j in range(4):
        for h in range(2):
            hs[64 * h:64 * h + 64, j, 2 * j + h] = 1
            hb[2 * j + h, j, 64 * h:64 * h + 64] = 1
    put("hsel", hs)
    put("hbr", hb)
    put("gidx", np.broadcast_to(8 - np.arange(4), (128, 4)))
    put("eidx", np.broadcast_to(64 - np.arange(32), (128, 32)))
    return np.concatenate(out, axis=1), parts


def small_columns():
    at = 0
    parts = {}
    for i in range(2):
        for name, n in (("gmix", 8), ("gqa", 1), ("gka", 1), ("gqb", 1), ("gkb", 1), ("gsub", 1), ("lam", 4),
                        ("gffn", 8), ("cw0", 44), ("cw1", 44), ("cw2", 44), ("cb", 44), ("gple", 8)):
            parts[f"{name}{i}"] = (at, at + n)
            at += n
    for name, n in (("lnig", 8), ("lnib", 8), ("mu", 15), ("dbase", 4), ("abase", 4), ("kk", 4), ("ka", 4),
                    ("rk", 4), ("gng", 4), ("gnb", 4), ("lng", 24), ("lnb", 24), ("rbias", 36), ("wrt", 288)):
        parts[name] = (at, at + n)
        at += n
    return parts, at


class Queue:

    def __init__(self, engine, sem, name):
        self.engine, self.sem, self.name = engine, sem, name
        self.count = 0
        self.seen = {}

    def w(self, *tickets):
        for t in tickets:
            if t is None:
                continue
            if isinstance(t, list):
                self.w(*t)
                continue
            sem, name, value = t
            if self.seen.get(name, 0) < value:
                self.engine.wait_ge(sem, value)
                self.seen[name] = value

    def inc(self, ins):
        self.count += 1
        ins.then_inc(self.sem, 1)
        return (self.sem, self.name, self.count)

    def last(self):
        return (self.sem, self.name, self.count) if self.count else None


class Slot:
    def __init__(self, ap):
        self.ap = ap
        self.free = []


class Pool:

    def __init__(self, aps):
        self.slots = [Slot(a) for a in aps]

    def get(self):
        assert self.slots, "no slot is free"
        return self.slots.pop(0)

    def put(self, slot, *tickets):
        slot.free = list(tickets)
        self.slots.append(slot)


def program(nc, A, out, sizes, cparts, stop=None, dbg=None):
    sp, n_small = small_columns()
    n_const = A["consts"].shape[1]
    ctx = ExitStack()
    with ctx:
        def sb(name, shape, dt=F32):
            return ctx.enter_context(nc.sbuf_tensor(name, shape, dt))

        def sem(name):
            return ctx.enter_context(nc.semaphore(name))

        pe, dve, act, pool, sync = nc.tensor, nc.vector, nc.scalar, nc.gpsimd, nc.sync
        P = Queue(pe, sem("s_pe"), "pe")
        V = Queue(dve, sem("s_dve"), "dve")
        S = Queue(act, sem("s_act"), "act")
        G = Queue(pool, sem("s_pool"), "pool")
        Y = Queue(sync, None, "sync")

        class Dma:

            def __init__(self, name):
                self.sem, self.name, self.n = sem(name), name, 0

            def start(self, queue, dst, src):
                self.n += 16
                queue.engine.dma_start(dst, src).then_inc(self.sem, 16)
                return (self.sem, self.name, self.n)

        hT = sb("hT", [128, KT, T])
        XH = sb("XH", [128, KT, T], F32R)
        XL = sb("XL", [128, KT, T], F32R)
        raw = sb("raw", [128, 2, BLK])
        wh = sb("wh", [128, 3, BLK], F32R)
        wl = sb("wl", [128, 3, BLK], F32R)
        cst = sb("cst", [128, n_const])
        sml = sb("sml", [128, n_small])
        NAR = 15120
        base = (nc.sbuf_base + 31) // 32 * 32
        ar = sb("arena", [128, NAR])
        rounded = nc.alloc_sbuf_tensor_at("arena_rounded", [128, NAR], F32R, offset=base)
        arr_r = rounded[:, :]
        slots = sb("slots", [128, 2, NT], mybir.dt.int32)
        owner = sb("owner", [1, 128], mybir.dt.int32)
        gsave = nc.dram_tensor("gsave", (4, 2, 2, 128, T), F32, kind="Internal").ap()
        hsave = nc.dram_tensor("hsave", (128, KT, T), F32, kind="Internal").ap()
        ysave = nc.dram_tensor("ysave", (128, 4, T), F32, kind="Internal").ap()
        d_sp, d_sp2 = Dma("d_sp"), Dma("d_sp2")
        xtok = nc.dram_tensor("xtok", (T, D), F32, kind="Internal").ap()
        ytok = nc.dram_tensor("ytok", (2 * T, D), F32, kind="Internal").ap()
        scr = sb("scr", [128, 9, T])
        tiny = sb("tiny", [128, 256])
        weight = tiny[:, 0:8]

        def C(name):
            a, b = cparts[name]
            return cst[:, a:b]

        def K(name, j=None):
            a, b = sp[name]
            return sml[:, a:b] if j is None else sml[:, a + j:a + j + 1]

        banks = Pool([ctx.enter_context(nc.psum_tensor(f"bank{i}", [128, T], F32))[:, :] for i in range(8)])
        scratch = Pool([scr[:, i, :] for i in range(9)])

        def everything():
            return [P.last(), V.last(), S.last(), G.last()]

        d_c, d_s = Dma("d_c"), Dma("d_s")
        t_xs = []
        for i in range(4):
            t_xs.append(Dma(f"d_x{i}").start(Y, hT[:, 2 * i:2 * i + 2, :], A["xT"][:, 2 * i:2 * i + 2, :]))
        t_s = d_s.start(Y, sml[:, :], A["small"])
        t_c = d_c.start(Y, cst[:, :], A["consts"])
        d_raw = [Dma(f"d_raw{i}") for i in range(2)]

        class Stream:
            def __init__(self):
                self.loaded = 0
                self.split = 0
                self.used = 0
                self.raw_t = []
                self.split_t = []
                self.done = {}

            def load(self):
                n = self.loaded
                if n >= len(sizes):
                    return
                if n >= 2:
                    Y.w(*self.split_t[n - 2])
                k = sizes[n]
                self.raw_t.append(d_raw[n % 2].start(Y, raw[:, n % 2, 0:k], A["W"][n, :, 0:k]))
                self.loaded += 1

            def cut(self):
                n = self.split
                if n >= len(sizes):
                    return
                k = sizes[n]
                r, h, l = raw[:, n % 2, 0:k], wh[:, n % 3, 0:k], wl[:, n % 3, 0:k]
                if n >= 3:
                    S.w(self.done[n - 3])
                    V.w(self.done[n - 3])
                S.w(self.raw_t[n])
                th = S.inc(act.activation(h, r, ACT.Copy))
                V.w(th, self.raw_t[n])
                tl = V.inc(dve.tensor_tensor(l, r, h.bitcast(F32), ALU.subtract))
                self.split_t.append((th, tl))
                self.split += 1
                self.load()

            def next(self, n_cols):
                n = self.used
                self.used += 1
                while self.split <= n:
                    self.cut()
                P.w(*self.split_t[n])
                k = sizes[n]
                return [x[:, n % 3, 0:k].rearrange("p (k n) -> p k n", n=n_cols) for x in (wh, wl)]

            def finished(self, ticket):
                self.done[self.used - 1] = ticket
                while self.split < self.used + 2:
                    if self.split >= len(sizes) or (self.split >= 3 and self.split - 3 not in self.done):
                        break
                    self.cut()

        stream = Stream()
        for _ in range(2):
            stream.load()

        bg = []

        def background(n):
            while n and bg:
                if next(bg[0], None) is None:
                    bg.pop(0)
                n -= 1

        later = []

        def settle(n):
            while n and later:
                if next(later[0], None) is None:
                    later.pop(0)
                n -= 1

        def units(jobs, every=1, fill=0, beside=None, n=0):
            jobs, live, r = list(jobs), [], 0
            while jobs or live:
                if jobs and r % every == 0:
                    live.append(jobs.pop(0))
                r += 1
                still, due = [], 0.0
                for g in live:
                    if next(g, None) is not None:
                        still.append(g)
                    due += n / len(live)
                    while due >= 1 and beside:
                        next(beside, None)
                        due -= 1
                live = still
                background(fill)

        def products(ps, w, x, ks, c0, c1, first, last):
            h, l = w
            n = len(ks)
            for i, (k, xh, xl, *ready) in enumerate(ks):
                P.w(*(ready or [x_ready[k] if ks is xk else None]))
                a, z = first and i == 0, last and i == n - 1
                pe.matmul(ps, h[:, k, c0:c1], xh, start=a, stop=False)
                pe.matmul(ps, h[:, k, c0:c1], xl, start=False, stop=False)
                mm = pe.matmul(ps, l[:, k, c0:c1], xh, start=False, stop=z)
            return P.inc(mm)

        def linear(n_cols, ks, evac, step=3):
            w = stream.next(n_cols)
            got = []
            for i in range((n_cols + 127) // 128):
                m = min(128, n_cols - 128 * i)
                b = banks.get()
                P.w(*b.free)
                t = products(b.ap[0:m, :], w, None, ks, 128 * i, 128 * i + m, True, True)
                got.append((b, t))
            stream.finished(t)
            for i, (b, t) in enumerate(got):
                evac(i, b, t)
            settle(SETTLE)
            background(step)

        def natural(n_cols, evac):
            h, l = stream.next(n_cols)
            got = []
            for ti in range(4):
                b = banks.get()
                P.w(*b.free)
                tt = slice(128 * ti, 128 * ti + 128)
                for k in range(KT):
                    P.w(x_ready[k])
                    pe.matmul(b.ap[:, 0:n_cols], XH[:, k, tt], h[:, k, :], start=k == 0, stop=False)
                    pe.matmul(b.ap[:, 0:n_cols], XL[:, k, tt], h[:, k, :], start=False, stop=False)
                    mm = pe.matmul(b.ap[:, 0:n_cols], XH[:, k, tt], l[:, k, :], start=False, stop=k == KT - 1)
                got.append((b, P.inc(mm)))
            stream.finished(got[-1][1])
            for ti, (b, t) in enumerate(got):
                evac(ti, b, t)
            settle(SETTLE)
            background(8)

        xk = [(k, XH[:, k, :], XL[:, k, :]) for k in range(KT)]
        x_ready = [None] * KT
        h_ready = [None] * KT

        def tz(a, b=None):
            return tiny[:, a:a + 1] if b is None else tiny[:, a:b]

        cols = [0]

        def tiny4():
            cols[0] = (cols[0] + 1) % 16
            return 160 + 4 * cols[0]

        class Running:

            def __init__(self, square=True):
                self.square, self.acc, self.t = square, None, None

            def add(self, src, *ready):
                if self.acc is None:
                    self.acc = scratch.get()
                    S.w(*ready, *self.acc.free)
                    self.t = S.inc(act.activation(self.acc.ap, src, ACT.Square if self.square else ACT.Copy))
                elif self.square:
                    s = scratch.get()
                    S.w(*ready, *s.free)
                    t = S.inc(act.activation(s.ap, src, ACT.Square))
                    V.w(t, self.t)
                    self.t = V.inc(dve.tensor_tensor(self.acc.ap, self.acc.ap, s.ap, ALU.add))
                    scratch.put(s, self.t)
                else:
                    V.w(*ready, self.t)
                    self.t = V.inc(dve.tensor_tensor(self.acc.ap, self.acc.ap, src, ALU.add))

            def sums(self):
                b = banks.get()
                P.w(*b.free, self.t)
                for ti in range(4):
                    mm = pe.matmul(b.ap[:, ti:ti + 1], self.acc.ap[:, 128 * ti:128 * ti + 128], C("ones")[:, 0:1],
                                   start=True, stop=True)
                t = P.inc(mm)
                scratch.put(self.acc, t)
                return b, t

        def narrow_root(b, t, scale, eps):
            c = tiny4()
            r = tz(c, c + 4)
            V.w(t)
            t1 = V.inc(dve.tensor_scalar(r, b.ap[:, 0:4], scale, eps, ALU.mult, ALU.add))
            banks.put(b, t1)
            S.w(t1)
            t2 = S.inc(act.activation(r, r, ACT.Sqrt))
            V.w(t2)
            return r, V.inc(dve.reciprocal(r, r))

        def spread(r, t):
            b = banks.get()
            P.w(*b.free, t)
            for ti in range(4):
                mm = pe.matmul(b.ap[:, 128 * ti:128 * ti + 128], r[:, ti:ti + 1].to_broadcast([128, 128]), C("ident"),
                               start=True, stop=True)
            return b, P.inc(mm)

        def total(acc, t_acc, ones="ones"):
            b = banks.get()
            P.w(*b.free, t_acc)
            t = P.inc(pe.matmul(b.ap, C(ones), acc.ap, start=True, stop=True))
            scratch.put(acc, t)
            return b, t

        def inverse_root(b, t, scale, eps):
            r = scratch.get()
            V.w(t, *r.free)
            t1 = V.inc(dve.tensor_scalar(r.ap, b.ap, scale, eps, ALU.mult, ALU.add))
            banks.put(b, t1)
            S.w(t1)
            t2 = S.inc(act.activation(r.ap, r.ap, ACT.Sqrt))
            V.w(t2)
            t3 = V.inc(dve.reciprocal(r.ap, r.ap))
            return r, t3

        def split_x(dh, dl, src, *tickets):
            S.w(*tickets)
            th = S.inc(act.activation(dh, src, ACT.Copy))
            V.w(th, *tickets)
            return V.inc(dve.tensor_tensor(dl, src, dh.bitcast(F32), ALU.subtract))

        def rms(gain, run, meanwhile=None):
            fence = everything()
            b, t = run.sums()
            r, t = narrow_root(b, t, 1.0 / D, EPS)
            if meanwhile:
                meanwhile()
            b, t = spread(r, t)
            V.w(*fence)
            S.w(*fence)
            V.w(t)
            us = []
            for k in range(KT + 1):
                if k < KT:
                    u = scratch.get()
                    V.w(*u.free)
                    tu = V.inc(dve.scalar_tensor_tensor(out=u.ap, in0=hT[:, k, :], scalar=K(gain, k), in1=b.ap,
                                                        op0=ALU.mult, op1=ALU.mult))
                    S.w(tu)
                    th = S.inc(act.activation(XH[:, k, :], u.ap, ACT.Copy))
                    us.append((u, tu, th))
                if k:
                    u, tu_, th = us[k - 1]
                    V.w(tu_, th)
                    x_ready[k - 1] = V.inc(dve.tensor_tensor(XL[:, k - 1, :], u.ap, XH[:, k - 1, :].bitcast(F32),
                                                             ALU.subtract))
                    scratch.put(u, x_ready[k - 1], th)
            banks.put(b, tu)
            return fence

        def layer_norm(g, b_, j, run, split=True, each=None):
            fence = everything()
            b, t = run.sums()
            c = tiny4()
            V.w(t)
            t = V.inc(dve.tensor_scalar(tz(c, c + 4), b.ap[:, 0:4], -1.0 / D, None, ALU.mult))
            banks.put(b, t)
            b, t = spread(tz(c, c + 4), t)
            V.w(*fence)
            S.w(*fence)
            V.w(t)
            b2 = banks.get()
            P.w(*b2.free)
            for k in range(KT):
                tk = V.inc(dve.tensor_tensor(hT[:, k, :], hT[:, k, :], b.ap, ALU.add))
                s = scratch.get()
                S.w(tk, *s.free)
                t = S.inc(act.activation(s.ap, hT[:, k, :], ACT.Square))
                P.w(t)
                t = P.inc(pe.matmul(b2.ap[0:1, :], C("ones")[:, 0:1], s.ap, start=k == 0, stop=k == KT - 1))
                scratch.put(s, t)
            banks.put(b, tk)
            s = scratch.get()
            S.w(t, *s.free)
            t = S.inc(act.activation(s.ap[0:1, :], b2.ap[0:1, :], ACT.Copy))
            banks.put(b2, t)
            b2 = banks.get()
            P.w(*b2.free, t)
            for ti in range(4):
                mm = pe.matmul(b2.ap[:, ti:ti + 1], s.ap[0:1, 128 * ti:128 * ti + 128], C("ones")[0:1, 0:1],
                               start=True, stop=True)
            t = P.inc(mm)
            scratch.put(s, t)
            r, t = narrow_root(b2, t, 1.0 / D, LN_EPS)
            b, t = spread(r, t)
            V.w(t)
            us = []
            for k in range(KT + 1):
                if k < KT:
                    u = scratch.get()
                    V.w(*u.free)
                    tu = V.inc(dve.scalar_tensor_tensor(out=u.ap, in0=hT[:, k, :], scalar=K(g, j + k), in1=b.ap,
                                                        op0=ALU.mult, op1=ALU.mult))
                    th = None
                    if split:
                        S.w(tu)
                        th = S.inc(act.activation(XH[:, k, :], u.ap, ACT.Identity, bias=K(b_, j + k)))
                    V.w(tu)
                    tn = V.inc(dve.tensor_scalar(hT[:, k, :], u.ap, K(b_, j + k), None, ALU.add))
                    h_ready[k] = tn
                    if each and k % 2:
                        each(k, tn)
                    us.append((u, tn, th))
                if k:
                    u, tn_, th = us[k - 1]
                    if split:
                        V.w(tn_, th)
                        x_ready[k - 1] = V.inc(dve.tensor_tensor(XL[:, k - 1, :], hT[:, k - 1, :],
                                                                 XH[:, k - 1, :].bitcast(F32), ALU.subtract))
                    scratch.put(u, tn_, th)
            banks.put(b, tu)
            return tn

        def rope(dst, t_dst, scale=None):
            b = banks.get()
            P.w(*b.free, t_dst)
            t = P.inc(pe.matmul(b.ap, C("rot"), dst, start=True, stop=True))
            u = scratch.get()
            V.w(t, *u.free)
            t1 = V.inc(dve.tensor_tensor(u.ap, b.ap, C("sin"), ALU.mult))
            banks.put(b, t1)
            G.w(t_dst, t)
            t2 = G.inc(pool.tensor_tensor(dst, dst, C("cos"), ALU.mult))
            V.w(t1, t2)
            t3 = V.inc(dve.tensor_tensor(dst, dst, u.ap, ALU.add))
            scratch.put(u, t3)
            if scale is not None:
                sb_, ts = scale
                V.w(ts, t3)
                t3 = V.inc(dve.tensor_tensor(dst, dst, sb_.ap, ALU.mult))
                banks.put(sb_, t3)
            return t3

        class HeadNorm:

            def __init__(self, n):
                self.n = n
                self.b = banks.get()
                P.w(*self.b.free)
                self.tiles = []

            def add(self, dst, gain, b, t):
                j = len(self.tiles)
                s = scratch.get()
                S.w(t, *s.free)
                ts = S.inc(act.activation(s.ap, b.ap, ACT.Square))
                V.w(ts)
                td = V.inc(dve.tensor_scalar(dst, b.ap, K(gain, 0), None, ALU.mult))
                banks.put(b, ts, td)
                self.tiles.append((dst, td))

                def heads():
                    P.w(ts)
                    a, _ = cparts["hsel"]
                    self.tp = P.inc(pe.matmul(self.b.ap[0:8, :], cst[:, a + 8 * j:a + 8 * j + 8], s.ap,
                                              start=j == 0, stop=j == self.n - 1))
                    scratch.put(s, self.tp)
                    yield True
                later.append(heads())

            def close(self, put):
                n = 2 * self.n
                r = scratch.get()
                V.w(self.tp, *r.free)
                t1 = V.inc(dve.tensor_scalar(r.ap[0:n, :], self.b.ap[0:n, :], 1.0 / 64, EPS, ALU.mult, ALU.add))
                banks.put(self.b, t1)
                S.w(t1)
                t2 = S.inc(act.activation(r.ap[0:n, :], r.ap[0:n, :], ACT.Sqrt))
                V.w(t2)
                t3 = V.inc(dve.reciprocal(r.ap[0:n, :], r.ap[0:n, :]))
                yield True
                a, _ = cparts["hbr"]
                for j, (dst, td) in enumerate(self.tiles):
                    b = banks.get()
                    P.w(*b.free, t3)
                    t = P.inc(pe.matmul(b.ap, cst[0:n, a + 128 * j:a + 128 * j + 128], r.ap[0:n, :],
                                        start=True, stop=True))
                    if j == self.n - 1:
                        scratch.put(r, t)
                    put(j, rope(dst, td, (b, t)))
                    yield True

        def probs(q, k, mask, n, scale, tq, got):
            b = banks.get()
            P.w(*b.free, *tq)
            t = P.inc(pe.matmul(b.ap[:, 0:n], q, k, start=True, stop=True))
            yield True
            s, c = scratch.get(), tiny4()
            V.w(t, *s.free, *tq)
            t1 = V.inc(dve.tensor_tensor_reduce(s.ap[:, 0:n], b.ap[:, 0:n], mask, scale, GONE, ALU.add, ALU.max, tz(c)))
            banks.put(b, t1)
            V.w(t1)
            t2 = V.inc(dve.tensor_scalar(tz(c + 1), tz(c), -1.0, None, ALU.mult))
            yield True
            S.w(t2)
            t3 = S.inc(act.activation(s.ap[:, 0:n], s.ap[:, 0:n], ACT.Exp, bias=tz(c + 1), accum_out=tz(c + 2)))
            yield True
            V.w(t3)
            t4 = V.inc(dve.reciprocal(tz(c + 3), tz(c + 2)))
            V.w(t4)
            got.append((s, c, t4))

        def turned(s, t, ti, got):
            n = 128 * (ti + 1)
            b = banks.get()
            P.w(*b.free, t)
            for j in range(ti + 1):
                mm = pe.transpose(b.ap[:, 128 * j:128 * j + 128], s.ap[:, 128 * j:128 * j + 128], C("ident"))
            tt = P.inc(mm)
            scratch.put(s, tt)
            yield True
            o = scratch.get()
            S.w(tt, *o.free)
            to = S.inc(act.activation(o.ap[:, 0:n], b.ap[:, 0:n], ACT.Copy))
            banks.put(b, to)
            yield True
            P.w(to)
            got.append(o)

        def attend(q, k, v, mask, ti, tq, acc, out_ap, first, finish):
            n = 128 * (ti + 1)
            got = []
            yield from probs(q, k, mask, n, 0.125, tq, got)
            s, c, t = got.pop()
            t = V.inc(dve.tensor_scalar(s.ap[:, 0:n], s.ap[:, 0:n], tz(c + 3), None, ALU.mult))
            yield True
            yield from turned(s, t, ti, got)
            o = got.pop()
            if first:
                acc.append(banks.get())
                P.w(*acc[0].free)
            for j in range(ti + 1):
                mm = pe.matmul(out_ap(acc[0]), v(j), o.ap[:, 128 * j:128 * j + 128], start=j == 0, stop=j == ti)
            t = P.inc(mm)
            scratch.put(o, t)
            yield True
            if finish:
                yield from finish(acc[0], t)

        def A_(off, n):
            return ar[:, off:off + n]

        def A3(off, k, n=T):
            return ar[:, off:off + k * n].rearrange("p (k n) -> p k n", n=n)

        def evac_add(n0, run=None):
            def f(i, b, t):
                V.w(t)
                t = V.inc(dve.tensor_tensor(hT[:, n0 + i, :], b.ap, hT[:, n0 + i, :], ALU.add))
                banks.put(b, t)
                if run:
                    run.add(hT[:, n0 + i, :], t)
            return f

        def dump(src, *tickets):
            d = Dma("d_dump")
            Y.w(*everything())
            t = d.start(Y, out, src)
            Y.w(t)

        d_gw = [Dma(f"d_gw{i}") for i in range(4)]
        d_gr = [Dma(f"d_gr{i}") for i in range(8)]
        n_gate = [0]
        gate_t = [None] * 4

        def gates(js):
            for j in js:
                for which in range(2):
                    h, l = stream.next(256)
                    for i in range(2):
                        while len(banks.slots) < 2:
                            yield True
                        b = banks.get()
                        P.w(*b.free)
                        c = slice(128 * i, 128 * i + 128)
                        for k, xh, xl in xk:
                            P.w(x_ready[k])
                            pe.matmul(b.ap, h[:, k, c], xh, start=k == 0, stop=False)
                            pe.matmul(b.ap, h[:, k, c], xl, start=False, stop=False)
                            mm = pe.matmul(b.ap, l[:, k, c], xh, start=False, stop=k == KT - 1)
                            if k % 2 and k < KT - 1:
                                yield True
                        t = P.inc(mm)
                        if i:
                            stream.finished(t)
                        while len(scratch.slots) < 2:
                            yield True
                        s = scratch.get()
                        S.w(t, *s.free)
                        ts = S.inc(act.activation(s.ap, b.ap, ACT.Sigmoid))
                        banks.put(b, ts)
                        n = n_gate[0] % 4
                        n_gate[0] += 1
                        Y.w(ts, gate_t[n])
                        gate_t[n] = d_gw[n].start(Y, gsave[j, which, i], s.ap)
                        scratch.put(s, gate_t[n])
                        yield True

        def gated_branches(XA, XB, t_in, c0):
            mixf = A3(c0, 8)
            fence = everything()
            V.w(*fence)
            Y.w(*gate_t)
            ahead = {}

            def fetch(j):
                Y.w(V.last())
                for which in range(2):
                    for i in range(2):
                        s = scratch.get()
                        Y.w(*s.free)
                        ahead[j, which, i] = (s, d_gr[4 * (j % 2) + 2 * which + i].start(Y, s.ap, gsave[j, which, i]))
            fetch(0)
            for j in range(4):
                if j < 3:
                    fetch(j + 1)
                sg = {(which, i): ahead[j, which, i] for which in range(2) for i in range(2)}
                w = stream.next(256)
                P.w(*t_in)
                done = []
                for i in range(2):
                    for which, X in ((0, XA), (1, XB)):
                        b = banks.get()
                        P.w(*b.free)
                        t = products(b.ap, w, None, [(4 * which + k, X[0][:, k, :], X[1][:, k, :]) for k in range(4)],
                                     128 * i, 128 * i + 128, True, True)
                        done.append((i, which, b, t))
                stream.finished(t)
                for i, which, b, t in done:
                    s, ts = sg[which, i]
                    o = mixf[:, 2 * j + i, :]
                    V.w(t, ts)
                    if which == 0:
                        t0 = V.inc(dve.tensor_tensor(o, b.ap, s.ap, ALU.mult))
                        banks.put(b, t0)
                        scratch.put(s, t0)
                    else:
                        t1 = V.inc(dve.tensor_tensor(s.ap, b.ap, s.ap, ALU.mult))
                        banks.put(b, t1)
                        V.w(t0, t1)
                        t2 = V.inc(dve.tensor_tensor(o, o, s.ap, ALU.add))
                        scratch.put(s, t2)
            fence = everything()
            S.w(*fence)
            V.w(*fence)
            for k in range(KT):
                x_ready[k] = split_x(XH[:, k, :], XL[:, k, :], mixf[:, k, :], t2)

        def first_layer(li, run, run_out):
            lam_init = 0.8 - 0.6 * math.exp(-0.3 * li)
            o = 0

            def take(n):
                nonlocal o
                o += n
                return o - n
            KI, QI = take(512), take(1024)
            o = 2048
            OBL = take(2048)
            KA, WV, QA, MB = take(512), take(4 * 68), take(2048), take(2048)
            QB, KB, VB = take(2048), take(2048), take(2048)
            assert o <= NAR
            rms(f"gmix{li}", run)
            ready = {}

            def keep(dst, name):
                def f(b, t):
                    V.w(t)
                    td = V.inc(dve.tensor_copy(dst, b.ap))
                    banks.put(b, td)

                    def turn():
                        ready[name] = rope(dst, td)
                        yield True
                    later.append(turn())
                return f

            hk = HeadNorm(1)
            linear(256, xk, lambda i, b, t: keep(A_(KI, 512), "ki")(b, t) if i == 0 else keep(A_(QI, 512), "qi0")(b, t))
            linear(256, xk, lambda i, b, t: keep(A_(QI + 512, 512), "qi1")(b, t) if i == 0
                   else hk.add(A_(KA, 512), f"gka{li}", b, t))
            b = banks.get()
            t = None
            for j in range(2):
                t = V.inc(dve.tensor_tensor(tz(60 + j), K(f"lam{li}", 2 * j), K(f"lam{li}", 2 * j + 1), ALU.mult))
            P.w(*b.free, t)
            t = P.inc(pe.matmul(b.ap[:, 0:2], C("ones"), tz(60, 62), start=True, stop=True))
            S.w(t)
            t = S.inc(act.activation(tz(62, 64), b.ap[:, 0:2], ACT.Exp))
            banks.put(b, t)
            V.w(t)
            t = V.inc(dve.tensor_tensor(tz(64), tz(63), tz(62), ALU.subtract))
            V.w(t)
            t_lam = V.inc(dve.tensor_scalar(tz(65), tz(64), -lam_init, None, ALU.add))

            wv = A3(WV, 4, 68)

            def evac_wv(ti, b, t):
                V.w(t)
                ready["wv", ti] = V.inc(dve.tensor_copy(wv[:, ti, :], b.ap[:, 0:68]))
                banks.put(b, ready["wv", ti])
            natural(68, evac_wv)
            later.append(hk.close(lambda j, t: ready.__setitem__("ka", t)))
            settle(SETTLE)

            mb = A3(MB, 4)
            t_mask = {0: None}

            def scores(ti):
                n = 128 * (ti + 1)
                t_prev = None
                V.w(ready["wv", ti])
                for h in range(4):
                    r0 = 64 * (h % 2)
                    b = banks.get()
                    P.w(*b.free, ready["ki"], ready[f"qi{h // 2}"])
                    t = P.inc(pe.matmul(b.ap[:, 0:n], A_(QI + 512 * (h // 2), 512)[r0:r0 + 64, 128 * ti:128 * ti + 128],
                                        A_(KI, 512)[r0:r0 + 64, 0:n], start=True, stop=True))
                    s = scratch.get()
                    S.w(t, *s.free)
                    t = S.inc(act.activation(s.ap[:, 0:n], b.ap[:, 0:n], ACT.Relu, scale=1.0 / 16))
                    banks.put(b, t)
                    w_ = wv[:, ti, 64 + h:65 + h]
                    V.w(t, t_prev)
                    if h == 0:
                        t_prev = V.inc(dve.tensor_scalar(mb[:, ti, 0:n], s.ap[:, 0:n], w_, None, ALU.mult))
                    else:
                        t_prev = V.inc(dve.scalar_tensor_tensor(out=mb[:, ti, 0:n], in0=s.ap[:, 0:n], scalar=w_,
                                                                in1=mb[:, ti, 0:n], op0=ALU.mult, op1=ALU.add))
                    scratch.put(s, t_prev)
                V.w(t_prev)
                return V.inc(dve.tensor_tensor(mb[:, ti, 0:n], mb[:, ti, 0:n], C("causal")[:, 512 - n:512], ALU.add))

            def choose(ti, t):
                n = 128 * (ti + 1)
                m = mb[:, ti, 0:n]
                top = tz(64 + 8 * ti, 72 + 8 * ti)
                for r in range(16):
                    V.w(t)
                    t = V.inc(dve.max(top, m))
                    yield t
                    V.w(t)
                    t = V.inc(dve.match_replace(m, top, m, GONE))
                    yield t
                V.w(t)
                t = V.inc(dve.tensor_scalar(m, m, -2.0e38, NEG, ALU.is_gt, ALU.mult))
                V.w(t)
                t_mask[ti] = V.inc(dve.tensor_tensor(m, m, C("causal")[:, 512 - n:512], ALU.add))
                yield t_mask[ti]

            for ti in (1, 2, 3):
                bg.append(choose(ti, scores(ti)))

            hn = HeadNorm(4)
            for j in range(2):
                linear(256, xk, lambda i, b, t, j=j: hn.add(A_(QA + 512 * (2 * j + i), 512), f"gqa{li}", b, t), 16)
            tqa, tqb, tkb = {}, {}, {}
            later.append(hn.close(tqa.__setitem__))
            hn = HeadNorm(4)
            for j in range(2):
                linear(256, xk, lambda i, b, t, j=j: hn.add(A_(QB + 512 * (2 * j + i), 512), f"gqb{li}", b, t), 16)
            later.append(hn.close(tqb.__setitem__))
            hn = HeadNorm(4)
            for j in range(2):
                linear(256, xk, lambda i, b, t, j=j: hn.add(A_(KB + 512 * (2 * j + i), 512), f"gkb{li}", b, t), 16)
            later.append(hn.close(tkb.__setitem__))
            vb = A3(VB, 4)
            tvb = []

            def evac_vb(c0):
                def f(ti, b, t):
                    V.w(t)
                    td = V.inc(dve.tensor_copy(vb[:, ti, c0:c0 + 256], b.ap[:, 0:256]))
                    banks.put(b, td)
                    tvb.append(td)
                return f
            natural(256, evac_vb(0))
            natural(256, evac_vb(256))

            obh = arr_r[:, 0:2048].rearrange("p (k n) -> p k n", n=T)
            obl = arr_r[:, OBL:OBL + 2048].rearrange("p (k n) -> p k n", n=T)
            fence = everything()
            S.w(*fence)
            V.w(*fence)
            settle(1000)
            P.w(*tvb)
            last = {}

            def diff_head(ti, h, acc):
                n = 128 * (ti + 1)
                cm = C("causal")[:, 512 - n:512]
                got = [[], []]
                two = []
                for e in range(2):
                    r0 = 64 * e
                    qt = A_(QB + 512 * h, 512)[r0:r0 + 64, 128 * ti:128 * ti + 128]
                    kt = A_(KB + 512 * h, 512)[r0:r0 + 64, 0:n]
                    two.append(probs(qt, kt, cm, n, 0.125, [tqb[h], tkb[h]], got[e]))
                while two:
                    two = [g for g in two if next(g, None) is not None]
                    last["qk"] = P.last()
                    if two:
                        yield True
                (s1, c1, u1), (s2, c2, u2) = got[0][0], got[1][0]
                V.w(t_lam, u2)
                t = V.inc(dve.tensor_scalar(s2.ap[:, 0:n], s2.ap[:, 0:n], tz(c2 + 3), tz(65), ALU.mult, ALU.mult))
                V.w(t, u1)
                t = V.inc(dve.scalar_tensor_tensor(out=s1.ap[:, 0:n], in0=s1.ap[:, 0:n], scalar=tz(c1 + 3),
                                                   in1=s2.ap[:, 0:n], op0=ALU.mult, op1=ALU.add))
                scratch.put(s2, t)
                yield True
                yield from turned(s1, t, ti, got[0])
                pt = got[0].pop()
                if h == 0:
                    acc.append(banks.get())
                    P.w(*acc[0].free)
                for j in range(ti + 1):
                    mm = pe.matmul(acc[0].ap[:, 128 * h:128 * h + 128], vb[:, j, 128 * h:128 * h + 128],
                                   pt.ap[:, 128 * j:128 * j + 128], start=j == 0, stop=j == ti)
                t = P.inc(mm)
                scratch.put(pt, t)
                yield True
                if h < 3:
                    return
                acc = acc[0]
                s, q = scratch.get(), scratch.get()
                S.w(t, *s.free, *q.free)
                ts = S.inc(act.activation(s.ap, acc.ap, ACT.Copy))
                tq = S.inc(act.activation(q.ap, acc.ap, ACT.Square))
                banks.put(acc, tq)
                yield True
                b, t = total(q, tq)
                yield True
                r, t = inverse_root(b, t, 1.0 / 128, EPS)
                V.w(t, ts)
                t = V.inc(dve.scalar_tensor_tensor(out=s.ap, in0=s.ap, scalar=K(f"gsub{li}", 0), in1=r.ap,
                                                   op0=ALU.mult, op1=ALU.mult))
                scratch.put(r, t)
                V.w(t)
                t = V.inc(dve.tensor_scalar(s.ap, s.ap, 1.0 - lam_init, None, ALU.mult))
                yield True
                s3 = s.ap.rearrange("p (h n) -> p h n", h=4)
                tt = slice(128 * ti, 128 * ti + 128)
                last["ob"] = split_x(obh[:, :, tt], obl[:, :, tt], s3, t)
                scratch.put(s, last["ob"])

            jobs = []
            for ti in range(4):
                acc = []
                jobs += [diff_head(ti, h, acc) for h in range(4)]
            beside = gates(range(4))
            units(jobs, every=2, fill=4, beside=beside, n=GATE_STEPS[0])
            background(1000)

            oah = arr_r[:, QB:QB + 2048].rearrange("p (k n) -> p k n", n=T)
            oal = arr_r[:, KB:KB + 2048].rearrange("p (k n) -> p k n", n=T)
            S.w(last["qk"])
            V.w(last["qk"])
            P.w(ready["wv", 3])

            def keep_oa(ti):
                def f(acc, t):
                    a3 = acc.ap.rearrange("p (h n) -> p h n", h=4)
                    tt = slice(128 * ti, 128 * ti + 128)
                    last["oa"] = split_x(oah[:, :, tt], oal[:, :, tt], a3, t)
                    banks.put(acc, last["oa"])
                    yield True
                return f

            def out_of(h):
                r0 = 64 * (h % 2)
                return lambda b: b.ap[r0:r0 + 64, 128 * (h // 2):128 * (h // 2) + 128]

            jobs = []
            for ti in range(4):
                n = 128 * (ti + 1)
                mask = C("causal")[:, 512 - n:512] if ti == 0 else mb[:, ti, 0:n]
                acc = []
                for h in range(8):
                    r0 = 64 * (h % 2)
                    jobs.append(attend(A_(QA + 512 * (h // 2), 512)[r0:r0 + 64, 128 * ti:128 * ti + 128],
                                       A_(KA, 512)[r0:r0 + 64, 0:n], lambda j: wv[:, j, 0:64], mask, ti,
                                       [tqa[h // 2], ready["ka"], t_mask[ti]], acc, out_of(h), h == 0,
                                       keep_oa(ti) if h == 7 else None))
            units(jobs, beside=beside, n=GATE_STEPS[1])
            for _ in beside:
                pass
            t_oa, t_ob = last["oa"], last["ob"]

            gated_branches((oah, oal), (obh, obl), [t_oa, t_ob], 4096)
            run = Running()
            for j in range(4):
                linear(256, xk, evac_add(2 * j, run))

            if stop == f"mix{li}":
                return
            rms(f"gffn{li}", run)
            run = Running()
            pp = A3(8192, 8)
            ple = fetch_p(li)
            f0 = 0
            for c in FCH:
                uh = arr_r[:, 0:4096].rearrange("p (k n) -> p k n", n=T)
                ul = arr_r[:, 4096:8192].rearrange("p (k n) -> p k n", n=T)
                fence = [P.last()]
                S.w(*fence)
                V.w(*fence)
                ready_u = {}
                for j in range(0, c, 2):
                    conv = {}

                    def evac_conv(which, j=j):
                        def f(i, b, t):
                            fi = f0 + j + i + 22 * which
                            s = scratch.get()
                            S.w(t, *s.free)
                            t0 = S.inc(act.activation(s.ap, b.ap, ACT.Identity, scale=K(f"cw2{li}", fi),
                                                      bias=K(f"cb{li}", fi)))
                            V.w(t0, t)
                            t1 = V.inc(dve.scalar_tensor_tensor(out=s.ap[:, 1:T], in0=b.ap[:, 0:T - 1],
                                                                scalar=K(f"cw1{li}", fi), in1=s.ap[:, 1:T],
                                                                op0=ALU.mult, op1=ALU.add))
                            V.w(t1)
                            t2 = V.inc(dve.scalar_tensor_tensor(out=s.ap[:, 2:T], in0=b.ap[:, 0:T - 2],
                                                                scalar=K(f"cw0{li}", fi), in1=s.ap[:, 2:T],
                                                                op0=ALU.mult, op1=ALU.add))
                            banks.put(b, t0, t2)
                            if which == 0:
                                S.w(t2)
                                t2 = S.inc(act.activation(s.ap, s.ap, ACT.Gelu_apprx_tanh))
                                conv[i] = (s, t2)
                            else:
                                g, tg = conv[i]
                                V.w(t2, tg)
                                t3 = V.inc(dve.tensor_tensor(s.ap, s.ap, g.ap, ALU.mult))
                                scratch.put(g, t3)
                                t4 = split_x(uh[:, j + i, :], ul[:, j + i, :], s.ap, t3)
                                scratch.put(s, t4)
                                ready_u[j + i] = t4
                        return f
                    linear(256, xk, evac_conv(0))
                    linear(256, xk, evac_conv(1))
                ku = [(k, uh[:, k, :], ul[:, k, :], ready_u[k]) for k in range(c)]
                for j in range(4):
                    linear(256, ku, evac_add(2 * j, run if c == FCH[-1] and f0 + c == 22 else None))
                f0 += c

            if stop == f"ffn{li}":
                return
            rms(f"gple{li}", run, lambda: embed(pp, ple))
            for j in range(4):
                def f(i, b, t, j=j):
                    s = scratch.get()
                    S.w(t, *s.free)
                    ts = S.inc(act.activation(s.ap, b.ap, ACT.Sigmoid))
                    banks.put(b, ts)
                    V.w(ts)
                    t1 = V.inc(dve.tensor_tensor(s.ap, s.ap, pp[:, 2 * j + i, :], ALU.mult))
                    V.w(t1)
                    t1 = V.inc(dve.tensor_tensor(hT[:, 2 * j + i, :], hT[:, 2 * j + i, :], s.ap, ALU.add))
                    scratch.put(s, t1)
                    run_out.add(hT[:, 2 * j + i, :], t1)
                linear(256, xk, f)

        d_p = [Dma(f"d_p{i}") for i in range(2)]

        def fetch_p(i):
            ph = arr_r[:, 12288:13312].rearrange("p (k n) -> p k n", n=T)
            pl = arr_r[:, 13312:14336].rearrange("p (k n) -> p k n", n=T)
            two = []
            for k in range(2):
                s = scratch.get()
                Y.w(*s.free)
                two.append((s, d_p[k].start(Y, s.ap, A["pT"][i, :, k])))
            for k, (s, t) in enumerate(two):
                t = split_x(ph[:, k, :], pl[:, k, :], s.ap, t)
                scratch.put(s, t)
            return [(k, ph[:, k, :], pl[:, k, :], t) for k in range(2)]

        def embed(pp, ks):
            w = stream.next(1024)
            for i in range(8):
                b = banks.get()
                P.w(*b.free)
                t = products(b.ap, w, None, ks, 128 * i, 128 * i + 128, True, True)
                if i == 7:
                    stream.finished(t)
                S.w(t)
                tc = S.inc(act.activation(pp[:, i, :], b.ap, ACT.Copy))
                banks.put(b, tc)


        run = Running()
        for k in range(KT):
            run.add(hT[:, k, :], t_xs[k // 2])
        for q in (P, V, S, G):
            q.w(t_c, t_s, t_xs)
        for _ in range(2):
            stream.cut()
        for li in range(2):
            run_out = Running(li == 0)
            first_layer(li, run, run_out)
            run = run_out
            if stop in (f"layer{li}", f"mix{li}", f"ffn{li}"):
                dump(hT[:, :, :])
                return
        def bc(ap, shape):
            return ap.to_broadcast(shape)

        fence = everything()
        layer_norm("lnig", "lnib", 0, run)
        if stop == "ln2":
            dump(hT[:, :, :])
            return
        Y.w(*fence)
        YA, YR, QO, KO, VO, BI = 0, 2048, 2048, 4096, 6144, 8192
        bias = A3(BI, 8)
        d_b = Dma("d_b")
        t_b = d_b.start(Y, ar[:, BI:BI + 4096], A["bias"])
        V.w(t_b)
        t_b = V.inc(dve.tensor_scalar(ar[:, BI:BI + 4096], ar[:, BI:BI + 4096], 8.0, None, ALU.mult))
        V.w(t_b)
        for h in range(8):
            t_b = V.inc(dve.tensor_tensor(bias[:, h, 448:512], bias[:, h, 448:512], C("chunk"), ALU.add))
        Y.w(*h_ready)
        t_hs = d_sp.start(Y, hsave, hT[:, :, :])
        rdy = {}

        def evac_to(dst, name):
            def f(i, b, t):
                S.w(t)
                rdy[name, i] = S.inc(act.activation(dst(i), b.ap, ACT.Copy))
                banks.put(b, rdy[name, i])
            return f

        for name, off in (("q", QO), ("k", KO)):
            for j in range(2):
                linear(256, xk, evac_to(lambda i, off=off, j=j: A_(off + 512 * (2 * j + i), 512), (name, j)))
        vn = A3(VO, 4)

        def evac_vn(c0):
            def f(ti, b, t):
                S.w(t)
                rdy["v"] = S.inc(act.activation(vn[:, ti, c0:c0 + 256], b.ap[:, 0:256], ACT.Copy))
                banks.put(b, rdy["v"])
            return f
        natural(256, evac_vn(0))
        natural(256, evac_vn(256))
        ya = A3(YA, 4)
        P.w(rdy["v"])
        V.w(t_b)
        last = {}

        def keep_ya(ti):
            def f(acc, t):
                S.w(t)
                last["ya"] = S.inc(act.activation(ya[:, :, 128 * ti:128 * ti + 128],
                                                  acc.ap.rearrange("p (h n) -> p h n", h=4), ACT.Copy))
                banks.put(acc, last["ya"])
                yield True
            return f

        def out_of(h):
            r0 = 64 * (h % 2)
            return lambda b: b.ap[r0:r0 + 64, 128 * (h // 2):128 * (h // 2) + 128]

        jobs = []
        for ti in range(4):
            n = 128 * (ti + 1)
            acc = []
            for h in range(8):
                r0 = 64 * (h % 2)
                j, i = divmod(h // 2, 2)
                jobs.append(attend(A_(QO + 512 * (h // 2), 512)[r0:r0 + 64, 128 * ti:128 * ti + 128],
                                   A_(KO + 512 * (h // 2), 512)[r0:r0 + 64, 0:n],
                                   lambda j, h=h: vn[:, j, 64 * h:64 * h + 64], bias[:, h, 512 - n:512], ti,
                                   [rdy[("q", j), i], rdy[("k", j), i]], acc, out_of(h), h == 0,
                                   keep_ya(ti) if h == 7 else None))
        units(jobs)
        Y.w(last["ya"])
        t_ys = d_sp2.start(Y, ysave, ya)

        fence = everything()
        for q in (V, S, P):
            q.w(*fence)
        yr = A3(YR, 4)
        WD, GD = A_(4096, 512), A3(4608, 2)
        omu = tz(128, 143)
        V.w()
        t_omu = V.inc(dve.tensor_scalar(omu, K("mu"), -1.0, 1.0, ALU.mult, ALU.add))
        S.w(t_omu)

        def mixed(dst, b, t, col, rows=128):
            S.w(t)
            t0 = S.inc(act.activation(dst, b.ap[0:rows, :], ACT.Identity, scale=tz(128 + col)[0:rows, :]))
            V.w(t0)
            t1 = V.inc(dve.scalar_tensor_tensor(out=dst[:, 1:T], in0=b.ap[0:rows, 0:T - 1], scalar=K("mu", col)[0:rows, :],
                                                in1=dst[:, 1:T], op0=ALU.mult, op1=ALU.add))
            banks.put(b, t1)
            return t1

        def evac_lo(i, b, t):
            if i == 0:
                t = mixed(WD, b, t, 12)
                S.w(t)
                rdy["wd"] = S.inc(act.activation(WD[0:64, :], WD[0:64, :], ACT.Tanh))
            else:
                t = mixed(GD[:, 0, :], b, t, 13)
                S.w(t)
                rdy["gd"] = S.inc(act.activation(GD[:, 0, :], GD[:, 0, :], ACT.Sigmoid))

        def evac_g1(i, b, t):
            t = mixed(GD[0:32, 1, :], b, t, 14, 32)
            S.w(t)
            rdy["gd"] = S.inc(act.activation(GD[0:32, 1, :], GD[0:32, 1, :], ACT.Sigmoid))
        linear(256, xk, evac_lo)
        linear(32, xk, evac_g1)
        P.w(rdy["wd"], rdy["gd"])

        hm = (C("blk")[:, 0:1], C("blk")[:, 64:65])

        def c8(ap):
            return ap.rearrange("p (c t) -> p c t", c=8)

        def cells(v, n):
            return [v[:, 512 * i:512 * i + 512] for i in range(n)]
        ca = cparts["cos"][0]
        hflat = hT[:, :, :].rearrange("p k n -> p (k n)")
        places = [(ar[:, 5632:6656], cells(ar[:, 6656:7680], 2), cells(ar[:, 7680:9216], 3), ar[:, 9216:9728],
                   ar[:, 9728:13824], ar[:, 13824:14080]),
                  (ar[:, 0:1024], cells(ar[:, 1024:2048], 2), cells(cst[:, ca:ca + 1536], 3), ar[:, 14080:14592],
                   hflat, ar[:, 14592:14848])]
        assert cparts["sin"][0] == ca + 512 and cparts["causal"] == (ca + 1024, ca + 1536)
        freed = [everything(), everything() + [t_hs, t_ys]]
        d_l = [Dma(f"d_l{i}") for i in range(2)]
        out_t = []

        def recurrence(j):
            AR, (Bt, Kt), (Bn, Kn, Vn), BV, room, st = places[j % 2]
            for q in (V, S, P):
                q.w(*freed[j % 2])
            AR4 = AR.rearrange("p (c w t) -> p c w t", c=8, w=2)
            LR, MK = room[:, 0:1024], room[:, 1024:2048]
            X, XT, T1, Lm = cells(room[:, 2048:4096], 4)
            rT, kT, vT, lw, cc, aT, kkT, tm = cells(room, 8)
            YT = Bt
            STs = [st[:, 0:128], st[:, 128:256]]
            Bz, Kz = (Bt, T1), (Kt, Lm)
            for i in range(2):
                t = V.inc(dve.memset(STs[i], 0.0))
            V.w(t)
            lora = scratch.get()
            Y.w(*lora.free)
            t_l = d_l[j % 2].start(Y, lora.ap[:, 0:384], A["lora"][j])
            P.w(t_l)
            rk = {}

            def evac_rk(i, b, t):
                rk[i] = mixed((rT, kT)[i], b, t, 4 * i + j)
            linear(256, xk, evac_rk)
            linear(128, xk, lambda i, b, t: rk.__setitem__(2, mixed(vT, b, t, 8 + j)))

            yield True
            def low_rank(r0, r1, dst, base):
                b = banks.get()
                P.w(*b.free)
                t = P.inc(pe.matmul(b.ap, lora.ap[r0:r1, 0:128], WD[r0:r1, :], start=True, stop=True))
                yield True
                S.w(t)
                t = S.inc(act.activation(dst, b.ap, ACT.Sigmoid, bias=K(base, j)))
                banks.put(b, t)
                return t
            t = yield from low_rank(0, 64, lw, "dbase")
            V.w(t)
            yield True
            t_lw = V.inc(dve.tensor_scalar(lw, lw, -math.exp(-0.5), None, ALU.mult))
            t_a = yield from low_rank(64, 128, aT, "abase")

            t, src = t_lw, lw
            w2 = scratch.get()
            V.w(*w2.free)
            S.w(*w2.free)
            for n_, sh in enumerate((1, 2, 4, 8, 16, 32)):
                dst = cc if n_ % 2 else w2.ap
                V.w(t)
                S.w(t)
                t1 = V.inc(dve.tensor_tensor(c8(dst)[:, :, sh:64], c8(src)[:, :, sh:64], c8(src)[:, :, 0:64 - sh], ALU.add))
                t2 = S.inc(act.activation(c8(dst)[:, :, 0:sh], c8(src)[:, :, 0:sh], ACT.Copy))
                V.w(t2)
                S.w(t1)
                t, src = [t1, t2], dst
                yield True
            t_c = t
            scratch.put(w2, *t_c)

            V.w(rk[1], rk[0], rk[2])
            tk = V.inc(dve.tensor_scalar(kkT, kT, K("kk", j), None, ALU.mult))
            s = scratch.get()
            S.w(tk, *s.free)
            ts = S.inc(act.activation(s.ap, kkT, ACT.Square))
            yield True
            b, t = total(s, ts, "blk")
            yield True
            r = scratch.get()
            V.w(t, *r.free)
            t = V.inc(dve.tensor_scalar(r.ap, b.ap, 1e-24, None, ALU.max))
            banks.put(b, t)
            yield True
            S.w(t)
            t = S.inc(act.activation(r.ap, r.ap, ACT.Sqrt))
            yield True
            V.w(t)
            t = V.inc(dve.reciprocal(r.ap, r.ap))
            V.w(t)
            tk = V.inc(dve.tensor_tensor(kkT, kkT, r.ap, ALU.mult))
            scratch.put(r, tk)
            yield True
            V.w(t_a)
            t = V.inc(dve.tensor_scalar(tm, aT, -1.0, K("ka", j), ALU.add, ALU.mult))
            V.w(t)
            t_k = V.inc(dve.scalar_tensor_tensor(out=kT, in0=tm, scalar=1.0, in1=kT, op0=ALU.add, op1=ALU.mult))
            V.w(tk)
            t_a = V.inc(dve.tensor_tensor(aT, aT, kkT, ALU.mult))

            s = scratch.get()
            V.w(t_k, *s.free)
            t = V.inc(dve.scalar_tensor_tensor(out=s.ap, in0=rT, scalar=K("rk", j), in1=kT, op0=ALU.mult, op1=ALU.mult))
            yield True
            b, t = total(s, t, "blk")
            yield True
            V.w(t)
            t = V.inc(dve.tensor_tensor(BV, b.ap, vT, ALU.mult))
            banks.put(b, t)

            e = scratch.get()
            S.w(t_c, *e.free)
            t = S.inc(act.activation(e.ap, cc, ACT.Exp))
            yield True
            V.w(t)
            PC = tz(144, 152) if j % 2 else tz(224, 232)
            t_pc = V.inc(dve.tensor_copy(PC, c8(e.ap)[:, :, 63]))
            t_R = V.inc(dve.tensor_tensor(AR4[:, :, 1, :], c8(rT), c8(e.ap), ALU.mult))
            scratch.put(e, t_R)
            V.w(t_c)
            t = V.inc(dve.tensor_tensor(tm, cc, lw, ALU.subtract))
            S.w(t)
            t = S.inc(act.activation(tm, tm, ACT.Exp))
            yield True
            V.w(t)
            t_A = V.inc(dve.scalar_tensor_tensor(out=AR4[:, :, 0, :], in0=c8(kkT), scalar=-1.0, in1=c8(tm),
                                                 op0=ALU.mult, op1=ALU.mult))
            e = scratch.get()
            S.w(*e.free)
            t = S.inc(act.activation(e.ap, cc, ACT.Exp, scale=-1.0))
            yield True
            V.w(t, t_a, t_pc)
            V.w(t_A)
            for src, dst in ((aT, Bz), (kT, Kz)):
                for h in range(2):
                    t_BK = V.inc(dve.scalar_tensor_tensor(out=dst[h], in0=src, scalar=hm[h], in1=e.ap,
                                                          op0=ALU.mult, op1=ALU.mult))
            yield True
            V.w(t_BK)
            t = V.inc(dve.tensor_tensor(c8(e.ap), c8(e.ap), bc(PC.unsqueeze(2), [128, 8, 64]), ALU.mult))
            V.w(t)
            V.inc(dve.tensor_tensor(aT, aT, e.ap, ALU.mult))
            t = V.inc(dve.tensor_tensor(kT, kT, e.ap, ALU.mult))
            scratch.put(e, t)
            yield True
            P.w(t, rk[2])
            for src, dst in ((aT, Bn), (kT, Kn), (vT, Vn)):
                b = banks.get()
                P.w(*b.free)
                for i in range(4):
                    mm = pe.transpose(b.ap[:, 128 * i:128 * i + 128], src[:, 128 * i:128 * i + 128], C("ident"))
                t = P.inc(mm)
                S.w(t)
                t_n = S.inc(act.activation(dst, b.ap, ACT.Copy))
                banks.put(b, t_n)
                yield True

            P.w(t_R, t_A, t_BK)
            tri = C("tri").unsqueeze(1)
            V.w(t_n)
            for lhs, dst in ((Bz, LR), (Kz, MK)):
                for half in range(2):
                    b = banks.get()
                    P.w(*b.free)
                    for c in range(4 * half, 4 * half + 4):
                        for h in range(2):
                            pr = 64 * (c % 2)
                            col = 128 * (2 * (c // 2 - 2 * half) + h)
                            mm = pe.matmul(b.ap[pr:pr + 64, col:col + 128], lhs[h][:, 64 * c:64 * c + 64],
                                           AR[:, 128 * c:128 * c + 128], start=True, stop=True)
                    t = P.inc(mm)
                    yield True
                    V.w(t)
                    t_m = V.inc(dve.tensor_tensor(dst[:, 512 * half:512 * half + 512].rearrange("p (g n) -> p g n", g=4),
                                                  b.ap.rearrange("p (g n) -> p g n", g=4), bc(tri, [128, 4, 128]), ALU.mult))
                    banks.put(b, t_m)
            b = banks.get()
            P.w(*b.free)
            for c in range(8):
                for h in range(2):
                    pr = 64 * (c % 2)
                    col = 64 * (2 * (c // 2) + h)
                    mm = pe.matmul(b.ap[pr:pr + 64, col:col + 64], AR4[:, c, 0, :],
                                   Bz[h][:, 64 * c:64 * c + 64], start=True, stop=True)
            t = P.inc(mm)
            LT = LR.rearrange("p (g w n) -> p g w n", g=8, w=2)[:, :, 0, :]

            def m8(name):
                return bc(C(name).unsqueeze(1), [128, 8, 64])
            V.w(t)
            t = V.inc(dve.tensor_tensor(c8(X), c8(b.ap), m8("lv1"), ALU.mult))
            banks.put(b, t)
            V.w(t)
            t_X = V.inc(dve.tensor_tensor(c8(X), c8(X), m8("eye"), ALU.add))
            V.w(t_m)
            t = V.inc(dve.tensor_tensor(c8(XT), LT, m8("lt1"), ALU.mult))
            V.w(t)
            t_X = V.inc(dve.tensor_tensor(c8(XT), c8(XT), m8("eye"), ALU.add))

            def small(lhs, rhs):
                b = banks.get()
                P.w(*b.free)
                for c in range(8):
                    for h in range(2):
                        pr = 64 * (c % 2)
                        col = 64 * (2 * (c // 2) + h)
                        mm = pe.matmul(b.ap[pr:pr + 64, col:col + 64], lhs[pr:pr + 64, col:col + 64],
                                       rhs[pr:pr + 64, col:col + 64], start=True, stop=True)
                return b, P.inc(mm)

            yield True
            V.w(t_m)
            t_L = V.inc(dve.tensor_tensor(c8(Lm), LT, m8("lt2"), ALU.mult))
            for m in (2, 4, 8, 16, 32):
                yield True
                P.w(t_L, t_X)
                b, t = small(Lm, X)
                if m < 32:
                    V.w(t)
                    t_L = V.inc(dve.tensor_tensor(c8(Lm), LT, m8(f"lt{2 * m}"), ALU.mult))
                yield True
                S.w(t)
                t = S.inc(act.activation(T1, b.ap, ACT.Copy))
                banks.put(b, t)
                yield True
                P.w(t)
                if m < 32:
                    b1, u1 = small(XT, T1)
                b2, t = small(T1, XT)
                yield True
                V.w(t)
                if m < 32:
                    t_x1 = V.inc(dve.tensor_tensor(X, X, b1.ap, ALU.add))
                    banks.put(b1, t_x1)
                t_X = V.inc(dve.tensor_tensor(XT, XT, b2.ap, ALU.add))
                banks.put(b2, t_X)
            yield True

            P.w(t_X)
            yb = banks.get()
            P.w(*yb.free)
            gu = scratch.get()
            V.w(*gu.free)
            t_S = None
            for c in range(8):
                pr = 64 * (c % 2)
                cp = c // 2
                S0, S1 = STs[c % 2], STs[(c + 1) % 2]
                b = banks.get()
                P.w(*b.free, t_S)
                o = b.ap[pr:pr + 64, 0:128]
                if c:
                    pe.matmul(o, AR4[:, c, 0, :], S0, start=True, stop=False, skip_group_check=True)
                for h in range(2):
                    hr = 64 * h
                    col = 128 * (2 * cp + h)
                    mm = pe.matmul(o[:, hr:hr + 64], MK[pr:pr + 64, col:col + 64],
                                   Vn[pr:pr + 64, 128 * cp + hr:128 * cp + hr + 64], start=c == 0, stop=True,
                                   skip_group_check=True)
                t = P.inc(mm)
                yield True
                V.w(t)
                t = V.inc(dve.tensor_copy(gu.ap[pr:pr + 64, 0:128], o))
                yield True
                P.w(t)
                for h in range(2):
                    col = 64 * (2 * cp + h)
                    mm = pe.matmul(b.ap[pr:pr + 64, 128 + 64 * h:192 + 64 * h], XT[pr:pr + 64, col:col + 64],
                                   gu.ap[pr:pr + 64, 64 * h:64 * h + 64], start=True, stop=True)
                t = P.inc(mm)
                yield True
                V.w(t)
                t = V.inc(dve.tensor_copy(gu.ap[pr:pr + 64, 128:256], b.ap[pr:pr + 64, 128:256]))
                yield True
                P.w(t)
                u = gu.ap[pr:pr + 64, 128:256]
                v_ = Vn[pr:pr + 64, 128 * cp:128 * cp + 128]
                o = b.ap[:, 256:384]
                pe.matmul(o, Bn[pr:pr + 64, 128 * cp:128 * cp + 128], u, start=True, stop=False)
                t = P.inc(pe.matmul(o, Kn[pr:pr + 64, 128 * cp:128 * cp + 128], v_, start=False, stop=True))
                if c:
                    pe.matmul(yb.ap[:, 64 * c:64 * c + 64], S0, AR4[:, c, 1, :], start=True, stop=False,
                              skip_group_check=True)
                for h in range(2):
                    hr = 64 * h
                    o = yb.ap[hr:hr + 64, 64 * c:64 * c + 64]
                    col = 128 * (2 * cp + h)
                    pe.matmul(o, u[:, hr:hr + 64], LR[pr:pr + 64, col + 64:col + 128], start=c == 0, stop=False,
                              skip_group_check=True)
                    mm = pe.matmul(o, v_[:, hr:hr + 64], MK[pr:pr + 64, col + 64:col + 128], start=False, stop=True,
                                   skip_group_check=True)
                t_Y = P.inc(mm)
                yield True
                V.w(t)
                for h in range(2):
                    hr = 64 * h
                    d = (slice(hr, hr + 64), slice(hr, hr + 64))
                    ps = b.ap[hr:hr + 64, 256 + hr:320 + hr]
                    if c:
                        t_S = V.inc(dve.scalar_tensor_tensor(out=S1[d], in0=S0[d], scalar=PC[hr:hr + 64, c:c + 1],
                                                             in1=ps, op0=ALU.mult, op1=ALU.add))
                    else:
                        t_S = V.inc(dve.tensor_copy(S1[d], ps))
                V.w(t_S, t_Y)
                banks.put(b, t_S)
                yield True
            scratch.put(gu, t_Y)
            S.w(t_Y)
            t = S.inc(act.activation(YT, yb.ap, ACT.Copy))
            banks.put(yb, t)
            yield True

            b = banks.get()
            P.w(*b.free, t)
            t = P.inc(pe.matmul(b.ap, C("blk"), YT, start=True, stop=True))
            yield True
            V.w(t)
            t = V.inc(dve.scalar_tensor_tensor(out=YT, in0=b.ap, scalar=-1.0 / 64, in1=YT, op0=ALU.mult, op1=ALU.add))
            banks.put(b, t)
            s = scratch.get()
            S.w(t, *s.free)
            ts = S.inc(act.activation(s.ap, YT, ACT.Square))
            yield True
            b, t = total(s, ts, "blk")
            yield True
            r, t = inverse_root(b, t, 1.0 / 64, GN_EPS)
            V.w(t)
            t = V.inc(dve.scalar_tensor_tensor(out=YT, in0=YT, scalar=K("gng", j), in1=r.ap, op0=ALU.mult, op1=ALU.mult))
            scratch.put(r, t)
            V.w(t)
            t = V.inc(dve.scalar_tensor_tensor(out=YT, in0=YT, scalar=K("gnb", j), in1=BV, op0=ALU.add, op1=ALU.add))
            b = banks.get()
            P.w(*b.free)
            pe.matmul(b.ap, lora.ap[:, 128:256], GD[:, 0, :], start=True, stop=False)
            tg = P.inc(pe.matmul(b.ap, lora.ap[0:32, 256:384], GD[0:32, 1, :], start=False, stop=True))
            scratch.put(lora, tg)
            yield True
            V.w(tg, t)
            t_yr = V.inc(dve.tensor_tensor(yr[:, j, :], b.ap, YT, ALU.mult))
            banks.put(b, t_yr)
            freed[j % 2] = everything()
            out_t.append(t_yr)

        XA = [arr_r[:, o:o + 2048].rearrange("p (k n) -> p k n", n=T) for o in (5632, 7680)]
        XB = [arr_r[:, o:o + 2048].rearrange("p (k n) -> p k n", n=T) for o in (9728, 11776)]
        d_ya = [Dma(f"d_ya{i}") for i in range(4)]
        early = {}

        def ahead_of_branches():
            for q in (V, S, Y):
                q.w(*freed[0])
            for i in range(4):
                s = scratch.get()
                Y.w(*s.free)
                t = d_ya[i].start(Y, s.ap, ysave[:, i])
                yield True
                early["a"] = split_x(XA[0][:, i, :], XA[1][:, i, :], s.ap, t)
                scratch.put(s, early["a"])
                yield True
            for i in range(3):
                early["b"] = split_x(XB[0][:, i, :], XB[1][:, i, :], yr[:, i, :], *out_t[0:3])
                yield True

        waiting, live, since, beside = [recurrence(j) for j in range(4)], [], 0, iter(())
        while waiting or live:
            if waiting and len(live) < 2 and (not live or since >= LAG):
                for _ in beside:
                    pass
                live.append(waiting.pop(0))
                next(live[-1])
                beside = gates([3 - len(waiting)])
                since = 0
            since += 1
            still = []
            for g in live:
                if next(g, None) is not None:
                    still.append(g)
                if since % 2:
                    next(beside, None)
            live = still
            if not waiting and len(live) == 1 and not early:
                early["a"] = None
                live.append(ahead_of_branches())
        for _ in beside:
            pass
        t_yr = out_t

        Y.w(*everything())
        t_hr = d_sp.start(Y, hT[:, :, :], hsave)
        if stop == "rwkv":
            t_yb = d_sp2.start(Y, ya, ysave)

        if stop in ("rwkv", "attn2"):
            V.w(t_yr, t_hr, t_yb)
            t = V.inc(dve.memset(hT[:, 0:4, :], 0.0))
            V.w(t)
            V.inc(dve.tensor_copy(hT[:, 0:4, :], ya))
            V.inc(dve.tensor_copy(hT[:, 4:8, :], yr))
            dump(hT[:, :, :])
            return

        fence = everything()
        for q in (V, S):
            q.w(*fence)
        t2 = split_x(XB[0][:, 3, :], XB[1][:, 3, :], yr[:, 3, :])
        gated_branches(XA, XB, [early["a"], early["b"], t2], 0)
        V.w(t_hr)
        run = Running(False)

        def evac_alpha(n0):
            def f(i, b, t):
                V.w(t)
                t = V.inc(dve.scalar_tensor_tensor(out=hT[:, n0 + i, :], in0=hT[:, n0 + i, :], scalar=ALPHA,
                                                   in1=b.ap, op0=ALU.mult, op1=ALU.add))
                banks.put(b, t)
                run.add(hT[:, n0 + i, :], t)
            return f
        for j in range(4):
            linear(256, xk, evac_alpha(2 * j))
        fence = everything()
        layer_norm("lng", "lnb", 0, run, split=False)
        if stop == "ln3":
            dump(hT[:, :, :])
            return

        RO = ar[:, 14000:15100]

        def R(a, n, *dims):
            v = RO[:, a:a + n]
            if len(dims) == 2:
                return v.rearrange("p (x y) -> p x y", x=dims[0])
            return v
        d_m = Dma("d_m")
        Y.w(*fence)
        G.w(*[t for s_ in scratch.slots for t in s_.free])
        t = G.inc(pool.memset(scr[:, 0:6, :], 0.0))
        for s_ in scratch.slots:
            s_.free = [t]
        t_cm = d_m.start(Y, A_(MOEC, A["moec"].shape[1]), A["moec"])
        lg = R(0, 144, 4, 36)
        wrt = K("wrt").rearrange("p (k n) -> p k n", n=36)
        b = banks.get()
        P.w(*b.free)
        for k in range(KT):
            P.w(h_ready[k])
            mm = pe.matmul(b.ap[0:36, :], wrt[:, k, :], hT[:, k, :], start=k == 0, stop=k == KT - 1)
        t = P.inc(mm)
        lgT = ar[0:36, 12288:12800]
        S.w(t)
        t = S.inc(act.activation(lgT, b.ap[0:36, :], ACT.Copy))
        banks.put(b, t)
        b = banks.get()
        P.w(*b.free, t)
        for ti in range(4):
            mm = pe.transpose(b.ap[:, 36 * ti:36 * ti + 36], lgT[:, 128 * ti:128 * ti + 128], C("ident")[0:36, 0:36])
        t = P.inc(mm)

        xn = A3(8192, 4, 1024)
        d_t = Dma("d_t")
        for ti in range(4):
            for half in range(2):
                b1 = banks.get()
                P.w(*b1.free)
                for k in range(4):
                    mm = pe.transpose(b1.ap[:, 128 * k:128 * k + 128],
                                      hT[:, 4 * half + k, 128 * ti:128 * ti + 128], C("ident"))
                t1 = P.inc(mm)
                S.w(t1)
                t1 = S.inc(act.activation(xn[:, ti, 512 * half:512 * half + 512], b1.ap, ACT.Copy))
                banks.put(b1, t1)
            Y.w(t1)
            t_tok = d_t.start(Y, xtok[128 * ti:128 * ti + 128, :], xn[:, ti, :])

        def vv(ins):
            V.w(V.inc(ins))
        V.w(t)
        vv(dve.tensor_tensor(lg, b.ap[:, 0:144].rearrange("p (x y) -> p x y", x=4),
                             bc(K("rbias").unsqueeze(1), [128, 4, 36]), ALU.add))
        banks.put(b, V.last())
        gl, el = lg[:, :, 0:4], lg[:, :, 4:36]
        gm, gs = R(144, 4), R(148, 4)
        gd, oh, eq = R(152, 16, 4, 4), R(168, 16, 4, 4), R(184, 16, 4, 4)
        mx = R(200, 4)
        m1, m2, w1, w2_, dd = R(204, 4), R(208, 4), R(212, 4), R(216, 4), R(220, 4)
        me, oa, ob, qq = R(224, 128, 4, 32), R(352, 128, 4, 32), R(480, 128, 4, 32), R(608, 128, 4, 32)
        comb = R(736, 128, 4, 32)

        def w4(v, n):
            return bc(v.unsqueeze(2), [128, 4, n])
        vv(dve.tensor_reduce(gm, gl, AX.X, ALU.max))
        vv(dve.tensor_tensor(gd, gl, w4(gm, 4), ALU.subtract))
        vv(dve.tensor_scalar(oh, gd, 0.0, None, ALU.is_equal))
        S.w(V.last())
        V.w(S.inc(act.activation(gd, gd, ACT.Exp)))
        vv(dve.tensor_reduce(gs, gd, AX.X, ALU.add))
        vv(dve.reciprocal(gs, gs))
        vv(dve.tensor_tensor(eq, oh, bc(C("gidx").unsqueeze(1), [128, 4, 4]), ALU.mult))
        vv(dve.tensor_reduce(mx, eq, AX.X, ALU.max))
        vv(dve.tensor_tensor(oh, eq, w4(mx, 4), ALU.is_equal))
        vv(dve.tensor_scalar(oh, oh, -1.0, 1.0e30, ALU.add, ALU.mult))
        for g in range(4):
            vv(dve.tensor_tensor(me[:, :, 8 * g:8 * g + 8], el[:, :, 8 * g:8 * g + 8],
                                 w4(oh[:, :, g], 8), ALU.add))

        def first_of(dst, v, m):
            vv(dve.tensor_reduce(m, v, AX.X, ALU.max))
            vv(dve.tensor_tensor(qq, v, w4(m, 32), ALU.is_equal))
            vv(dve.tensor_tensor(qq, qq, bc(C("eidx").unsqueeze(1), [128, 4, 32]), ALU.mult))
            vv(dve.tensor_reduce(mx, qq, AX.X, ALU.max))
            vv(dve.tensor_tensor(dst, qq, w4(mx, 32), ALU.is_equal))
        first_of(oa, me, m1)
        vv(dve.scalar_tensor_tensor(out=me, in0=oa, scalar=-2.0e30, in1=me, op0=ALU.mult, op1=ALU.add))
        first_of(ob, me, m2)
        vv(dve.tensor_tensor(dd, m2, m1, ALU.subtract))
        S.w(V.last())
        V.w(S.inc(act.activation(dd, dd, ACT.Exp)))
        vv(dve.tensor_scalar(w1, dd, 1.0, None, ALU.add))
        vv(dve.reciprocal(w1, w1))
        vv(dve.tensor_tensor(w1, w1, gs, ALU.mult))
        vv(dve.tensor_tensor(w2_, w1, dd, ALU.mult))
        cm = A_(MOEC, A["moec"].shape[1])
        V.w(t_cm)
        P.w(t_cm)
        before, count_to = cm[:, 0:128], cm[:, 128:256]
        tile_to, pair, upto, part = cm[:, 256:256 + NT], cm[:, 256 + NT:264 + NT], cm[0:32, 264 + NT:328 + NT], \
            cm[:, 328 + NT:329 + NT]
        onehot_p, onehot_t = A3(12288, 8, 128), A3(12288 + 1024, 8, NT)
        oab, rank, owned, basis = qq, R(224, 128, 4, 32), R(736, 8), R(744, 64)
        prod = R(808, 128, 4, 32)
        place, tile_, over = R(936, 8), R(944, 8), R(952, 8)
        fidx, gidx_ = R(960, NT), R(1000, NT)
        vv(dve.tensor_copy(weight[:, 0:4], w1))
        vv(dve.tensor_copy(weight[:, 4:8], w2_))
        vv(dve.tensor_tensor(oab, oa, ob, ALU.add))
        b, b2 = banks.get(), banks.get()
        P.w(*b.free, *b2.free, V.last())
        for ti in range(4):
            for tj in range(ti):
                pe.matmul(b.ap[:, 32 * ti:32 * ti + 32], C("ones"), oab[:, tj, :], start=tj == 0, stop=False)
            mm = pe.matmul(b.ap[:, 32 * ti:32 * ti + 32], before, oab[:, ti, :], start=ti == 0, stop=True)
        t = P.inc(mm)
        for ti in range(4):
            mm = pe.matmul(b2.ap[0:32, 0:1], oab[:, ti, :], C("ones")[:, 0:1], start=ti == 0, stop=ti == 3)
        t2 = P.inc(mm)
        V.w(t2)
        vv(dve.tensor_scalar(owned[0:32, 0:1], b2.ap[0:32, 0:1], 0.0, None, ALU.is_gt))
        for j in (1, 2, 3):
            vv(dve.scalar_tensor_tensor(out=owned[0:32, 0:1], in0=b2.ap[0:32, 0:1], scalar=128.0 * j,
                                        in1=owned[0:32, 0:1], op0=ALU.is_gt, op1=ALU.add))
        banks.put(b2, V.last())
        b2 = banks.get()
        P.w(*b2.free, V.last())
        t2 = P.inc(pe.matmul(b2.ap[:, 0:64], owned[0:32, 0:1].to_broadcast([32, 128]), upto, start=True, stop=True))
        V.w(t)
        vv(dve.tensor_copy(rank, b.ap[:, 0:128].rearrange("p (x y) -> p x y", x=4)))
        banks.put(b, V.last())
        V.w(t2)
        vv(dve.tensor_copy(basis, b2.ap[:, 0:64]))
        banks.put(b2, V.last())
        vv(dve.tensor_scalar(prod[:, 0, :], basis[:, 32:64], part, None, ALU.is_le))
        vv(dve.tensor_reduce(owned[:, 1:2], prod[:, 0, :], AX.X, ALU.add))
        vv(dve.tensor_scalar(owned[:, 1:2], owned[:, 1:2], 31.0, None, ALU.min))
        b = banks.get()
        P.w(*b.free, V.last())
        t_own = P.inc(pe.matmul(b.ap[0:1, 0:128], owned[:, 1:2], C("ident"), start=True, stop=True))
        V.w(t_own)
        vv(dve.tensor_copy(owner[0:1, :], b.ap[0:1, 0:128]))
        banks.put(b, V.last())
        vv(dve.tensor_copy(owner[0:1, 127:128], basis[0:1, 63:64]))
        Y.w(V.last())
        for c_, one in ((0, oa), (1, ob)):
            vv(dve.tensor_tensor(prod, one, rank, ALU.mult))
            vv(dve.tensor_reduce(place[:, 4 * c_:4 * c_ + 4], prod, AX.X, ALU.add))
            vv(dve.tensor_tensor(prod, one, bc(basis[:, 0:32].unsqueeze(1), [128, 4, 32]), ALU.mult))
            vv(dve.tensor_reduce(tile_[:, 4 * c_:4 * c_ + 4], prod, AX.X, ALU.add))
        vv(dve.tensor_scalar(over, place, 128.0, None, ALU.is_ge))
        for j in (2, 3):
            vv(dve.scalar_tensor_tensor(out=over, in0=place, scalar=128.0 * j, in1=over, op0=ALU.is_ge, op1=ALU.add))
        vv(dve.tensor_tensor(tile_, tile_, over, ALU.add))
        vv(dve.scalar_tensor_tensor(out=place, in0=over, scalar=-128.0, in1=place, op0=ALU.mult, op1=ALU.add))
        for x in range(8):
            V.inc(dve.tensor_scalar(onehot_p[:, x, :], count_to, place[:, x:x + 1], None, ALU.is_equal))
            t = V.inc(dve.tensor_scalar(onehot_t[:, x, :], tile_to, tile_[:, x:x + 1], pair[:, x:x + 1],
                                        ALU.is_equal, ALU.mult))
        b = banks.get()
        P.w(*b.free, t)
        for x in range(8):
            mm = pe.matmul(b.ap[:, 0:NT], onehot_p[:, x, :], onehot_t[:, x, :], start=x == 0, stop=x == 7)
        V.w(P.inc(mm))
        vv(dve.tensor_scalar(fidx, b.ap[:, 0:NT], 4096.0, None, ALU.add))
        banks.put(b, V.last())
        vv(dve.tensor_copy(slots[:, 1, :], fidx))
        vv(dve.tensor_scalar(gidx_, fidx, 512.0, -512.0, ALU.is_ge, ALU.mult))
        vv(dve.tensor_tensor(gidx_, gidx_, fidx, ALU.add))
        vv(dve.tensor_copy(slots[:, 0, :], gidx_))

        assert len(scratch.slots) == 9
        fence = everything() + [t_tok]
        for q in (V, S, P, G):
            q.w(*fence)
        flat = "p a b -> p (a b)"
        xe = [scr[:, 2 * i:2 * i + 2, :].rearrange(flat) for i in range(3)]
        act_ = [scr[:, 6 + i, 0:256] for i in range(2)]
        ye = [A_(8192 + 1024 * i, 1024) for i in range(2)]
        xs = [[arr_r[:, 10240 + 2048 * w_ + 1024 * i:11264 + 2048 * w_ + 1024 * i].rearrange("p (k n) -> p k n", n=128)
               for w_ in range(2)] for i in range(2)]
        hs = [arr_r[:, 14336 + 256 * w_:14592 + 256 * w_].rearrange("p (k n) -> p k n", n=128) for w_ in range(2)]
        d_e = [Dma(f"d_e{i}") for i in range(4)]

        def run_tiles(lo, hi, d_g, d_y):
            order = []
            for i in range(lo, hi):
                order += [(i, 0), (i, 1)] + ([(i - 1, 2)] if i > lo else [])
            order.append((hi - 1, 2))

            class Experts:

                def __init__(self):
                    self.loaded = self.split = self.used = 0
                    self.raw_t, self.split_t, self.done = [], [], []
                    for _ in range(4):
                        self.load()

                def load(self):
                    n = self.loaded
                    if n >= len(order):
                        return
                    if n >= 4:
                        Y.w(*self.split_t[2 * (n - 4)], *self.split_t[2 * (n - 4) + 1])
                    i, part_ = order[n]
                    dst = A_(2048 * (n % 4), 2048)

                    def fetch():
                        e = nc.values_load(owner[0:1, i:i + 1], engines=[mybir.EngineType.SP], min_val=0, max_val=31)
                        return d_e[n % 4].start(Y, dst, A["WE"][bass.ds(e, 1), part_, :, :].rearrange("o p n -> p (o n)"))
                    if i < 8 or lo:
                        t = fetch()
                    else:
                        with sync.If(n_owned > i):
                            t = fetch()
                        with sync.Else():
                            sync.sem_inc(d_e[n % 4].sem, 16)
                    self.raw_t.append(t)
                    self.loaded += 1

                def cut(self):
                    n = self.split
                    if n >= 2 * len(order):
                        return
                    r = A_(2048 * (n // 2 % 4) + 1024 * (n % 2), 1024)
                    s_ = n % 4
                    h, l = (x[:, 2 * s_:2 * s_ + 2, :].rearrange(flat) for x in (XH, XL))
                    free = self.done[n - 4] if n >= 4 else None
                    Q, eng = (G, pool) if n % 6 in POOL_CUTS else (V, dve)
                    S.w(free, self.raw_t[n // 2])
                    th = S.inc(act.activation(h, r, ACT.Copy))
                    Q.w(free, th, self.raw_t[n // 2])
                    tl = Q.inc(eng.tensor_tensor(l, r, h.bitcast(F32), ALU.subtract))
                    self.split_t.append((th, tl))
                    self.split += 1
                    if n % 2:
                        self.load()

                def next(self, n_cols):
                    n = self.used
                    self.used += 1
                    while self.split <= n:
                        self.cut()
                    P.w(*self.split_t[n])
                    s_ = n % 4
                    return [x[:, 2 * s_:2 * s_ + 2, :].rearrange(flat).rearrange("p (k n) -> p k n", n=n_cols)
                            for x in (XH, XL)]

                def finished(self, ticket):
                    self.done.append(ticket)
                    while self.split < min(self.used + 3, 2 * len(order)):
                        self.cut()

            experts = Experts()
            t_gather, t_scatter, turned_t, xs_t, xs_read = {}, {}, {}, {}, {}

            def gather(i):
                if i >= hi:
                    return
                G.w(turned_t.get(i - 3))
                d = d_g[i % 3]
                d.n += 16
                pool.indirect_dma_start(xe[i % 3], None, xtok, bass.IndirectOffsetOnAxis(ap=slots[:, 0, i:i + 1], axis=0),
                                        bounds_check=T - 1, oob_is_err=False).then_inc(d.sem, 16)
                t_gather[i] = (d.sem, d.name, d.n)

            def tokens(i):
                if i >= hi:
                    return
                P.w(t_gather[i])
                two = []
                for half in range(2):
                    b = banks.get()
                    P.w(*b.free)
                    for k in range(4):
                        kk = 4 * half + k
                        mm = pe.transpose(b.ap[:, 128 * k:128 * k + 128], xe[i % 3][:, 128 * kk:128 * kk + 128], C("ident"))
                    two.append((b, P.inc(mm)))
                turned_t[i] = two[1][1]
                for half, (b, t) in enumerate(two):
                    src = b.ap.rearrange("p (k n) -> p k n", n=128)
                    kk = slice(4 * half, 4 * half + 4)
                    xs_t[i] = split_x(xs[i % 2][0][:, kk, :], xs[i % 2][1][:, kk, :], src, t, xs_read.get(i - 2))
                    banks.put(b, xs_t[i])
                gather(i + 3)

            def hidden(i):
                b = banks.get()
                P.w(*b.free, xs_t[i])
                xh, xl = xs[i % 2]
                for q in range(4):
                    h, l = experts.next(512)
                    for kk in range(2):
                        k = 2 * q + kk
                        pe.matmul(b.ap, xh[:, k, :], h[:, kk, :], start=k == 0, stop=False)
                        pe.matmul(b.ap, xl[:, k, :], h[:, kk, :], start=False, stop=False)
                        mm = pe.matmul(b.ap, xh[:, k, :], l[:, kk, :], start=False, stop=k == 7)
                    t = P.inc(mm)
                    experts.finished(t)
                xs_read[i] = t
                s = act_[i % 2]
                S.w(t, hid_t.get(i - 2))
                ts = S.inc(act.activation(s, b.ap[:, 0:256], ACT.Silu))
                V.w(ts)
                t1 = V.inc(dve.tensor_tensor(s, s, b.ap[:, 256:512], ALU.mult))
                banks.put(b, t1)
                return s, t1

            hid_t = {}

            def turn_hidden(i, s, t1):
                b = banks.get()
                P.w(*b.free, t1)
                for k in range(2):
                    mm = pe.transpose(b.ap[:, 128 * k:128 * k + 128], s[:, 128 * k:128 * k + 128], C("ident"))
                hid_t[i] = P.inc(mm)
                hid_t["x"] = split_x(hs[0], hs[1], b.ap[:, 0:256].rearrange("p (k n) -> p k n", n=128), hid_t[i])
                banks.put(b, hid_t["x"])

            def down(i):
                two = [banks.get(), banks.get()]
                P.w(*two[0].free, *two[1].free, hid_t["x"])
                for kt in range(2):
                    h, l = experts.next(512)
                    for half in range(2):
                        o = two[half].ap
                        pe.matmul(o, hs[0][:, kt, :], h[:, half, :], start=kt == 0, stop=False)
                        pe.matmul(o, hs[1][:, kt, :], h[:, half, :], start=False, stop=False)
                        mm = pe.matmul(o, hs[0][:, kt, :], l[:, half, :], start=False, stop=kt == 1)
                    t = P.inc(mm)
                    experts.finished(t)
                y_ = ye[i % 2]
                S.w(t, t_scatter.get(i - 2))
                ta = S.inc(act.activation(y_[:, 0:512], two[0].ap, ACT.Copy))
                banks.put(two[0], ta)
                V.w(t, t_scatter.get(i - 2))
                tb = V.inc(dve.tensor_copy(y_[:, 512:1024], two[1].ap))
                banks.put(two[1], tb)
                G.w(ta, tb)
                d = d_y[i % 2]
                d.n += 16
                pool.indirect_dma_start(ytok, bass.IndirectOffsetOnAxis(ap=slots[:, 1, i:i + 1], axis=0), y_, None,
                                        bounds_check=2 * T - 1, oob_is_err=False).then_inc(d.sem, 16)
                t_scatter[i] = (d.sem, d.name, d.n)

            for i in range(lo, lo + 3):
                gather(i)
            tokens(lo)
            for i in range(lo, hi):
                s, t1 = hidden(i)
                tokens(i + 1)
                if i > lo:
                    down(i - 1)
                turn_hidden(i, s, t1)
            down(hi - 1)
            return [t_scatter[hi - 1], t_scatter[hi - 2]]

        E = mybir.EngineType
        n_owned = nc.values_load(owner[0:1, 127:128], engines=[E.SP, E.PE, E.DVE, E.Activation, E.Pool],
                                 min_val=8, max_val=NT)
        gathers = [[Dma(f"d_g{w_}{i}") for i in range(3)] for w_ in range(2)]
        scatters = [[Dma(f"d_y{w_}{i}") for i in range(2)] for w_ in range(2)]
        done = run_tiles(0, NT_1, gathers[0], scatters[0])
        fence = everything() + done
        for q in (V, S, P, G, Y):
            q.w(*fence)
        queues = (P, V, S, G)
        before_q, before_d = [q.count for q in queues], [d.n for d in d_e]
        with nc.If(n_owned > NT_1):
            done = run_tiles(NT_1, NT, gathers[1], scatters[1])
            fence = everything() + done
            for q in (V, S, P, G, Y):
                q.w(*fence)
        with nc.Else():
            for q, n in zip(queues, before_q):
                q.engine.sem_inc(q.sem, q.count - n)
            for d, n in zip(d_e, before_d):
                sync.sem_inc(d.sem, d.n - n)

        pp = A3(8192, 8)
        ple = fetch_p(2)
        y2 = [A3(4096 * c_, 4, 1024) for c_ in range(2)]
        d_r = [Dma(f"d_r{i}") for i in range(4)]
        got = []
        for ti in range(4):
            for c_ in range(2):
                r0 = T * c_ + 128 * ti
                t = d_r[ti].start(Y, y2[c_][:, ti, :], ytok[r0:r0 + 128, :])
            got.append(t)
        embed(pp, ple)
        run = Running(False)
        eight = [banks.get() for _ in range(8)]
        for b in eight:
            P.w(*b.free)
        for ti in range(4):
            S.w(got[ti])
            t = S.inc(act.activation(y2[0][:, ti, :], y2[0][:, ti, :], ACT.Copy, scale=weight[:, ti:ti + 1]))
            V.w(t, got[ti])
            t = V.inc(dve.scalar_tensor_tensor(out=y2[0][:, ti, :], in0=y2[1][:, ti, :], scalar=weight[:, 4 + ti:5 + ti],
                                               in1=y2[0][:, ti, :], op0=ALU.mult, op1=ALU.add))
            P.w(t)
            for k in range(KT):
                t = P.inc(pe.transpose(eight[k].ap[:, 128 * ti:128 * ti + 128],
                                       y2[0][:, ti, 128 * k:128 * k + 128], C("ident")))
                if ti == 3:
                    V.w(t)
                    t = V.inc(dve.scalar_tensor_tensor(out=hT[:, k, :], in0=hT[:, k, :], scalar=ALPHA,
                                                       in1=eight[k].ap, op0=ALU.mult, op1=ALU.add))
                    banks.put(eight[k], t)
                    run.add(hT[:, k, :], t)
        layer_norm("lng", "lnb", 8, run)
        if stop == "ln4":
            dump(hT[:, :, :])
            return

        run = Running(False)
        for j in range(4):
            def f_e(i, b, t, j=j):
                s = scratch.get()
                S.w(t, *s.free)
                ts = S.inc(act.activation(s.ap, b.ap, ACT.Sigmoid))
                banks.put(b, ts)
                V.w(ts)
                t1 = V.inc(dve.tensor_tensor(s.ap, s.ap, pp[:, 2 * j + i, :], ALU.mult))
                V.w(t1)
                t1 = V.inc(dve.scalar_tensor_tensor(out=hT[:, 2 * j + i, :], in0=hT[:, 2 * j + i, :], scalar=ALPHA,
                                                    in1=s.ap, op0=ALU.mult, op1=ALU.add))
                scratch.put(s, t1)
                run.add(hT[:, 2 * j + i, :], t1)
            linear(256, xk, f_e)
        d_o = [Dma(f"d_o{i}") for i in range(4)]

        def give(k, t):
            Y.w(t)
            outs.append(d_o[k // 2].start(Y, out[:, k - 1:k + 1, :], hT[:, k - 1:k + 1, :]))
        outs = []
        layer_norm("lng", "lnb", 16, run, split=False, each=give)
        Y.w(outs)




def weight_blocks(W):
    blocks = []

    def cols(w, idx, k0=0, k1=None):
        w = w[128 * k0:(128 * k1 if k1 else None)]
        k = w.shape[0] // 128
        return w.reshape(k, 128, w.shape[1])[:, :, idx].transpose(1, 0, 2).reshape(128, -1)

    r = np.arange
    for i in range(2):
        w = W["w_in"][i]
        ka, ki = r(512, 576), r(896, 960)
        qa, qi, qb, kb, vb = r(0, 512), r(640, 896), r(964, 1476), r(1476, 1988), r(1988, 2500)
        blocks.append(cols(w, np.concatenate([ki, ki, qi[:128]])))
        blocks.append(cols(w, np.concatenate([qi[128:], ka, ka])))
        blocks.append(cols(w, np.concatenate([r(576, 640), r(960, 964)])))
        for c in (qa, qb, kb, vb):
            blocks += [cols(w, c[:256]), cols(w, c[256:])]
        for j in range(4):
            s = r(256 * j, 256 * j + 256)
            blocks += [cols(w, 2500 + s), cols(w, 3524 + s)]
        for j in range(4):
            s = r(256 * j, 256 * j + 256)
            blocks.append(np.concatenate([cols(W["w_branch_a"][i], s), cols(W["w_branch_b"][i], s)], axis=1))
        for j in range(4):
            blocks.append(cols(W["w_out"][i], r(256 * j, 256 * j + 256)))
        f0 = 0
        for c in FCH:
            for j in range(0, c, 2):
                s = r(128 * (f0 + j), 128 * (f0 + j) + 256)
                blocks += [cols(W["w_up"][i], s), cols(W["w_up"][i], 2816 + s)]
            for j in range(4):
                blocks.append(cols(W["w_down"][i], r(256 * j, 256 * j + 256), f0, f0 + c))
            f0 += c
        blocks.append(cols(W["w_ple_proj"][i], r(1024)))
        for j in range(4):
            blocks.append(cols(W["w_ple_gate"][i], r(256 * j, 256 * j + 256)))
    w = W["w_in_2"][0]
    for c in (r(0, 512), r(512, 1024), r(1024, 1536)):
        blocks += [cols(w, c[:256]), cols(w, c[256:])]
    RW = 1536
    blocks.append(cols(w, r(RW + 1536, RW + 1792)))
    blocks.append(cols(w, r(RW + 1792, RW + 1824)))
    for j in range(4):
        s = r(RW + 128 * j, RW + 128 * j + 128)
        blocks += [cols(w, np.concatenate([s, 512 + s])), cols(w, 1024 + s)]
        s = r(256 * j, 256 * j + 256)
        blocks += [cols(w, 3360 + s), cols(w, 4384 + s)]
    for j in range(4):
        s = r(256 * j, 256 * j + 256)
        blocks.append(np.concatenate([cols(W["w_branch_attn_2"][0], s), cols(W["w_branch_rwkv_2"][0], s)], axis=1))
    for j in range(4):
        blocks.append(cols(W["w_out_2"][0], r(256 * j, 256 * j + 256)))
    blocks.append(cols(W["ple_proj_2"][0], r(1024)))
    for j in range(4):
        blocks.append(cols(W["ple_gate_2"][0], r(256 * j, 256 * j + 256)))
    return blocks


def expert_weights(W):
    gu = np.concatenate([W["exp_gate_2"][0], W["exp_up_2"][0]], axis=2)
    gu = gu.reshape(32, 2, 4, 128, 512).transpose(0, 1, 3, 2, 4).reshape(32, 2, 128, BLK)
    dn = W["exp_down_2"][0].reshape(32, 2, 128, 1024).transpose(0, 2, 1, 3).reshape(32, 1, 128, BLK)
    return np.ascontiguousarray(np.concatenate([gu, dn], axis=1))


def slot_consts():
    p = np.arange(128)[:, None]
    x = np.arange(8)[None, :]
    upto = np.zeros((128, 64))
    e = np.arange(32)
    upto[0:32, 0:32] = e[:, None] < e[None, :]
    upto[0:32, 32:64] = e[:, None] <= e[None, :]
    parts = [p < np.arange(128)[None, :], np.arange(128)[None, :] + 0 * p, np.arange(NT)[None, :] + 0 * p,
             128 * x + p - 4096, upto, p]
    return np.concatenate([np.asarray(a, np.float32) for a in parts], axis=1)


def columns(v):
    return np.asarray(v).reshape(-1, 128).T


def lay_out(inp):
    W = {k: np.asarray(v) for k, v in inp.items()}
    consts, cparts = const_table()
    parts, n_small = small_columns()
    small = np.zeros((128, n_small), np.float32)

    def put(name, a):
        x, y = parts[name]
        small[:, x:y] = a

    def twice(v):
        return np.concatenate([v, v])[:, None]

    for i in range(2):
        put(f"gmix{i}", columns(W["g_mix_norm"][i]))
        for n, s in (("gqa", "g_qa"), ("gka", "g_ka"), ("gqb", "g_qb"), ("gkb", "g_kb")):
            put(f"{n}{i}", twice(W[s][i]))
        put(f"gsub{i}", W["g_subln"][i][:, None])
        a, _ = parts[f"lam{i}"]
        for j, s in enumerate(("lam_q1", "lam_k1", "lam_q2", "lam_k2")):
            small[0:64, a + j] = W[s][i]
        put(f"gffn{i}", columns(W["g_ffn_norm"][i]))
        for j in range(3):
            put(f"cw{j}{i}", columns(W["conv_w"][i, j]))
        put(f"cb{i}", columns(W["conv_b"][i]))
        put(f"gple{i}", columns(W["g_ple_norm"][i]))
    put("lnig", columns(W["ln_in_g_2"]))
    put("lnib", columns(W["ln_in_b_2"]))
    a, _ = parts["mu"]
    mu = W["tok_mix_2"][0]
    small[:, a:a + 14] = columns(mu[:1792])
    small[0:32, a + 14] = mu[1792:]
    for n, s in (("dbase", "decay_base_2"), ("abase", "aaa_base_2"), ("kk", "k_k_2"), ("ka", "k_a_2"),
                 ("gng", "gn_g_2"), ("gnb", "gn_b_2")):
        put(n, columns(W[s][0]))
    put("rk", columns(W["r_k_2"][0].reshape(-1)))
    put("lng", columns(W["ln_g_2"][0].reshape(-1)))
    put("lnb", columns(W["ln_b_2"][0].reshape(-1)))
    put("rbias", np.concatenate([W["router_grp_bias_2"][0], W["router_exp_bias_2"][0]])[None, :])
    wr = np.concatenate([W["router_grp_2"][0], W["router_exp_2"][0]], axis=1)
    put("wrt", wr.reshape(8, 128, 36).transpose(1, 0, 2).reshape(128, -1))
    lora = np.zeros((4, 128, 384), np.float32)
    for j in range(4):
        c = slice(128 * j, 128 * j + 128)
        lora[j, 0:64, 0:128] = W["decay_up_2"][0][:, c]
        lora[j, 64:128, 0:128] = W["aaa_up_2"][0][:, c]
        lora[j, :, 128:256] = W["gate_up_2"][0][0:128, c]
        lora[j, 0:32, 256:384] = W["gate_up_2"][0][128:160, c]
    dist = 384 + np.arange(128)[:, None] - np.arange(512)[None, :]
    bias = W["rel_bias_2"][:, np.clip(dist, -128, 128) + 128]
    p_all = np.concatenate([W["p"][:, 0], W["p_2"][:, 0]])
    tiles = {
        "lora": lora,
        "bias": np.ascontiguousarray(bias.transpose(1, 0, 2).reshape(128, -1)),
        "consts": consts,
        "small": small,
        "xT": np.ascontiguousarray(W["x"][0].T.reshape(8, 128, 512).transpose(1, 0, 2)),
        "pT": np.ascontiguousarray(p_all.transpose(0, 2, 1).reshape(3, 2, 128, 512).transpose(0, 2, 1, 3)),
    }
    blocks = weight_blocks(W)
    sizes = [b.shape[1] for b in blocks]
    big = np.zeros((len(blocks), 128, BLK), np.float32)
    for i, b in enumerate(blocks):
        big[i, :, :b.shape[1]] = b
    tiles["W"] = big
    tiles["WE"] = expert_weights(W)
    tiles["moec"] = slot_consts()
    return tiles, sizes, cparts


def kernel(**inputs):
    import concourse.bacc as _bacc
    from concourse.bass_utils import run_bass_kernel_spmd as _run

    tiles, sizes, cparts = lay_out(inputs)
    nc = _bacc.Bacc("TRN2", target_bir_lowering=False, num_devices=1)
    arrays, args = {}, {}
    for name, a in tiles.items():
        arrays[f"in_{name}"] = a
        args[name] = nc.dram_tensor(f"in_{name}", a.shape, mybir.dt.from_np(a.dtype), kind="ExternalInput").ap()
    out = nc.dram_tensor("out_y", (128, 8, 512), F32, kind="ExternalOutput").ap()
    program(nc, args, out, sizes, cparts)
    r = _run(nc, [arrays], core_ids=[0])
    y = np.asarray(r.results[0]["out_y"])
    return y.transpose(1, 0, 2).reshape(1024, 512).T.reshape(1, 512, 1024)
```
